# Optimizing a Trainium2 kernel written in Bass

```python
import math, functools
import jax, jax.numpy as jnp
from jax import lax
import numpy as np
import math

D_MODEL = 1024
BATCH = 1
SEQ = 256
DEPTH = 1

N_HEADS_A = 8
HEAD_DIM = 64
N_KV_GROUPS = 2
Q_PER_GROUP = N_HEADS_A // N_KV_GROUPS
D_ATTN = N_HEADS_A * HEAD_DIM
D_KV = N_KV_GROUPS * HEAD_DIM
CMP_BLOCK = 32
CMP_STRIDE = 16
CMP_HIDDEN = 256
SLC_BLOCK = 64
N_SELECT = 16
N_LOCAL = 2
WINDOW = 512
Q_CHUNK = 128
ATTN_SCALE = HEAD_DIM ** -0.5
NEG = -1e30
FORCE_SCORE = 1e4
D_RNN = D_MODEL
N_RNN_BLOCKS = 16
RNN_BLOCK = D_RNN // N_RNN_BLOCKS
CONV_WIDTH = 4
LRU_C = 8.0
D_FF = 4 * D_MODEL
EPS = 1e-6

IN_SIZES = (D_ATTN, D_KV, D_KV, D_KV, D_KV, D_KV, D_KV, N_HEADS_A * 3, D_RNN, D_RNN, D_MODEL, D_MODEL)
IN_SPLITS = tuple(int(v) for v in np.cumsum(IN_SIZES)[:-1])
D_IN = int(sum(IN_SIZES))


def rms_norm(x, w):
    xf = x.astype(jnp.float32)
    var = jnp.mean(xf * xf, axis=-1, keepdims=True)
    return (xf * lax.rsqrt(var + EPS) * w.astype(jnp.float32)).astype(x.dtype)

def masked_softmax(s, mask):
    s = jnp.where(mask, s.astype(jnp.float32), NEG)
    m = jnp.max(s, axis=-1, keepdims=True)
    e = jnp.where(mask, jnp.exp(s - m), 0.0)
    return e / jnp.maximum(jnp.sum(e, axis=-1, keepdims=True), 1e-20)

def compress_blocks(k, pos, w1, w2):
    B, S = k.shape[0], k.shape[1]
    kb = k.reshape(B, S // CMP_STRIDE, CMP_STRIDE, N_KV_GROUPS, HEAD_DIM)
    blocks = jnp.concatenate([kb[:, :-1], kb[:, 1:]], axis=2) + pos[:, None, :]
    nc = blocks.shape[1]
    flat = blocks.transpose(0, 1, 3, 2, 4).reshape(B, nc, N_KV_GROUPS, CMP_BLOCK * HEAD_DIM)
    c = jax.nn.gelu(flat @ w1) @ w2
    return c.transpose(0, 2, 1, 3)

def nsa_attention(q, k_cmp, v_cmp, k_slc, v_slc, k_win, v_win, gates, pos_k, pos_v, ck_w1, ck_w2, cv_w1, cv_w2):
    B, S = q.shape[0], q.shape[1]
    G, R, dh = N_KV_GROUPS, Q_PER_GROUP, HEAD_DIM
    nb = S // SLC_BLOCK
    nc = S // CMP_STRIDE - 1
    nqb = S // Q_CHUNK
    k_sel = min(N_SELECT, nb)
    r_s = SLC_BLOCK // CMP_STRIDE
    r_c = CMP_BLOCK // CMP_STRIDE
    off = r_s + r_c - 2

    qh = q.reshape(B, S, G, R, dh).transpose(0, 2, 3, 1, 4)
    gh = gates.reshape(B, S, G, R, 3).transpose(0, 2, 3, 1, 4)
    kc = compress_blocks(k_cmp, pos_k, ck_w1, ck_w2)
    vc = compress_blocks(v_cmp, pos_v, cv_w1, cv_w2)
    ks_blk = k_slc.transpose(0, 2, 1, 3).reshape(B, G, nb, SLC_BLOCK, dh)
    vs_blk = v_slc.transpose(0, 2, 1, 3).reshape(B, G, nb, SLC_BLOCK, dh)
    pad_w = ((0, 0), (0, 0), (WINDOW, 0), (0, 0))
    kw_pad = jnp.pad(k_win.transpose(0, 2, 1, 3), pad_w)
    vw_pad = jnp.pad(v_win.transpose(0, 2, 1, 3), pad_w)
    cmp_end = jnp.arange(nc) * CMP_STRIDE + CMP_BLOCK - 1
    blk = jnp.arange(nb)
    gather = jax.vmap(jax.vmap(lambda blocks, ix: blocks[ix]))

    def chunk(qb):
        t0 = qb * Q_CHUNK
        qc = lax.dynamic_slice_in_dim(qh, t0, Q_CHUNK, axis=3)
        gc = lax.dynamic_slice_in_dim(gh, t0, Q_CHUNK, axis=3)
        tpos = t0 + jnp.arange(Q_CHUNK)
        s = jnp.einsum('bgrcd,bgnd->bgrcn', qc, kc) * ATTN_SCALE
        p_cmp = masked_softmax(s, cmp_end[None, :] <= tpos[:, None])
        o_cmp = jnp.einsum('bgrcn,bgnd->bgrcd', p_cmp, vc.astype(jnp.float32))
        ps = jnp.pad(p_cmp.sum(axis=2), ((0, 0), (0, 0), (0, 0), (off, 0)))
        imp = 0.0
        for m in range(r_s):
            for n in range(r_c):
                st = off - m - n
                imp = imp + ps[..., st:st + r_s * (nb - 1) + 1:r_s]
        cur = tpos // SLC_BLOCK
        valid_b = blk[None, :] <= cur[:, None]
        forced = (blk[None, :] == 0) | (blk[None, :] > cur[:, None] - N_LOCAL)
        score = jnp.where(valid_b, jnp.where(forced, FORCE_SCORE, imp), NEG)
        top_s, idx = lax.top_k(score, k_sel)
        sel_ok = top_s > NEG / 2
        ksel = gather(ks_blk, idx).reshape(B, G, Q_CHUNK, k_sel * SLC_BLOCK, dh)
        vsel = gather(vs_blk, idx).reshape(B, G, Q_CHUNK, k_sel * SLC_BLOCK, dh)
        kpos = idx[..., None] * SLC_BLOCK + jnp.arange(SLC_BLOCK)
        m_slc = (sel_ok[..., None] & (kpos <= tpos[:, None, None])).reshape(B, G, 1, Q_CHUNK, k_sel * SLC_BLOCK)
        s = jnp.einsum('bgrcd,bgcnd->bgrcn', qc, ksel) * ATTN_SCALE
        o_slc = jnp.einsum('bgrcn,bgcnd->bgrcd', masked_softmax(s, m_slc), vsel.astype(jnp.float32))
        kw = lax.dynamic_slice_in_dim(kw_pad, t0, Q_CHUNK + WINDOW, axis=2)
        vw = lax.dynamic_slice_in_dim(vw_pad, t0, Q_CHUNK + WINDOW, axis=2)
        kpos_w = t0 - WINDOW + jnp.arange(Q_CHUNK + WINDOW)
        diff = tpos[:, None] - kpos_w[None, :]
        m_win = (diff >= 0) & (diff < WINDOW) & (kpos_w[None, :] >= 0)
        s = jnp.einsum('bgrcd,bgnd->bgrcn', qc, kw) * ATTN_SCALE
        o_win = jnp.einsum('bgrcn,bgnd->bgrcd', masked_softmax(s, m_win), vw.astype(jnp.float32))
        out = gc[..., 0:1] * o_cmp + gc[..., 1:2] * o_slc + gc[..., 2:3] * o_win
        return out.astype(q.dtype)

    res = lax.map(chunk, jnp.arange(nqb))
    return res.transpose(1, 0, 4, 2, 3, 5).reshape(B, S, D_ATTN)

def rg_lru_branch(xr, gate, conv_w, conv_b, w_a, b_a, w_i, b_i, lam):
    B, S = xr.shape[0], xr.shape[1]
    xp = jnp.pad(xr, ((0, 0), (CONV_WIDTH - 1, 0), (0, 0)))
    xc = conv_b
    for i in range(CONV_WIDTH):
        xc = xc + xp[:, i:i + S] * conv_w[i]
    xb = xc.reshape(B, S, N_RNN_BLOCKS, RNN_BLOCK)
    r = jax.nn.sigmoid(jnp.einsum('bshi,hij->bshj', xb, w_a).reshape(B, S, D_RNN) + b_a)
    ig = jax.nn.sigmoid(jnp.einsum('bshi,hij->bshj', xb, w_i).reshape(B, S, D_RNN) + b_i)
    log_a = -LRU_C * r.astype(jnp.float32) * jax.nn.softplus(-lam.astype(jnp.float32))
    a = jnp.exp(log_a)
    bt = jnp.sqrt(-jnp.expm1(2.0 * log_a)) * (ig * xc).astype(jnp.float32)

    def combine(lhs, rhs):
        a1, b1 = lhs
        a2, b2 = rhs
        return a1 * a2, a2 * b1 + b2

    _, h = lax.associative_scan(combine, (a, bt), axis=1)
    return h.astype(xr.dtype) * jax.nn.gelu(gate)

def first_inputs(seed: int = 0) -> dict:
    key = jax.random.key(seed)
    ks = jax.random.split(key, 24)
    f32 = jnp.float32

    def nrm(k, shape, fan_in):
        return jax.random.normal(k, shape, f32) * (fan_in ** -0.5)

    a_c = jax.random.uniform(ks[17], (DEPTH, D_RNN), f32, 0.9, 0.999)
    s_l = a_c ** (1.0 / LRU_C)
    lam = jnp.log(s_l) - jnp.log1p(-s_l)
    return {
        "x": jax.random.normal(ks[0], (BATCH, SEQ, D_MODEL), f32),
        "norm1_w": 1.0 + 0.02 * jax.random.normal(ks[1], (DEPTH, D_MODEL), f32),
        "w_in": nrm(ks[2], (DEPTH, D_MODEL, D_IN), D_MODEL),
        "cmp_pos_k": 0.1 * jax.random.normal(ks[3], (DEPTH, CMP_BLOCK, HEAD_DIM), f32),
        "cmp_pos_v": 0.1 * jax.random.normal(ks[4], (DEPTH, CMP_BLOCK, HEAD_DIM), f32),
        "cmp_k_w1": nrm(ks[5], (DEPTH, CMP_BLOCK * HEAD_DIM, CMP_HIDDEN), CMP_BLOCK * HEAD_DIM),
        "cmp_k_w2": nrm(ks[6], (DEPTH, CMP_HIDDEN, HEAD_DIM), CMP_HIDDEN),
        "cmp_v_w1": nrm(ks[7], (DEPTH, CMP_BLOCK * HEAD_DIM, CMP_HIDDEN), CMP_BLOCK * HEAD_DIM),
        "cmp_v_w2": nrm(ks[8], (DEPTH, CMP_HIDDEN, HEAD_DIM), CMP_HIDDEN),
        "conv_w": nrm(ks[9], (DEPTH, CONV_WIDTH, D_RNN), CONV_WIDTH),
        "conv_b": 0.01 * jax.random.normal(ks[10], (DEPTH, D_RNN), f32),
        "lru_w_a": nrm(ks[11], (DEPTH, N_RNN_BLOCKS, RNN_BLOCK, RNN_BLOCK), RNN_BLOCK),
        "lru_b_a": 0.01 * jax.random.normal(ks[12], (DEPTH, D_RNN), f32),
        "lru_w_i": nrm(ks[13], (DEPTH, N_RNN_BLOCKS, RNN_BLOCK, RNN_BLOCK), RNN_BLOCK),
        "lru_b_i": 0.01 * jax.random.normal(ks[14], (DEPTH, D_RNN), f32),
        "lru_lambda": lam,
        "w_up_attn": nrm(ks[15], (DEPTH, D_ATTN, D_MODEL), D_ATTN),
        "w_up_rnn": nrm(ks[16], (DEPTH, D_RNN, D_MODEL), D_RNN),
        "w_out": nrm(ks[18], (DEPTH, D_MODEL, D_MODEL), D_MODEL),
        "norm2_w": 1.0 + 0.02 * jax.random.normal(ks[19], (DEPTH, D_MODEL), f32),
        "mlp_w1": nrm(ks[20], (DEPTH, D_MODEL, D_FF), D_MODEL),
        "mlp_w2": nrm(ks[21], (DEPTH, D_FF, D_MODEL), D_FF),
        "final_norm_w": 1.0 + 0.02 * jax.random.normal(ks[22], (D_MODEL,), f32),
    }

def first_block(x, norm1_w, w_in, cmp_pos_k, cmp_pos_v, cmp_k_w1, cmp_k_w2, cmp_v_w1, cmp_v_w2,
              conv_w, conv_b, lru_w_a, lru_b_a, lru_w_i, lru_b_i, lru_lambda,
              w_up_attn, w_up_rnn, w_out, norm2_w, mlp_w1, mlp_w2, final_norm_w):
    B, S = x.shape[0], x.shape[1]
    for l in range(DEPTH):
        xn = rms_norm(x, norm1_w[l])
        z = xn @ w_in[l]
        (q, k_c, v_c, k_s, v_s, k_w, v_w, g_nsa, xr, gr, g_a, g_b) = jnp.split(z, IN_SPLITS, axis=-1)
        kv_shape = (B, S, N_KV_GROUPS, HEAD_DIM)
        attn = nsa_attention(
            q.reshape(B, S, N_HEADS_A, HEAD_DIM),
            k_c.reshape(kv_shape), v_c.reshape(kv_shape),
            k_s.reshape(kv_shape), v_s.reshape(kv_shape),
            k_w.reshape(kv_shape), v_w.reshape(kv_shape),
            jax.nn.sigmoid(g_nsa).reshape(B, S, N_HEADS_A, 3),
            cmp_pos_k[l], cmp_pos_v[l], cmp_k_w1[l], cmp_k_w2[l], cmp_v_w1[l], cmp_v_w2[l])
        rnn = rg_lru_branch(xr, gr, conv_w[l], conv_b[l], lru_w_a[l], lru_b_a[l],
                            lru_w_i[l], lru_b_i[l], lru_lambda[l])
        merged = jax.nn.sigmoid(g_a) * (attn @ w_up_attn[l]) + jax.nn.sigmoid(g_b) * (rnn @ w_up_rnn[l])
        x = x + merged @ w_out[l]
        hn = rms_norm(x, norm2_w[l])
        x = x + jnp.square(jax.nn.relu(hn @ mlp_w1[l])) @ mlp_w2[l]
    return rms_norm(x, final_norm_w)


DEPTH_2 = 2

Q_BLOCK = 128
RMS_EPS = 1e-6
NEG_INF = -1e30
A_HEADS = 8
A_LATENT = 256
IDX_HEADS = 8
IDX_DIM = 64
TOPK_MAX = 256
B_HEADS = 4
C_HEADS = 16
REL_BUCKETS = 32
REL_MAX_DIST = 128
REL_HEADS = A_HEADS + B_HEADS
PEER_HEADS = 8
PEER_QDIM = 256
PEER_NKEYS = 128
PEER_EXPERTS = PEER_NKEYS * PEER_NKEYS
PEER_TOPK = 16
PEER_CHUNK = 128
EVEN_SIZES = (A_HEADS * HEAD_DIM, A_LATENT, IDX_HEADS * IDX_DIM, IDX_DIM, IDX_HEADS,
              B_HEADS * 2 * HEAD_DIM, B_HEADS * 2 * HEAD_DIM, B_HEADS * 2 * HEAD_DIM)
EVEN_IN = A_HEADS * HEAD_DIM + A_LATENT + IDX_HEADS * IDX_DIM + IDX_DIM + IDX_HEADS + 3 * B_HEADS * 2 * HEAD_DIM
EVEN_MIX = A_HEADS * HEAD_DIM + B_HEADS * 2 * HEAD_DIM
ODD_SIZES = (C_HEADS * HEAD_DIM, C_HEADS * HEAD_DIM, C_HEADS * HEAD_DIM, C_HEADS)
ODD_IN = 3 * C_HEADS * HEAD_DIM + C_HEADS
ODD_MIX = C_HEADS * HEAD_DIM


def rmsnorm(x, g):
    xf = x.astype(jnp.float32)
    y = xf * lax.rsqrt(jnp.mean(xf * xf, axis=-1, keepdims=True) + RMS_EPS)
    return (y * g.astype(jnp.float32)).astype(x.dtype)

def split_cols(p, sizes):
    points = np.cumsum(np.array(sizes))[:-1].tolist()
    return jnp.split(p, points, axis=-1)

def rel_bucket(dist):
    max_exact = REL_BUCKETS // 2
    d = jnp.maximum(dist, 0)
    df = jnp.maximum(d, 1).astype(jnp.float32)
    large = max_exact + (jnp.log(df / max_exact) / math.log(REL_MAX_DIST / max_exact)
                         * (REL_BUCKETS - max_exact)).astype(jnp.int32)
    large = jnp.minimum(large, REL_BUCKETS - 1)
    return jnp.where(d < max_exact, d, large)

def sweep_blocks(fn, batch, seq_len):
    n = seq_len // Q_BLOCK
    out = lax.map(fn, jnp.arange(n, dtype=jnp.int32) * Q_BLOCK)
    out = jnp.moveaxis(out, 0, 1)
    return out.reshape((batch, seq_len) + out.shape[3:])

def dsa_attention(q, ckv, q_idx, k_idx, w_idx, w_uk, w_uv, bias_a):
    B, S = q.shape[0], q.shape[1]
    topk = min(TOPK_MAX, S // 4)
    key_pos = jnp.arange(S, dtype=jnp.int32)
    scale = HEAD_DIM ** -0.5
    idx_scale = IDX_DIM ** -0.5
    q_lat = jnp.einsum('bthd,chd->bthc', q, w_uk)

    def block(start):
        qpos = start + jnp.arange(Q_BLOCK, dtype=jnp.int32)
        qi = lax.dynamic_slice_in_dim(q_idx, start, Q_BLOCK, axis=1)
        wi = lax.dynamic_slice_in_dim(w_idx, start, Q_BLOCK, axis=1)
        ql = lax.dynamic_slice_in_dim(q_lat, start, Q_BLOCK, axis=1)
        li = jnp.einsum('bthd,bsd->bths', qi, k_idx).astype(jnp.float32) * idx_scale
        iscore = jnp.einsum('bths,bth->bts', jax.nn.relu(li), wi.astype(jnp.float32))
        causal = key_pos[None, :] <= qpos[:, None]
        iscore = jnp.where(causal[None], iscore, -jnp.inf)
        _, sel = lax.top_k(iscore, topk)
        kv_sel = jax.vmap(lambda lat, ix: lat[ix])(ckv, sel)
        dist = qpos[None, :, None] - sel
        s = jnp.einsum('bthc,btkc->bthk', ql, kv_sel).astype(jnp.float32) * scale
        s = s + jnp.moveaxis(bias_a[rel_bucket(dist)], -1, 2).astype(jnp.float32)
        s = jnp.where((dist >= 0)[:, :, None, :], s, NEG_INF)
        p = jax.nn.softmax(s, axis=-1).astype(ckv.dtype)
        o_lat = jnp.einsum('bthk,btkc->bthc', p, kv_sel)
        o = jnp.einsum('bthc,chd->bthd', o_lat, w_uv)
        return o.reshape(B, Q_BLOCK, A_HEADS * HEAD_DIM)

    return sweep_blocks(block, B, S)

def diff_attention(q1, q2, k1, k2, v, lam, lam_init, subln_g, bias_b):
    B, S = q1.shape[0], q1.shape[1]
    key_pos = jnp.arange(S, dtype=jnp.int32)
    scale = HEAD_DIM ** -0.5

    def block(start):
        qpos = start + jnp.arange(Q_BLOCK, dtype=jnp.int32)
        causal = key_pos[None, :] <= qpos[:, None]
        bias = jnp.moveaxis(bias_b[rel_bucket(qpos[:, None] - key_pos[None, :])], -1, 0)
        bias = bias.astype(jnp.float32)

        def probs(q, k):
            qb = lax.dynamic_slice_in_dim(q, start, Q_BLOCK, axis=1)
            s = jnp.einsum('bthd,bshd->bhts', qb, k).astype(jnp.float32) * scale + bias
            return jax.nn.softmax(jnp.where(causal, s, NEG_INF), axis=-1)

        a = probs(q1, k1) - lam * probs(q2, k2)
        return jnp.einsum('bhts,bshe->bthe', a.astype(v.dtype), v)

    o = sweep_blocks(block, B, S)
    o = rmsnorm(o, subln_g) * (1.0 - lam_init)
    return o.reshape(B, S, B_HEADS * 2 * HEAD_DIM)

def forgetting_attention(q, k, v, f_logit):
    B, S = q.shape[0], q.shape[1]
    key_pos = jnp.arange(S, dtype=jnp.int32)
    scale = HEAD_DIM ** -0.5
    cum = jnp.moveaxis(jnp.cumsum(jax.nn.log_sigmoid(f_logit.astype(jnp.float32)), axis=1), -1, 1)

    def block(start):
        qpos = start + jnp.arange(Q_BLOCK, dtype=jnp.int32)
        causal = key_pos[None, :] <= qpos[:, None]
        qb = lax.dynamic_slice_in_dim(q, start, Q_BLOCK, axis=1)
        cq = lax.dynamic_slice_in_dim(cum, start, Q_BLOCK, axis=2)
        s = jnp.einsum('bthd,bshd->bhts', qb, k).astype(jnp.float32) * scale
        s = s + cq[..., :, None] - cum[..., None, :]
        p = jax.nn.softmax(jnp.where(causal, s, NEG_INF), axis=-1).astype(v.dtype)
        return jnp.einsum('bhts,bshd->bthd', p, v)

    return sweep_blocks(block, B, S).reshape(B, S, C_HEADS * HEAD_DIM)

def even_mixer(h, w_in, w_out, kv_norm, w_uk, w_uv, lam_vec, subln_g, rel_bias, lam_init):
    B, S, _ = h.shape
    q_a, ckv, q_i, k_i, w_i, q_b, k_b, v_b = split_cols(h @ w_in, EVEN_SIZES)
    q_a = q_a.reshape(B, S, A_HEADS, HEAD_DIM)
    ckv = rmsnorm(ckv, kv_norm)
    q_i = q_i.reshape(B, S, IDX_HEADS, IDX_DIM)
    w_i = w_i * (IDX_HEADS ** -0.5)
    o_a = dsa_attention(q_a, ckv, q_i, k_i, w_i, w_uk, w_uv, rel_bias[:, :A_HEADS])
    q_b = q_b.reshape(B, S, B_HEADS, 2, HEAD_DIM)
    k_b = k_b.reshape(B, S, B_HEADS, 2, HEAD_DIM)
    v_b = v_b.reshape(B, S, B_HEADS, 2 * HEAD_DIM)
    lv = lam_vec.astype(jnp.float32)
    lam = jnp.exp(jnp.sum(lv[0] * lv[1])) - jnp.exp(jnp.sum(lv[2] * lv[3])) + lam_init
    o_b = diff_attention(q_b[..., 0, :], q_b[..., 1, :], k_b[..., 0, :], k_b[..., 1, :],
                         v_b, lam, lam_init, subln_g, rel_bias[:, A_HEADS:])
    return jnp.concatenate([o_a, o_b], axis=-1) @ w_out

def odd_mixer(h, w_in, b_forget, w_out):
    B, S, _ = h.shape
    q, k, v, f = split_cols(h @ w_in, ODD_SIZES)
    shp = (B, S, C_HEADS, HEAD_DIM)
    o = forgetting_attention(q.reshape(shp), k.reshape(shp), v.reshape(shp), f + b_forget)
    return o @ w_out

def peer_ffn(h, w_q, sub_keys, u, v):
    B, S, D = h.shape
    T = B * S
    ht = h.reshape(T, D)
    q = (ht @ w_q).reshape(T, PEER_HEADS, 2, PEER_QDIM // 2)
    s = jnp.einsum('thpd,pnd->thpn', q, sub_keys).astype(jnp.float32)
    top_s, top_i = lax.top_k(s, PEER_TOPK)
    cand_s = top_s[:, :, 0, :, None] + top_s[:, :, 1, None, :]
    cand_i = top_i[:, :, 0, :, None] * PEER_NKEYS + top_i[:, :, 1, None, :]
    best_s, best_j = lax.top_k(cand_s.reshape(T, PEER_HEADS, -1), PEER_TOPK)
    experts = jnp.take_along_axis(cand_i.reshape(T, PEER_HEADS, -1), best_j, axis=-1)
    gates = jax.nn.softmax(best_s, axis=-1)
    n_chunks = T // PEER_CHUNK
    hk = PEER_HEADS * PEER_TOPK

    def chunk(args):
        xc, ec, gc = args
        act = jax.nn.gelu(jnp.einsum('cd,ced->ce', xc, u[ec]))
        return jnp.einsum('ce,ced->cd', gc.astype(xc.dtype) * act, v[ec])

    out = lax.map(chunk, (ht.reshape(n_chunks, PEER_CHUNK, D),
                          experts.reshape(n_chunks, PEER_CHUNK, hk),
                          gates.reshape(n_chunks, PEER_CHUNK, hk)))
    return out.reshape(B, S, D)

def second_inputs(seed: int = 0) -> dict:
    key = jax.random.key(seed)
    ks = jax.random.split(key, 24)
    n_even = (DEPTH_2 + 1) // 2
    n_odd = DEPTH_2 // 2

    def nrm(k, shape, scale):
        return jax.random.normal(k, shape, jnp.float32) * scale

    return {
        "x": nrm(ks[0], (BATCH, SEQ, D_MODEL), 1.0),
        "c": nrm(ks[1], (BATCH, D_MODEL), 1.0),
        "rel_bias": nrm(ks[2], (REL_BUCKETS, REL_HEADS), 0.5),
        "ada_w": nrm(ks[3], (DEPTH_2, D_MODEL, 6 * D_MODEL), 0.5 * D_MODEL ** -0.5),
        "ada_b": nrm(ks[4], (DEPTH_2, 6 * D_MODEL), 0.02),
        "norm_mix": 1.0 + nrm(ks[5], (DEPTH_2, D_MODEL), 0.02),
        "norm_ffn": 1.0 + nrm(ks[6], (DEPTH_2, D_MODEL), 0.02),
        "norm_final": 1.0 + nrm(ks[7], (D_MODEL,), 0.02),
        "even_w_in": nrm(ks[8], (n_even, D_MODEL, EVEN_IN), D_MODEL ** -0.5),
        "even_w_out": nrm(ks[9], (n_even, EVEN_MIX, D_MODEL), EVEN_MIX ** -0.5),
        "a_kv_norm": 1.0 + nrm(ks[10], (n_even, A_LATENT), 0.02),
        "a_w_uk": nrm(ks[11], (n_even, A_LATENT, A_HEADS, HEAD_DIM), A_LATENT ** -0.5),
        "a_w_uv": nrm(ks[12], (n_even, A_LATENT, A_HEADS, HEAD_DIM), A_LATENT ** -0.5),
        "b_lambda": nrm(ks[13], (n_even, 4, HEAD_DIM), 0.1),
        "b_subln": 1.0 + nrm(ks[14], (n_even, 2 * HEAD_DIM), 0.02),
        "odd_w_in": nrm(ks[15], (n_odd, D_MODEL, ODD_IN), D_MODEL ** -0.5),
        "odd_b_forget": 2.0 + nrm(ks[16], (n_odd, C_HEADS), 0.5),
        "odd_w_out": nrm(ks[17], (n_odd, ODD_MIX, D_MODEL), ODD_MIX ** -0.5),
        "peer_w_q": nrm(ks[18], (DEPTH_2, D_MODEL, PEER_HEADS * PEER_QDIM), D_MODEL ** -0.5),
        "peer_sub_keys": nrm(ks[19], (DEPTH_2, 2, PEER_NKEYS, PEER_QDIM // 2), (PEER_QDIM // 2) ** -0.5),
        "peer_u": nrm(ks[20], (DEPTH_2, PEER_EXPERTS, D_MODEL), D_MODEL ** -0.5),
        "peer_v": nrm(ks[21], (DEPTH_2, PEER_EXPERTS, D_MODEL), PEER_HEADS ** -0.5),
    }

def second_block(x, c, rel_bias, ada_w, ada_b, norm_mix, norm_ffn, norm_final,
              even_w_in, even_w_out, a_kv_norm, a_w_uk, a_w_uv, b_lambda, b_subln,
              odd_w_in, odd_b_forget, odd_w_out,
              peer_w_q, peer_sub_keys, peer_u, peer_v):
    c_act = jax.nn.silu(c)
    for layer in range(DEPTH_2):
        mod = (c_act @ ada_w[layer] + ada_b[layer])[:, None, :]
        sh1, sc1, g1, sh2, sc2, g2 = jnp.split(mod, 6, axis=-1)
        h = rmsnorm(x, norm_mix[layer]) * (1.0 + sc1) + sh1
        if layer % 2 == 0:
            e = layer // 2
            lam_init = 0.8 - 0.6 * math.exp(-0.3 * layer)
            y = even_mixer(h, even_w_in[e], even_w_out[e], a_kv_norm[e], a_w_uk[e], a_w_uv[e],
                           b_lambda[e], b_subln[e], rel_bias, lam_init)
        else:
            o = layer // 2
            y = odd_mixer(h, odd_w_in[o], odd_b_forget[o], odd_w_out[o])
        x = x + g1 * y
        h = rmsnorm(x, norm_ffn[layer]) * (1.0 + sc2) + sh2
        x = x + g2 * peer_ffn(h, peer_w_q[layer], peer_sub_keys[layer], peer_u[layer], peer_v[layer])
    return rmsnorm(x, norm_final)


def setup_inputs(seed=0):
    out = dict(first_inputs(seed))
    for name, value in second_inputs(seed + 1).items():
        if name != "x":
            out[name + "_2"] = value
    return out


def reference(
    x, norm1_w, w_in, cmp_pos_k, cmp_pos_v, cmp_k_w1, cmp_k_w2, cmp_v_w1, cmp_v_w2, conv_w,
    conv_b, lru_w_a, lru_b_a, lru_w_i, lru_b_i, lru_lambda, w_up_attn, w_up_rnn, w_out, norm2_w,
    mlp_w1, mlp_w2, final_norm_w, c_2, rel_bias_2, ada_w_2, ada_b_2, norm_mix_2, norm_ffn_2,
    norm_final_2, even_w_in_2, even_w_out_2, a_kv_norm_2, a_w_uk_2, a_w_uv_2, b_lambda_2,
    b_subln_2, odd_w_in_2, odd_b_forget_2, odd_w_out_2, peer_w_q_2, peer_sub_keys_2, peer_u_2,
    peer_v_2,
):
    x = first_block(
        x, norm1_w, w_in, cmp_pos_k, cmp_pos_v, cmp_k_w1, cmp_k_w2, cmp_v_w1, cmp_v_w2, conv_w,
        conv_b, lru_w_a, lru_b_a, lru_w_i, lru_b_i, lru_lambda, w_up_attn, w_up_rnn, w_out,
        norm2_w, mlp_w1, mlp_w2, final_norm_w,
    )
    return second_block(
        x, c_2, rel_bias_2, ada_w_2, ada_b_2, norm_mix_2, norm_ffn_2, norm_final_2, even_w_in_2,
        even_w_out_2, a_kv_norm_2, a_w_uk_2, a_w_uv_2, b_lambda_2, b_subln_2, odd_w_in_2,
        odd_b_forget_2, odd_w_out_2, peer_w_q_2, peer_sub_keys_2, peer_u_2, peer_v_2,
    )


_drawn_inputs = setup_inputs


def setup_inputs(seed=0):
    import zlib

    import numpy as np

    out = dict(_drawn_inputs(seed))
    spreads = {}
    factors = {'norm1_w': 4.917,
     'cmp_pos_k': 8.0,
     'cmp_pos_v': 2.999,
     'conv_b': 3.28,
     'lru_b_a': 8.0,
     'lru_b_i': 8.0,
     'norm2_w': 2.669,
     'norm_mix_2': 5.18,
     'norm_ffn_2': 4.563,
     'norm_final_2': 2.794,
     'a_kv_norm_2': 8.0,
     'b_lambda_2': 2.811,
     'b_subln_2': 8.0}
    for name, (base, spread) in spreads.items():
        noise = np.random.default_rng([zlib.crc32(name.encode()), seed]).standard_normal(out[name].shape)
        drawn = base * np.exp(spread * noise) if base else spread * noise
        out[name] = __import__('jax').numpy.asarray(drawn.astype(out[name].dtype))
    for name, factor in factors.items():
        out[name] = (out[name] * factor).astype(out[name].dtype)
    return out
```

```python
import math
from contextlib import ExitStack

import concourse.bass as bass
from concourse import mybir

F32 = mybir.dt.float32
U32 = mybir.dt.uint32
ACT = mybir.ActivationFunctionType
ALU = mybir.AluOpType
AX = mybir.AxisListType

P = 128
S = 256
NT = S // P
D = 1024
KC = D // P
WRING = 8
ARING = 4
GRING = 8
NEG = -1e30
EPS = 1e-6
NCMP = 15
NKEYS = 128
NEXP = NKEYS * NKEYS
TOPK = 16
PH = 8
SLOTS = PH * TOPK
LAM_INIT = 0.8 - 0.6 * math.exp(-0.3 * 0)

STREAM = [("in", 45, 45), ("cmp", 8, 4), ("lru", 2, 16), ("upattn", 4, 8),
          ("uprnn", 8, 8), ("out", 8, 8), ("mlp1", 32, 32), ("mlp2", 32, 8), ("ein", 24, 24),
          ("ukv", 2, 6), ("eout", 8, 8), ("pq0", 16, 16), ("oin", 25, 25), ("oout", 8, 8),
          ("pq1", 16, 16)]
UNIT0, OUT0 = {}, {}
_u, _o = 0, 0
for _n, _a, _b in STREAM:
    UNIT0[_n], OUT0[_n] = _u, _o
    _u, _o = _u + _a, _o + _b
UNITS = _u
N_OUT = {n: b for n, _, b in STREAM}

ZQ, ZKC, ZVC, ZKS, ZVS, ZKW, ZVW, ZG, ZXR, ZGR, ZGA, ZGB = 0, 4, 6, 8, 9, 10, 11, 12, 13, 21, 29, 37
EQA, ECKV, EQI, EKI, EWI, EQB, EKB, EVB = 0, 4, 6, 10, 11, 12, 16, 20
OQ, OK, OV, OF = 0, 8, 16, 24

VEC = {}
_c = 0
for _n, _w in [("norm1", 8), ("norm2", 8), ("final1", 8), ("conv_w", 32), ("conv_b", 8), ("b_a", 8),
               ("b_i", 8), ("lam", 8), ("c", 8), ("ada_b", 96), ("mix", 16), ("ffn", 16), ("final2", 8),
               ("kvn", 2), ("subln", 1), ("bf", 1), ("pos_k", 16), ("pos_v", 16), ("blam", 4),
               ("rel", 12)]:
    VEC[_n] = _c
    _c += _w
NVEC = _c
CON = {}
_c = 0
for _n, _w in [("ident", 128), ("flip", 128), ("mean", 128), ("mean128", 128), ("ones", 128), ("causal", 256),
               ("cmask", 32), ("cbias", 32), ("iota", 16), ("buckets", 384), ("ind", 16)]:
    CON[_n] = _c
    _c += _w
NCON = _c


def build(nc, x_dram, c_row, ada, weights, small, vecs, cons, experts_u, experts_v, out):
    ctx = ExitStack()
    with ctx:
        def sb(name, shape, dt=F32):
            return ctx.enter_context(nc.sbuf_tensor(name, shape, dt))

        def ps(name, shape):
            return ctx.enter_context(nc.psum_tensor(name, shape, F32))

        def sem(name):
            return ctx.enter_context(nc.semaphore(name))

        wring = [sb(f"wring{i}", [P, KC * P]) for i in range(WRING)]
        X = sb("X", [P, KC * S])
        N = sb("N", [P, KC * S])
        Z = sb("Z", [P, 45 * S])
        W = sb("W", [P, GRING * D])
        AT = sb("AT", [P, KC * S])
        vec = sb("vec", [P, NVEC])
        con = sb("con", [P, NCON])
        wsm = sb("wsm", [P, 896])
        bias0 = sb("bias0", [P, 12 * P])
        bias1 = sb("bias1", [P, 12 * S])
        relrow = sb("relrow", [12, 384])
        mod = sb("mod", [P, 96])
        crow = sb("crow", [P, D])
        aring = sb("aring", [P, ARING, D])
        amul = sb("amul", [P, 4 * KC])
        rstd = sb("rstd", [P, 2 * S])
        var = sb("var", [P, 2 * S])
        Sb = sb("Sb", [P, 2, 512])
        Pb = sb("Pb", [P, 2, 512])
        PT = sb("PT", [P, 2, 512])
        mx = sb("mx", [P, 2, 8])
        sums = sb("sums", [P, 2, 8])
        facs = sb("facs", [P, 2, 8])
        VT = sb("VT", [P, 4 * 512])
        G = sb("G", [P, NT, 24])
        sel = crow[:, 0:2 * S].rearrange("p (t s) -> p t s", t=NT)
        work = crow[:, 2 * S:4 * S].rearrange("p (t s) -> p t s", t=NT)
        m8 = sb("m8", [P, NT, 8])
        wi = sb("wi", [P, NT, 8])
        tiny = sb("tiny", [P, 64])
        stage = sb("stage", [P, 4, 4], U32)
        lrow = crow[:, 0:S]
        idx = crow[:, S:S + NT * SLOTS].bitcast(U32)
        dots = crow[:, 2 * S:2 * S + NT * SLOTS]
        gate = crow[:, 3 * S:3 * S + NT * SLOTS]
        psL = ps("psL", [P, 4, 512])
        psS = ps("psS", [P, 2, 512])
        psT = ps("psT", [P, 512])
        psO = ps("psO", [P, 512])
        reld = nc.dram_tensor("rel_rows", [12, 384], F32, kind="Internal").ap()

        def V(name, a=0, b=None):
            b = a + 1 if b is None else b
            return vec[:, VEC[name] + a:VEC[name] + b]

        def C(name, w, parts=P, a=0):
            return con[0:parts, CON[name] + a:CON[name] + a + w]

        def zu(u, n=1, parts=slice(0, P)):
            return Z[parts, u * S:(u + n) * S]

        def chunk(t, k, n=1):
            return t[:, k * S:(k + n) * S]

        def toks(t, u, T, parts=slice(0, P), w=P):
            return t[parts, u * S + T * P:u * S + T * P + w]

        def hid(kv, m):
            a = 1024 + (kv * 2 + m) * 32
            return W[:, a:a + 30]

        cprob, kcT, VTc = W[:, 1280:1536], W[:, 1536:1552], W[:, 1664:1792]
        Wt = [W[:, i * KC * S:(i + 1) * KC * S] for i in range(4)]
        ident = C("ident", P)

        x_in, vec_in, con_in, small_in = sem("x_in"), sem("vec_in"), sem("con_in"), sem("small_in")
        landed = [sem(f"unit_landed{i}") for i in range(WRING)]
        unit_done, out_taken = sem("unit_done"), sem("out_taken")
        relrow_ready, relrow_copied, rel_stored = sem("relrow_ready"), sem("relrow_copied"), sem("rel_stored")
        rel_loaded, flipped, bias_ready = sem("rel_loaded"), sem("flipped"), sem("bias_ready")
        c_in, csil_ready, ada_used = sem("c_in"), sem("csil_ready"), sem("ada_used")
        ada_landed = [sem(f"ada_landed{i}") for i in range(ARING)]
        sq_ready, ss_ready, rv_ready, rstd_ready, n_ready = (
            sem(n) for n in ("sq_ready", "ss_ready", "rv_ready", "rstd_ready", "n_ready"))
        dve_step, act_step = sem("dve_step"), sem("act_step")
        scores_ready, smax_ready, exp_done, p_ready = (
            sem(n) for n in ("scores_ready", "smax_ready", "exp_done", "p_ready"))
        pt_ready, pt_copied, o_ready, o_copied = (
            sem(n) for n in ("pt_ready", "pt_copied", "o_ready", "o_copied"))
        turned, turn_taken = sem("turned"), sem("turn_taken")
        gates_ready = sem("gates_ready")
        flat_ready, kv2_ready, kv2_taken = (sem(n) for n in ("flat_ready", "kv2_ready", "kv2_taken"))
        cs_ready, csub_ready, cexp_ready, cp_ready, cpt_ready = (
            sem(n) for n in ("cs_ready", "csub_ready", "cexp_ready", "cp_ready", "cpt_ready"))
        xc_ready, lru_act, lru_dve, h_ready = (sem(n) for n in ("xc_ready", "lru_act", "lru_dve", "h_ready"))
        sig_ready, hsq_ready, pair_ready = sem("sig_ready"), sem("hsq_ready"), sem("pair_ready")
        ckv_sq, ckv_ss, ckv_ready = sem("ckv_sq"), sem("ckv_ss"), sem("ckv_ready")
        lam_in, lam_sum, lam_exp = sem("lam_in"), sem("lam_sum"), sem("lam_exp")
        li_ready, li_relu, li_added, sel_ready = (
            sem(n) for n in ("li_ready", "li_relu", "li_added", "sel_ready"))
        od_sq, od_ss, od_rv, od_rstd, od_ready = (
            sem(n) for n in ("od_sq", "od_ss", "od_rv", "od_rstd", "od_ready"))
        f_act, f_ready = sem("f_act"), sem("f_ready")
        key_scores, key_taken, best_in, gexp = (
            sem(n) for n in ("key_scores", "key_taken", "best_in", "gexp"))
        idx_ready, staged, gather_next = sem("idx_ready"), sem("staged"), sem("gather_next")
        row_landed = [sem(f"row_landed{j}") for j in range(GRING)]
        row_used, act_ready = sem("row_used"), sem("act_ready")
        stored = sem("stored")

        def weights_at(eng, name, j, i=0):
            g = UNIT0[name] + j
            eng.wait_ge(landed[g % WRING], (i + g // WRING + 1) * 16)
            return wring[g % WRING]

        def rounds(eng, n, body, per=8, peel=False):
            full = n // per
            for j in range(per if peel else 0):
                body(j, 0)
            if full > 1:
                with eng.Fori(int(peel), full) as i:
                    for j in range(per):
                        body(j, i)
            else:
                full = 0
            for m in range(full * per, n):
                body(m % per, m // per)

        def keys_of(T):
            return P * (T + 1)

        def causal(T):
            return con[:, CON["causal"] + P * (1 - T):CON["causal"] + S]

        def relbias(h, T):
            return bias0[:, h * P:(h + 1) * P] if T == 0 else bias1[:, h * S:(h + 1) * S]

        jobs = []
        for T in range(NT):
            for h in range(8):
                j, b = h % 4, h // 4
                rows = slice(64 * b, 64 * b + 64)
                jobs.append(dict(kind="nsa", T=T, rows=[rows, rows], q=[ZQ + j] * 2, k=[ZKS, ZKW],
                                 bias=[causal(T)] * 2,
                                 fac=[G[:, T, 3 * h + 1:3 * h + 2], G[:, T, 3 * h + 2:3 * h + 3]],
                                 v=[lambda kt: VT[:, kt * P:(kt + 1) * P],
                                    lambda kt: VT[:, (2 + kt) * P:(3 + kt) * P]],
                                 slot=[0, 0], cmp=T * 8 + h, outs=[(0, rows, j)]))
        for T in range(NT):
            for j in range(4):
                jobs.append(dict(kind="dsa", T=T, rows=[slice(0, 64), slice(64, 128)],
                                 q=[EQA + j] * 2, k=[24 + j] * 2,
                                 bias=[relbias(2 * j, T), relbias(2 * j + 1, T)], fac=[None, None],
                                 v=[lambda kt, j=j: VT[:, kt * 512 + j * P:kt * 512 + (j + 1) * P]] * 2,
                                 slot=[0, 1], cmp=None,
                                 outs=[(0, slice(0, 64), j), (1, slice(64, 128), j)]))
        for T in range(NT):
            for h in range(4):
                jobs.append(dict(kind="diff", T=T, rows=[slice(0, 64), slice(64, 128)],
                                 q=[EQB + h] * 2, k=[EKB + h] * 2, bias=[relbias(8 + h, T)] * 2,
                                 fac=[None, tiny[:, 60:61]],
                                 v=[lambda kt, h=h: VT[:, 1024 + kt * 512 + h * P:1024 + kt * 512 + (h + 1) * P]] * 2,
                                 slot=[0, 0], cmp=None, outs=[(0, slice(0, P), 4 + h)]))
        for T in range(NT):
            for j in range(8):
                jobs.append(dict(kind="forget", T=T, rows=[slice(0, 64), slice(64, 128)],
                                 q=[OQ + j] * 2, k=[OK + j] * 2, bias=[causal(T)] * 2, fac=[None, None],
                                 v=[lambda kt, j=j: W[:, 4096 + kt * 1024 + j * P:4096 + kt * 1024 + (j + 1) * P]] * 2,
                                 slot=[0, 1], cmp=None, head=[2 * j, 2 * j + 1],
                                 outs=[(0, slice(0, 64), j), (1, slice(64, 128), j)]))
        for n, jb in enumerate(jobs):
            jb["n"] = n
        JOBS = {k: [jb for jb in jobs if jb["kind"] == k] for k in ("nsa", "dsa", "diff", "forget")}

        ROUNDS = SLOTS // GRING
        TURNS_PEER = (13, 25)

        block = ctx.enter_context(nc.Block())

        @block.sync
        def _(sp):
            sp.dma_start(vec[:], vecs).then_inc(vec_in, 16)
            sp.dma_start(con[:], cons).then_inc(con_in, 16)

            def unit(j, i):
                g = i * WRING + j
                if not isinstance(g, int) or g >= WRING:
                    sp.wait_ge(unit_done, g - WRING + 1)
                src = weights[g] if isinstance(g, int) else weights[bass.ds(g, 1)].rearrange("a p n -> (a p) n")
                sp.dma_start(wring[j][:], src).then_inc(landed[j], 16)

            for j in range(WRING):
                unit(j, 0)
            sp.wait_ge(relrow_copied, 1)
            sp.dma_start(reld, relrow[:]).then_inc(rel_stored, 16)
            sp.wait_ge(rel_stored, 16)
            for T in range(NT):
                w = keys_of(T)
                src = bass.AP(tensor=reld.tensor, offset=P - T * P, ap=[[1, P], [384, 12], [1, w]])
                dst = W[:, T * 12 * P:T * 12 * P + 12 * w]
                sp.dma_start(dst.rearrange("p (h w) -> p h w", h=12), src).then_inc(rel_loaded, 16)
            with sp.Fori(1, UNITS // WRING) as i:
                for j in range(WRING):
                    unit(j, i)
            for g in range(UNITS // WRING * WRING, UNITS):
                unit(g % WRING, g // WRING)
            sp.wait_ge(n_ready, 8)
            sp.dma_start(out, N[:]).then_inc(stored, 16)
            sp.wait_ge(stored, 16)

        @block.gpsimd
        def _(pool):
            def ada_load(j, i):
                if not isinstance(i, int):
                    pool.wait_ge(ada_used, i * ARING + j - ARING + 1)
                    src = ada[bass.ds(i * ARING + j, 1)].rearrange("a p n -> (a p) n")
                else:
                    src = ada[j]
                pool.dma_start(aring[:, j, :], src).then_inc(ada_landed[j], 16)

            for j in range(ARING):
                ada_load(j, 0)
            with pool.Fori(1, 96 // ARING) as i:
                for j in range(ARING):
                    ada_load(j, i)
            per, group = 2 * GRING, 4
            for l in range(2):
                for n, table in enumerate((experts_u, experts_v)):
                    for T in range(NT):
                        loop = (l * 2 + n) * NT + T
                        used0 = loop * SLOTS
                        rounds_ = SLOTS // per
                        pool.wait_ge(idx_ready, l * NT + T + 1)

                        def gathers(i, first):
                            for q in range(per // group):
                                if not first:
                                    pool.wait_ge(row_used, i * per + used0 + q * group + group - per)
                                pool.tensor_copy(stage[:, q, :],
                                                 idx[:, bass.ds(i * per + T * SLOTS + q * group, group)]
                                                 ).then_inc(staged, 1)
                                for j in range(group):
                                    c = q * group + j
                                    slot = c % GRING
                                    if j == 0:
                                        pool.wait_ge(staged, i * (per // group) + loop * rounds_ * (per // group) + q + 1)
                                    if not (first and c < GRING):
                                        pool.wait_ge(row_used, i * per + used0 + c - GRING + 1)
                                    pool.sem_inc(gather_next, 1)
                                    pool.indirect_dma_start(
                                        W[:, slot * D:(slot + 1) * D], None, table,
                                        bass.IndirectOffsetOnAxis(ap=stage[:, q, j:j + 1], axis=0)
                                    ).then_inc(row_landed[slot], 16)

                        if loop == 0:
                            gathers(0, True)
                        with pool.Fori(1 if loop == 0 else 0, rounds_) as i:
                            gathers(i, False)

        @block.tensor
        def _(pe):
            def mm(o, l, r, first=True, last=True):
                return pe.matmul(o, l, r, start=first, stop=last)

            def project(name, rhs):
                if OUT0[name]:
                    pe.wait_ge(out_taken, OUT0[name])

                def unit(j, i):
                    w = weights_at(pe, name, j, i)
                    if not (isinstance(i, int) and OUT0[name] + i * 8 + j < 4):
                        pe.wait_ge(out_taken, OUT0[name] + i * 8 + j - 3)
                    for k in range(KC):
                        m = mm(psL[:, j % 4, 0:S], w[:, k * P:(k + 1) * P], rhs(k), k == 0, k == KC - 1)
                    m.then_inc(unit_done, 1)

                rounds(pe, N_OUT[name], unit, peel=OUT0[name] == 0)

            def norm_sum(n):
                pe.wait_ge(sq_ready, n + 1)
                for k in range(KC):
                    m = mm(psO[:, 0:S], C("mean", P), chunk(N, k), k == 0, k == KC - 1)
                m.then_inc(ss_ready, 1)

            def attention(kind):
                js = JOBS[kind]
                n0 = js[0]["n"]

                def scores(jb):
                    n, T = jb["n"], jb["T"]
                    if n >= 2:
                        pe.wait_ge(smax_ready, n - 1)
                    w = keys_of(T)
                    for m in range(2):
                        r = jb["rows"][m]
                        o = (psL if m else psS)[:, n % 2, 0:w]
                        last = mm(o, toks(Z, jb["q"][m], T, r), toks(Z, jb["k"][m], 0, r, w),
                                  True, kind != "forget")
                        if kind == "forget":
                            h = jb["head"][m]
                            last = mm(o, lrow[r, T * P:(T + 1) * P], W[r, h * S:h * S + w], False, True)
                    last.then_inc(scores_ready, 1)

                def values(jb):
                    n, T = jb["n"], jb["T"]
                    pe.wait_ge(p_ready, n + 1)
                    if n >= 1:
                        pe.wait_ge(pt_copied, n)
                    at = 0
                    for m in range(2):
                        for kt in range(T + 1):
                            last = pe.transpose(psT[:, at * P:(at + 1) * P],
                                                Pb[:, n % 2, m * S + kt * P:m * S + (kt + 1) * P], ident)
                            at += 1
                    last.then_inc(pt_ready, 1)
                    pe.wait_ge(pt_copied, n + 1)
                    if n >= 1:
                        pe.wait_ge(o_copied, n)
                    for slot in sorted(set(jb["slot"])):
                        parts = [(m, kt) for m in range(2) if jb["slot"][m] == slot for kt in range(T + 1)]
                        o = psO[:, slot * P:(slot + 1) * P]
                        for a, (m, kt) in enumerate(parts):
                            at = m * (T + 1) + kt
                            last = mm(o, jb["v"][m](kt), PT[:, n % 2, at * P:(at + 1) * P], a == 0,
                                      a == len(parts) - 1 and jb["cmp"] is None)
                        if jb["cmp"] is not None:
                            c = jb["cmp"]
                            last = mm(o, VTc[0:NCMP, 0:P], W[0:NCMP, 6144 + c * P:6144 + (c + 1) * P],
                                      False, True)
                    last.then_inc(o_ready, 1)

                scores(js[0])
                scores(js[1])
                for a, jb in enumerate(js):
                    values(jb)
                    if a + 2 < len(js):
                        scores(js[a + 2])

            turns = [0]

            def turn(pairs, tile=psT):
                if turns[0]:
                    pe.wait_ge(turn_taken, turns[0])
                for o, src in pairs:
                    last = pe.transpose(o, src, ident)
                last.then_inc(turned, 1)
                turns[0] += 1

            pe.wait_ge(vec_in, 16)
            pe.wait_ge(con_in, 16)
            mm(psO[0:12, 0:384], vec[0:32, VEC["rel"]:VEC["rel"] + 12], C("buckets", 384, 32)
               ).then_inc(relrow_ready, 1)
            pe.wait_ge(rel_loaded, 32)
            for n in range(9):
                if n >= 2:
                    pe.wait_ge(bias_ready, n - 1)
                mm(psS[:, n % 2, :], C("flip", P), W[:, n * 512:(n + 1) * 512]).then_inc(flipped, 1)
            pe.wait_ge(relrow_copied, 1)
            norm_sum(0)
            pe.wait_ge(n_ready, 1)
            project("in", lambda k: chunk(N, k))
            pe.wait_ge(out_taken, OUT0["in"] + 45)
            turn([(psT[:, (2 * a + kt) * P:(2 * a + kt + 1) * P], toks(Z, u, kt))
                  for a, u in enumerate((ZVS, ZVW)) for kt in range(NT)])
            pe.wait_ge(gates_ready, 1)
            turn([(psT[:, T * P:(T + 1) * P], toks(Z, ZG, T)) for T in range(NT)])
            pe.wait_ge(flat_ready, 8)
            for a in range(4):
                for u in range(2):
                    w = weights_at(pe, "cmp", 2 * a + u)
                    for k in range(KC):
                        i = 8 * u + k
                        r = W[:, (a // 2) * 512 + i * 30:(a // 2) * 512 + (i + 1) * 30]
                        m = mm(psL[:, a, 0:30], w[:, k * P:(k + 1) * P], r, i == 0, i == 15)
                    m.then_inc(unit_done, 1)
            pe.wait_ge(out_taken, OUT0["cmp"] + 4)
            pe.wait_ge(small_in, 16)
            for m_ in range(2):
                mm(psO[:, 0:30], wsm[:, m_ * P:(m_ + 1) * P], hid(0, m_), m_ == 0, m_ == 1)
            for g in range(2):
                for m_ in range(2):
                    m = mm(psO[0:NCMP, 64 + g * 64:128 + g * 64], hid(1, m_)[:, g * NCMP:(g + 1) * NCMP],
                           wsm[:, 256 + m_ * 64:256 + (m_ + 1) * 64], m_ == 0, m_ == 1)
            m.then_inc(kv2_ready, 1)
            pe.wait_ge(kv2_taken, 3)
            pe.wait_ge(turn_taken, 2)
            for T in range(NT):
                for h in range(8):
                    j, b = h % 4, h // 4
                    r = slice(64 * b, 64 * b + 64)
                    m = mm((psT if b else psO)[:, (T * 4 + j) * 16:(T * 4 + j) * 16 + NCMP], toks(Z, ZQ + j, T, r),
                           kcT[r, 0:NCMP])
            m.then_inc(cs_ready, 1)
            pe.wait_ge(cp_ready, 1)
            for c in range(16):
                m = pe.transpose(psL[0:NCMP, c // 4, (c % 4) * P:(c % 4 + 1) * P],
                                 cprob[:, c * 16:c * 16 + NCMP], ident)
            m.then_inc(cpt_ready, 1)
            pe.wait_ge(kv2_taken, 5)
            attention("nsa")
            pe.wait_ge(xc_ready, 1)
            for a in range(2):
                w = weights_at(pe, "lru", a)
                for k in range(KC):
                    o = a * KC + k
                    pe.wait_ge(out_taken, OUT0["lru"] + o - 3 if o >= 4 else OUT0["lru"])
                    m = mm(psL[:, o % 4, 0:S], w[:, k * P:(k + 1) * P], Wt[0][:, k * S:(k + 1) * S])
                    m.then_inc(h_ready if k < KC - 1 else unit_done, 1)
            pe.wait_ge(out_taken, OUT0["upattn"])
            pe.wait_ge(sig_ready, 1)
            pe.wait_ge(o_copied, 16)
            for u in range(4):
                w = weights_at(pe, "upattn", u)
                for b in range(2):
                    o = 2 * u + b
                    if o >= 4:
                        pe.wait_ge(out_taken, OUT0["upattn"] + o - 3)
                    for k in range(4):
                        m = mm(psL[:, o % 4, 0:S], w[:, (b * 4 + k) * P:(b * 4 + k + 1) * P], chunk(AT, k),
                               k == 0, k == 3)
                    if b == 0:
                        m.then_inc(pair_ready, 1)
                m.then_inc(unit_done, 1)
            pe.wait_ge(lru_dve, 4)
            project("uprnn", lambda k: Wt[1][:, k * S:(k + 1) * S])
            pe.wait_ge(out_taken, OUT0["uprnn"] + 8)
            project("out", lambda k: chunk(N, k))
            norm_sum(1)
            pe.wait_ge(n_ready, 2)
            project("mlp1", lambda k: chunk(N, k))
            pe.wait_ge(out_taken, OUT0["mlp2"])
            pe.wait_ge(hsq_ready, 32)

            def mlp2_unit(j, i):
                w = weights_at(pe, "mlp2", j, i)
                if j % 4 == 0:
                    pe.wait_ge(out_taken, OUT0["mlp2"] + i * 2 + j // 4 - 1)
                for k in range(KC):
                    m = mm(psL[:, j // 4, 0:S], w[:, k * P:(k + 1) * P], chunk(Z, (j % 4) * 8 + k),
                           j % 4 == 0 and k == 0, j % 4 == 3 and k == KC - 1)
                m.then_inc(unit_done, 1)

            rounds(pe, 32, mlp2_unit)
            norm_sum(2)
            norm_sum(3)
            pe.wait_ge(n_ready, 4)
            project("ein", lambda k: chunk(N, k))
            pe.wait_ge(out_taken, OUT0["ein"] + 24)
            turn([(psT[:, T * P:(T + 1) * P], toks(Z, EWI, T)) for T in range(NT)])
            pe.wait_ge(lam_in, 1)
            pe.wait_ge(rstd_ready, 4)
            mm(psO[:, 256:258], C("ones", P, 64), tiny[0:64, 0:2]).then_inc(lam_sum, 1)
            pe.wait_ge(lam_exp, 1)
            pe.wait_ge(ckv_sq, 1)
            for k in range(2):
                m = mm(psO[:, 0:S], C("mean", P), AT[:, k * S:(k + 1) * S], k == 0, k == 1)
            m.then_inc(ckv_ss, 1)
            for T in range(NT):
                for h in range(8):
                    n = T * 8 + h
                    if n >= 2:
                        pe.wait_ge(li_relu, n - 1)
                    r = slice(64 * (h % 2), 64 * (h % 2) + 64)
                    mm(psS[:, n % 2, 0:keys_of(T)], toks(Z, EQI + h // 2, T, r),
                       toks(Z, EKI, 0, r, keys_of(T))).then_inc(li_ready, 1)
            for kt in range(NT):
                turn([(psT[:, h * P:(h + 1) * P], toks(Z, EVB + h, kt)) for h in range(4)])
            pe.wait_ge(ckv_ready, 2)
            w = weights_at(pe, "ukv", 0)
            for o in range(4):
                for k in range(2):
                    m = mm(psL[:, o, 0:S], w[:, (o * 2 + k) * P:(o * 2 + k + 1) * P], chunk(Z, ECKV + k),
                           k == 0, k == 1)
                m.then_inc(h_ready if o < 3 else unit_done, 1)
            w = weights_at(pe, "ukv", 1)
            for kt in range(NT):
                pe.wait_ge(out_taken, OUT0["ukv"] + kt + 1)
                for k in range(2):
                    m = mm(psL[:, kt, 0:512], toks(Z, ECKV + k, kt), w[:, k * 512:(k + 1) * 512],
                           k == 0, k == 1)
                m.then_inc(h_ready if kt == 0 else unit_done, 1)
            pe.wait_ge(out_taken, OUT0["ukv"] + 6)
            pe.wait_ge(li_relu, 16)
            pe.wait_ge(turn_taken, 5)
            pe.wait_ge(ckv_ready, 1)
            attention("dsa")
            attention("diff")
            pe.wait_ge(od_sq, 1)
            pe.wait_ge(o_copied, 32)
            for m_ in range(2):
                mm(psO[:, 0:512] if m_ == 0 else psT[:, 0:512], C("mean128", P),
                   N[:, m_ * 512:(m_ + 1) * 512]).then_inc(od_ss, 1)
            pe.wait_ge(od_ready, 1)
            project("eout", lambda k: chunk(AT, k))

            def peer(l):
                norm = 4 + 2 * l
                norm_sum(norm)
                pe.wait_ge(n_ready, norm + 1)
                project(f"pq{l}", lambda k: chunk(N, k))
                for T in range(NT):
                    for q in range(2):
                        turn([(psT[:, a * P:(a + 1) * P], toks(N, q * 4 + a, T)) for a in range(4)])
                pe.wait_ge(out_taken, OUT0[f"pq{l}"] + 16)
                for T in range(NT):
                    for q in range(4):
                        n = (l * NT + T) * 4 + q
                        if n >= 2:
                            pe.wait_ge(key_taken, n - 1)
                        for a in range(4):
                            hp = q * 4 + a
                            m = mm(psS[:, n % 2, a * P:(a + 1) * P], toks(Z, hp, T),
                                   wsm[:, 384 + (l * 2 + hp % 2) * P:384 + (l * 2 + hp % 2 + 1) * P])
                        m.then_inc(key_scores, 1)
                for T in range(NT):
                    pe.wait_ge(row_used, (l * 4 + 3 + T) * SLOTS)
                    for q in range(2):
                        turn([(psT[:, a * P:(a + 1) * P],
                               AT[:, T * D + (q * 4 + a) * P:T * D + (q * 4 + a + 1) * P]) for a in range(4)])

            peer(0)
            norm_sum(5)
            pe.wait_ge(n_ready, 6)
            project("oin", lambda k: chunk(N, k))
            pe.wait_ge(out_taken, OUT0["oin"] + 25)
            for kt in range(NT):
                for q in range(2):
                    turn([(psT[:, a * P:(a + 1) * P], toks(Z, OV + q * 4 + a, kt)) for a in range(4)])
            pe.wait_ge(f_ready, 1)
            pe.wait_ge(turn_taken, turns[0])
            attention("forget")
            pe.wait_ge(o_copied, len(jobs))
            project("oout", lambda k: chunk(AT, k))
            peer(1)
            norm_sum(7)

        @block.vector
        def _(dve):
            steps = [0]

            def link(ins):
                steps[0] += 1
                ins.then_inc(dve_step, 1)
                dve.wait_ge(dve_step, steps[0])

            def stt(o, a, s, b, op0, op1):
                return dve.scalar_tensor_tensor(out=o, in0=a, scalar=s, in1=b, op0=op0, op1=op1)

            def ts(o, a, s1, s2, op0, op1=None):
                return dve.tensor_scalar(o, a, s1, s2, op0) if op1 is None else dve.tensor_scalar(o, a, s1, s2, op0, op1)

            def tt(o, a, b, op):
                return dve.tensor_tensor(o, a, b, op)

            def unit_out(name, j, i, take):
                dve.wait_ge(vec_in, 16)
                dve.wait_ge(unit_done, UNIT0[name] + i * 8 + j + 1)
                take(psL[:, j % 4, 0:S], j, i).then_inc(out_taken, 1)

            def project_copy(name, n, dst):
                rounds(dve, n, lambda j, i: unit_out(
                    name, j, i, lambda p, j, i: dve.tensor_copy(dst[:, bass.ds(i * 8 * S + j * S, S)], p)))

            def residual(name, gcol=None):
                for o in range(8):
                    dve.wait_ge(unit_done, UNIT0[name] + o + 1)
                    p = psL[:, o % 4, 0:S]
                    x = chunk(X, o)
                    if gcol is None:
                        tt(x, p, x, ALU.add).then_inc(out_taken, 1)
                    else:
                        stt(x, p, mod[:, gcol + o:gcol + o + 1], x, ALU.mult, ALU.add).then_inc(out_taken, 1)
                dve.wait_ge(out_taken, OUT0[name] + 8)

            def norm(n, wcol, shift=None, dst=None):
                dst = N if dst is None else dst
                dve.wait_ge(ss_ready, n + 1)
                link(ts(var[:, 0:S], psO[:, 0:S], EPS, None, ALU.add))
                dve.reciprocal(var[:, 0:S], var[:, 0:S]).then_inc(rv_ready, 1)
                dve.wait_ge(rstd_ready, n + 1)
                for k in range(KC):
                    m = stt(chunk(dst, k), chunk(X, k), wcol(k), rstd[:, 0:S], ALU.mult, ALU.mult)
                if shift is not None:
                    link(m)
                    for k in range(KC):
                        m = ts(chunk(dst, k), chunk(dst, k), mod[:, shift + k:shift + k + 1], None, ALU.add)
                m.then_inc(n_ready, 1)

            def attention(kind):
                js = JOBS[kind]

                def front(jb):
                    n, T, b = jb["n"], jb["T"], jb["n"] % 2
                    w = keys_of(T)
                    dve.wait_ge(scores_ready, n + 1)
                    if n >= 2:
                        dve.wait_ge(exp_done, n - 1)
                    for m in range(2):
                        ins = stt(Sb[:, b, m * S:m * S + w], (psL if m else psS)[:, b, 0:w], 0.125, jb["bias"][m],
                                  ALU.mult, ALU.add)
                    link(ins)
                    if kind == "dsa":
                        for m in range(2):
                            s = Sb[:, b, m * S:m * S + w]
                            ins = tt(s, s, sel[:, T, 0:w], ALU.add)
                        link(ins)
                    link(dve.tensor_reduce(mx[:, b, 0:2], Sb[:, b, :].rearrange("p (m w) -> p m w", m=2)[:, :, 0:w],
                                           AX.X, ALU.max))
                    ts(mx[:, b, 2:4], mx[:, b, 0:2], -1.0, None, ALU.mult).then_inc(smax_ready, 1)

                def scale(jb):
                    n, T, b = jb["n"], jb["T"], jb["n"] % 2
                    w = keys_of(T)
                    dve.wait_ge(exp_done, n + 1)
                    link(dve.reciprocal(facs[:, b, 0:2], sums[:, b, 0:2]))
                    for m in range(2):
                        if jb["fac"][m] is not None:
                            ins = tt(facs[:, b, m:m + 1], facs[:, b, m:m + 1], jb["fac"][m], ALU.mult)
                    if any(f is not None for f in jb["fac"]):
                        link(ins)
                    for m in range(2):
                        p_ = Pb[:, b, m * S:m * S + w]
                        ins = ts(p_, p_, facs[:, b, m:m + 1], None, ALU.mult)
                    ins.then_inc(p_ready, 1)

                def take(jb):
                    n, T = jb["n"], jb["T"]
                    dve.wait_ge(o_ready, n + 1)
                    for slot, rows, unit in jb["outs"]:
                        ins = dve.tensor_copy(toks(AT, unit, T, rows), psO[rows, slot * P:(slot + 1) * P])
                    ins.then_inc(o_copied, 1)

                front(js[0])
                for a, jb in enumerate(js):
                    if a + 1 < len(js):
                        front(js[a + 1])
                    scale(jb)
                    if a:
                        take(js[a - 1])
                take(js[-1])

            turns = [0]

            def turn_take(o, src):
                dve.wait_ge(turned, turns[0] + 1)
                turns[0] += 1
                dve.tensor_copy(o, src).then_inc(turn_taken, 1)

            dve.wait_ge(relrow_ready, 1)
            dve.tensor_copy(relrow[:], psO[0:12, 0:384]).then_inc(relrow_copied, 1)
            for n in range(9):
                dve.wait_ge(flipped, n + 1)
                T = n // 3 > 0
                w = keys_of(T)
                dst = bias1[:, (n - 3) * 512:(n - 2) * 512] if T else bias0[:, n * 512:(n + 1) * 512]
                tt(dst.rearrange("p (h w) -> p h w", w=w), psS[:, n % 2, :].rearrange("p (h w) -> p h w", w=w),
                   causal(T)[:, None, :].to_broadcast([P, 512 // w, w]), ALU.add).then_inc(bias_ready, 1)

            def ada_unit(slot, o, used):
                dve.wait_ge(ada_landed[slot], used)
                dve.scalar_tensor_tensor(out=aring[:, slot, :], in0=aring[:, slot, :], scalar=1.0, in1=crow[:],
                                         op0=ALU.mult, op1=ALU.mult, accum_out=mod[:, bass.ds(o, 1)]
                                         ).then_inc(ada_used, 1)

            norm(0, lambda k: V("norm1", k))
            dve.wait_ge(csil_ready, 1)

            def in_and_ada(j, i):
                unit_out("in", j, i, lambda p, j, i: dve.tensor_copy(Z[:, bass.ds(i * 8 * S + j * S, S)], p))
                ada_unit(j % ARING, i * 8 + j, (i * 2 + j // ARING + 1) * 16)

            rounds(dve, 45, in_and_ada)
            for o in range(45, 48):
                ada_unit(o % ARING, o, (o // ARING + 1) * 16)
            dve.wait_ge(out_taken, OUT0["in"] + 45)
            turn_take(VT[:, 0:512], psT[:])
            for kv, (u, pos) in enumerate(((ZKC, "pos_k"), (ZVC, "pos_v"))):
                for odd in range(2):
                    r = slice(64 * odd, 64 * odd + 64)
                    z = Z[r, u * S:(u + 2) * S].rearrange("p (g n a) -> p a g n", g=2, a=16)
                    f = W[r, kv * 512:kv * 512 + 480].rearrange("p (i g n) -> p i g n", i=16, g=2)
                    for late in range(2):
                        src = z[:, odd::2, :, late:late + NCMP]
                        b = vec[r, VEC[pos] + late * 8:VEC[pos] + late * 8 + 8]
                        for g in range(2):
                            m = tt(f[:, late * 8:late * 8 + 8, g, :], src[:, :, g, :],
                                   b[:, :, None].to_broadcast([64, 8, NCMP]), ALU.add)
                        m.then_inc(flat_ready, 1)
            dve.wait_ge(turned, 2)
            turns[0] += 1
            dve.tensor_copy(G[:], psT[:, 0:2 * P].rearrange("p (t c) -> p t c", t=2)[:, :, 0:24]).then_inc(turn_taken, 1)
            dve.wait_ge(kv2_ready, 1)
            dve.tensor_copy(kcT[0:64, 0:NCMP], psO[0:64, 0:NCMP]).then_inc(kv2_taken, 1)
            dve.tensor_copy(kcT[64:128, 0:NCMP], psO[64:128, NCMP:2 * NCMP]).then_inc(kv2_taken, 1)
            dve.tensor_copy(VTc[0:NCMP, 0:P], psO[0:NCMP, 64:192]).then_inc(kv2_taken, 1)
            dve.wait_ge(cs_ready, 1)
            cp3 = cprob.rearrange("p (c n) -> p c n", n=16)[:, :, 0:NCMP]
            po3 = [t[:, 0:128].rearrange("p (c n) -> p c n", n=16)[:, :, 0:NCMP] for t in (psO, psT)]

            def c_t(name, T, n=8):
                a = CON[name] + T * 16
                return con[:, a:a + NCMP][:, None, :].to_broadcast([P, n, NCMP])

            for T in range(NT):
                for b in range(2):
                    m = stt(cp3[:, T * 8 + 4 * b:T * 8 + 4 * b + 4, :], po3[b][:, T * 4:T * 4 + 4, :], 0.125,
                            c_t("cbias", T, 4), ALU.mult, ALU.add)
            link(m)
            link(dve.tensor_reduce(tiny[:, 0:16], cp3, AX.X, ALU.max))
            tt(cp3, cp3, tiny[:, 0:16][:, :, None].to_broadcast([P, 16, NCMP]), ALU.subtract).then_inc(csub_ready, 1)
            dve.wait_ge(cexp_ready, 1)
            for T in range(NT):
                m = tt(cp3[:, T * 8:T * 8 + 8, :], cp3[:, T * 8:T * 8 + 8, :], c_t("cmask", T), ALU.mult)
            link(m)
            link(dve.tensor_reduce(tiny[:, 16:32], cp3, AX.X, ALU.add))
            link(ts(tiny[:, 16:32], tiny[:, 16:32], 1e-20, None, ALU.max))
            link(dve.reciprocal(tiny[:, 16:32], tiny[:, 16:32]))
            dve.wait_ge(turn_taken, 2)
            for T in range(NT):
                g = G[:, T, :].rearrange("p (h b) -> p h b", b=3)[:, :, 0]
                m = tt(tiny[:, 16 + 8 * T:24 + 8 * T], tiny[:, 16 + 8 * T:24 + 8 * T], g, ALU.mult)
            link(m)
            tt(cp3, cp3, tiny[:, 16:32][:, :, None].to_broadcast([P, 16, NCMP]), ALU.mult).then_inc(cp_ready, 1)
            dve.wait_ge(cpt_ready, 1)
            for q in range(2):
                dve.tensor_copy(W[0:NCMP, 6144 + q * 1024:6144 + (q + 1) * 1024].rearrange("p (b n) -> p b n", b=2),
                                psL[0:NCMP, 2 * q:2 * q + 2, :]).then_inc(kv2_taken, 1)
            attention("nsa")
            for k in range(KC):
                m = ts(chunk(Wt[0], k), zu(ZXR + k), V("conv_w", 3 * 8 + k), V("conv_b", k), ALU.mult, ALU.add)
            link(m)
            for i in range(3):
                sh = 3 - i
                for k in range(KC):
                    o = chunk(Wt[0], k)[:, sh:S]
                    m = stt(o, zu(ZXR + k)[:, 0:S - sh], V("conv_w", i * 8 + k), o, ALU.mult, ALU.add)
                if i < 2:
                    link(m)
            m.then_inc(xc_ready, 1)
            dve.wait_ge(xc_ready, 1)
            dve.wait_ge(out_taken, OUT0["lru"] + 16)
            tt(Wt[0][:], Wt[0][:], Wt[2][:], ALU.mult).then_inc(lru_dve, 1)
            dve.wait_ge(lru_act, 1)
            link(ts(tiny[:, 32:40], V("lam", 0, 8), -1.0, 0.0, ALU.mult, ALU.max))
            link(tt(tiny[:, 32:40], tiny[:, 32:40], tiny[:, 40:48], ALU.add))
            ts(tiny[:, 40:48], tiny[:, 32:40], 8.0, None, ALU.mult)
            ts(tiny[:, 48:56], tiny[:, 32:40], -8.0, None, ALU.mult).then_inc(lru_dve, 1)
            dve.wait_ge(lru_act, 2)
            link(tt(Wt[1][:], Wt[3][:], Wt[3][:], ALU.mult))
            stt(Wt[2][:], Wt[1][:], 1.0, Wt[2][:], ALU.add, ALU.mult).then_inc(lru_dve, 1)
            dve.wait_ge(lru_act, 3)
            link(tt(Wt[2][:], Wt[2][:], Wt[0][:], ALU.mult))
            for k in range(KC):
                c = slice(k * S, (k + 1) * S)
                m = dve.tensor_tensor_scan(Wt[1][:, c], Wt[3][:, c], Wt[2][:, c], 0.0, ALU.mult, ALU.add)
            link(m)
            dve.wait_ge(lru_act, 4)
            tt(Wt[1][:], Wt[1][:], zu(ZGR, 8), ALU.mult).then_inc(lru_dve, 1)
            dve.wait_ge(sig_ready, 1)
            for o in range(8):
                if o % 2:
                    dve.wait_ge(unit_done, UNIT0["upattn"] + o // 2 + 1)
                else:
                    dve.wait_ge(pair_ready, o // 2 + 1)
                tt(chunk(N, o), psL[:, o % 4, 0:S], zu(ZGA + o), ALU.mult).then_inc(out_taken, 1)
            for o in range(8):
                dve.wait_ge(unit_done, UNIT0["uprnn"] + o + 1)
                link(tt(zu(ZGB + o), psL[:, o % 4, 0:S], zu(ZGB + o), ALU.mult))
                tt(chunk(N, o), chunk(N, o), zu(ZGB + o), ALU.add).then_inc(out_taken, 1)
            residual("out")
            norm(1, lambda k: V("norm2", k))
            def square_and_ada(j, i):
                dve.wait_ge(vec_in, 16)
                dve.wait_ge(out_taken, OUT0["mlp1"] + i * 8 + j + 1)
                z = Z[:, bass.ds(i * 8 * S + j * S, S)]
                tt(z, z, z, ALU.mult).then_inc(hsq_ready, 1)
                for a in range(j * 3 // 2, (j + 1) * 3 // 2):
                    ada_unit(a % ARING, i * 12 + 48 + a, (i * 3 + 12 + a // ARING + 1) * 16)

            rounds(dve, 32, square_and_ada)
            for o in range(8):
                dve.wait_ge(unit_done, UNIT0["mlp2"] + 4 * o + 4)
                tt(chunk(X, o), psL[:, o % 2, 0:S], chunk(X, o), ALU.add).then_inc(out_taken, 1)
            dve.wait_ge(out_taken, OUT0["mlp2"] + 8)
            norm(2, lambda k: V("final1", k), dst=X)
            dve.wait_ge(n_ready, 3)
            dve.wait_ge(ada_used, 96)
            link(tt(mod[:], mod[:], V("ada_b", 0, 96), ALU.add))
            for l in range(2):
                for a, wname in enumerate(("mix", "ffn")):
                    o = (2 * l + a) * KC
                    m = stt(amul[:, o:o + KC], mod[:, l * 48 + a * 24 + 8:l * 48 + a * 24 + 16], 1.0,
                            V(wname, l * 8, l * 8 + 8), ALU.add, ALU.mult)
            link(m)

            norm(3, lambda k: amul[:, k:k + 1], shift=0)
            tt(tiny[0:64, 0:2], vec[0:64, VEC["blam"]:VEC["blam"] + 4:2], vec[0:64, VEC["blam"] + 1:VEC["blam"] + 4:2],
               ALU.mult).then_inc(lam_in, 1)
            project_copy("ein", 24, Z)
            dve.wait_ge(turned, turns[0] + 1)
            turns[0] += 1
            ts(wi[:], psT[:, 0:2 * P].rearrange("p (t c) -> p t c", t=2)[:, :, 0:8], 8.0 ** -0.5, None, ALU.mult
               ).then_inc(turn_taken, 1)
            dve.wait_ge(lam_exp, 1)
            link(tt(tiny[:, 59:60], tiny[:, 57:58], tiny[:, 56:57], ALU.subtract))
            link(ts(tiny[:, 60:61], tiny[:, 59:60], -LAM_INIT, None, ALU.add))
            dve.wait_ge(ckv_ss, 1)
            link(ts(var[:, 0:S], psO[:, 0:S], 4.0, EPS, ALU.mult, ALU.add))
            dve.reciprocal(var[:, 0:S], var[:, 0:S]).then_inc(rv_ready, 1)
            dve.wait_ge(ckv_ready, 1)
            for k in range(2):
                m = stt(zu(ECKV + k), zu(ECKV + k), V("kvn", k), rstd[:, 0:S], ALU.mult, ALU.mult)
            m.then_inc(ckv_ready, 1)
            dve.wait_ge(turn_taken, turns[0])
            for T in range(NT):
                w = keys_of(T)
                for h in range(8):
                    n = T * 8 + h
                    dve.wait_ge(li_relu, n + 1)
                    src = work[:, n % 2, 0:w]
                    if h == 0:
                        m = ts(sel[:, T, 0:w], src, wi[:, T, h:h + 1], None, ALU.mult)
                    else:
                        m = stt(sel[:, T, 0:w], src, wi[:, T, h:h + 1], sel[:, T, 0:w], ALU.mult, ALU.add)
                    m.then_inc(li_added, 1)
                    dve.wait_ge(li_added, n + 1)
                link(tt(sel[:, T, 0:w], sel[:, T, 0:w], causal(T), ALU.add))
            for kt in range(NT):
                turn_take(VT[:, 1024 + kt * 512:1024 + (kt + 1) * 512], psT[:])
            for o in range(4):
                if o < 3:
                    dve.wait_ge(h_ready, 14 + o + 1)
                else:
                    dve.wait_ge(unit_done, UNIT0["ukv"] + 1)
                dve.tensor_copy(zu(24 + o), psL[:, o, 0:S]).then_inc(out_taken, 1)
            for kt in range(NT):
                if kt == 0:
                    dve.wait_ge(h_ready, 18)
                else:
                    dve.wait_ge(unit_done, UNIT0["ukv"] + 2)
                dve.tensor_copy(VT[:, kt * 512:(kt + 1) * 512], psL[:, kt, :]).then_inc(out_taken, 1)
            for r in range(8):
                for T in range(NT):
                    m = dve.max(out=m8[:, T, :], in_=sel[:, T, 0:keys_of(T)])
                link(m)
                for T in range(NT):
                    s = sel[:, T, 0:keys_of(T)]
                    m = dve.match_replace(out=s, in_to_replace=m8[:, T, :], in_values=s, imm_value=-3e38)
                link(m)
            for T in range(NT):
                s = sel[:, T, 0:keys_of(T)]
                m = ts(s, s, -2e38, NEG, ALU.is_gt, ALU.mult)
            link(m)
            dve.wait_ge(bias_ready, 9)
            attention("dsa")
            attention("diff")
            for m_ in range(2):
                dve.wait_ge(od_ss, m_ + 1)
                m = ts(var[:, 0:512], (psO if m_ == 0 else psT)[:, 0:512], EPS, None, ALU.add)
                link(m)
                dve.reciprocal(rstd[:, 0:512], var[:, 0:512]).then_inc(od_rv, 1)
                dve.wait_ge(od_rstd, m_ + 1)
                o = AT[:, (4 + 2 * m_) * S:(6 + 2 * m_) * S]
                link(stt(o, o, V("subln"), rstd[:, 0:512], ALU.mult, ALU.mult))
                m = ts(o, o, 1.0 - LAM_INIT, None, ALU.mult)
            m.then_inc(od_ready, 1)
            residual("eout", 16)

            def peer(l):
                n = 4 + 2 * l
                norm(n, lambda k: amul[:, (2 * l + 1) * KC + k:(2 * l + 1) * KC + k + 1], shift=l * 48 + 24)
                project_copy(f"pq{l}", 16, Z)
                for T in range(NT):
                    for q in range(2):
                        turn_take(Z[:, 16 * S + T * D + q * 512:16 * S + T * D + (q + 1) * 512], psT[:])
                for T in range(NT):
                    sc = Z[:, 24 * S:32 * S].rearrange("p (q n) -> p q n", q=16)
                    val = Z[:, 32 * S:33 * S].rearrange("p (q n) -> p q n", q=16)
                    vix = Z[:, 33 * S:34 * S].bitcast(U32).rearrange("p (q n) -> p q n", q=16)
                    ixf = Z[:, 34 * S:35 * S].rearrange("p (q n) -> p q n", q=16)
                    best = Z[:, 35 * S:35 * S + P].rearrange("p (q n) -> p q n", q=8)
                    bix = Z[:, 35 * S + P:36 * S].bitcast(U32)
                    ab = Z[:, 36 * S:37 * S].bitcast(U32)
                    abf = Z[:, 37 * S:38 * S]
                    cand = Z[:, 24 * S:32 * S].rearrange("p (h i j) -> p h i j", h=8, i=16)
                    candh = Z[:, 24 * S:32 * S].rearrange("p (h n) -> p h n", h=8)

                    def best16(src, v, ix, cnt):
                        for a in range(cnt):
                            m = dve.max(out=v[:, a, 0:8], in_=src[:, a, :])
                        link(m)
                        for a in range(cnt):
                            dve.max_index(out=ix[:, a, 0:8], in_max=v[:, a, 0:8], in_values=src[:, a, :])
                        for a in range(cnt):
                            m = dve.match_replace(out=src[:, a, :], in_to_replace=v[:, a, 0:8],
                                                  in_values=src[:, a, :], imm_value=-3e38)
                        link(m)
                        for a in range(cnt):
                            m = dve.max(out=v[:, a, 8:16], in_=src[:, a, :])
                        link(m)
                        for a in range(cnt):
                            m = dve.max_index(out=ix[:, a, 8:16], in_max=v[:, a, 8:16], in_values=src[:, a, :])
                        link(m)

                    dve.wait_ge(key_taken, (l * NT + T + 1) * 4)
                    best16(sc, val, vix, 16)
                    link(dve.tensor_copy(ixf, vix))
                    v4 = val.rearrange("p (h s) n -> p h s n", s=2)
                    link(tt(cand, v4[:, :, 0, :][:, :, :, None].to_broadcast([P, 8, 16, 16]),
                            v4[:, :, 1, :][:, :, None, :].to_broadcast([P, 8, 16, 16]), ALU.add))
                    bx = bix.rearrange("p (q n) -> p q n", q=8)
                    best16(candh, best, bx, 8)
                    dve.tensor_scalar(ab[:, 0:P], bix, 4, None, ALU.logical_shift_right)
                    link(dve.tensor_scalar(ab[:, P:2 * P], bix, 15, None, ALU.bitwise_and))
                    link(dve.tensor_copy(abf, ab))
                    f4 = ixf.rearrange("p (h s) n -> p h s n", s=2)
                    for side in range(2):
                        pick = abf[:, side * P:(side + 1) * P].rearrange("p (h k) -> p h k", h=8)
                        it = con[:, CON["iota"]:CON["iota"] + 16]
                        link(tt(cand, pick[:, :, :, None].to_broadcast([P, 8, 16, 16]),
                                it[:, None, None, :].to_broadcast([P, 8, 16, 16]), ALU.is_equal))
                        link(tt(cand, cand, f4[:, :, side, :][:, :, None, :].to_broadcast([P, 8, 16, 16]), ALU.mult))
                        link(dve.tensor_reduce(
                            Z[:, 38 * S + side * P:38 * S + (side + 1) * P].rearrange("p (h k) -> p h k", h=8),
                            cand, AX.X, ALU.add))
                    link(stt(abf[:, 0:P], Z[:, 38 * S:38 * S + P], float(NKEYS), Z[:, 38 * S + P:39 * S],
                             ALU.mult, ALU.add))
                    ts(idx[:, T * SLOTS:(T + 1) * SLOTS], abf[:, 0:P], float(l * NEXP), None, ALU.add
                       ).then_inc(idx_ready, 1)
                    gt = gate[:, T * SLOTS:(T + 1) * SLOTS].rearrange("p (h k) -> p h k", h=8)
                    tt(gt, best, best[:, :, 0:1].to_broadcast([P, 8, 16]), ALU.subtract).then_inc(best_in, 1)
                    dve.wait_ge(gexp, l * NT + T + 1)
                    link(dve.tensor_reduce(tiny[:, 0:8], gt, AX.X, ALU.add))
                    link(dve.reciprocal(tiny[:, 0:8], tiny[:, 0:8]))
                    link(tt(gt, gt, tiny[:, 0:8][:, :, None].to_broadcast([P, 8, 16]), ALU.mult))
                for T in range(NT):
                    loop = l * 4 + T
                    h_t = Z[:, 16 * S + T * D:16 * S + (T + 1) * D]
                    with dve.Fori(0, ROUNDS) as i:
                        for s in range(GRING):
                            r = W[:, s * D:(s + 1) * D]
                            dve.wait_ge(row_landed[s], (i + loop * ROUNDS + 1) * 16)
                            dve.scalar_tensor_tensor(out=r, in0=r, scalar=1.0, in1=h_t, op0=ALU.mult,
                                                     op1=ALU.mult, accum_out=dots[:, bass.ds(i * GRING + T * SLOTS + s, 1)]
                                                     ).then_inc(row_used, 1)
                for T in range(NT):
                    dve.wait_ge(act_ready, l * NT + T + 1)
                    g_ = gate[:, T * SLOTS:(T + 1) * SLOTS]
                    m = tt(g_, g_, dots[:, T * SLOTS:(T + 1) * SLOTS], ALU.mult)
                    m = dve.memset(AT[:, T * D:(T + 1) * D], 0.0)
                link(m)
                for T in range(NT):
                    loop = l * 4 + 2 + T
                    acc = AT[:, T * D:(T + 1) * D]
                    with dve.Fori(0, ROUNDS) as i:
                        for s in range(GRING):
                            r = W[:, s * D:(s + 1) * D]
                            dve.wait_ge(row_landed[s], (i + loop * ROUNDS + 1) * 16)
                            dve.scalar_tensor_tensor(out=acc, in0=r, scalar=gate[:, bass.ds(i * GRING + T * SLOTS + s, 1)],
                                                     in1=acc, op0=ALU.mult, op1=ALU.add).then_inc(row_used, 1)
                            dve.wait_ge(row_used, i * GRING + loop * SLOTS + s + 1)
                gcol = l * 48 + 40
                for T in range(NT):
                    for q in range(2):
                        dve.wait_ge(turned, turns[0] + 1)
                        turns[0] += 1
                        for a in range(4):
                            k = q * 4 + a
                            m = stt(toks(X, k, T), psT[:, a * P:(a + 1) * P], mod[:, gcol + k:gcol + k + 1],
                                    toks(X, k, T), ALU.mult, ALU.add)
                        m.then_inc(turn_taken, 1)
                dve.wait_ge(turn_taken, turns[0])
                assert turns[0] == TURNS_PEER[l]

            peer(0)
            norm(5, lambda k: amul[:, 2 * KC + k:2 * KC + k + 1], shift=48)
            project_copy("oin", 25, Z)
            for kt in range(NT):
                for q in range(2):
                    turn_take(W[:, 4096 + kt * 1024 + q * 512:4096 + kt * 1024 + (q + 1) * 512], psT[:])
            f = zu(OF)
            link(ts(f, f, V("bf"), None, ALU.add))
            dve.tensor_copy(lrow[:], f).then_inc(f_act, 1)
            link(ts(f, f, 0.0, None, ALU.min))
            dve.wait_ge(f_act, 3)
            link(tt(f, f, lrow[:], ALU.subtract))
            link(dve.memset(lrow[:], 1.0))
            link(dve.tensor_tensor_scan(var[:, 0:S], lrow[:], f, 0.0, ALU.mult, ALU.add))
            link(ts(f, var[:, 0:S], 8.0, None, ALU.mult))
            for q in (0, 64):
                dve.tensor_copy(lrow[q:q + 32, :], f[q:q + 32, :])
                m = dve.memset(lrow[q + 32:q + 64, :], -1.0)
            link(m)
            for q in (0, 64):
                m = dve.memset(Z[q:q + 32, OF * S:(OF + 1) * S], 1.0)
            link(m)
            for h in range(16):
                m = ts(W[:, h * S:(h + 1) * S], f, C("ind", 1, P, h), None, ALU.mult)
            m.then_inc(f_ready, 1)
            attention("forget")
            residual("oout", 48 + 16)
            peer(1)
            norm(7, lambda k: V("final2", k))

        @block.scalar
        def _(act):
            steps = [0]

            def link(ins):
                steps[0] += 1
                ins.then_inc(act_step, 1)
                act.wait_ge(act_step, steps[0])

            def f(o, i, fn, **k):
                return act.activation(o, i, fn, **k)

            def norm(n, done, count):
                act.wait_ge(done, count)
                f(N[:], X[:], ACT.Square).then_inc(sq_ready, 1)
                act.wait_ge(rv_ready, n + 1 + (n > 3))
                f(rstd[:, 0:S], var[:, 0:S], ACT.Sqrt).then_inc(rstd_ready, 1)

            def attention(kind):
                js = JOBS[kind]

                def exps(jb):
                    n, b = jb["n"], jb["n"] % 2
                    w = keys_of(jb["T"])
                    act.wait_ge(smax_ready, n + 1)
                    if n >= 2:
                        act.wait_ge(pt_ready, n - 1)
                    for m in range(2):
                        ins = f(Pb[:, b, m * S:m * S + w], Sb[:, b, m * S:m * S + w], ACT.Exp,
                                bias=mx[:, b, 2 + m:3 + m], accum_out=sums[:, b, m:m + 1])
                    ins.then_inc(exp_done, 1)

                def turned_maps(jb):
                    n, T = jb["n"], jb["T"]
                    act.wait_ge(pt_ready, n + 1)
                    if n >= 2:
                        act.wait_ge(o_ready, n - 1)
                    w = 2 * (T + 1) * P
                    f(PT[:, n % 2, 0:w], psT[:, 0:w], ACT.Copy).then_inc(pt_copied, 1)

                exps(js[0])
                for a, jb in enumerate(js):
                    if a + 1 < len(js):
                        exps(js[a + 1])
                    turned_maps(jb)

            act.dma_start(X[:], x_dram).then_inc(x_in, 16)
            act.dma_start(crow[:], c_row.partition_broadcast(P)).then_inc(c_in, 16)
            act.dma_start(wsm[:], small).then_inc(small_in, 16)
            act.wait_ge(vec_in, 16)
            act.wait_ge(c_in, 16)
            f(crow[:], crow[:], ACT.Silu).then_inc(csil_ready, 1)
            norm(0, x_in, 16)
            act.wait_ge(out_taken, OUT0["in"] + 45)
            f(zu(ZG), zu(ZG), ACT.Sigmoid).then_inc(gates_ready, 1)
            for a in range(4):
                act.wait_ge(unit_done, UNIT0["cmp"] + 2 * a + 2)
                f(hid(a // 2, a % 2), psL[:, a, 0:30], ACT.Gelu_apprx_tanh).then_inc(out_taken, 1)
            act.wait_ge(csub_ready, 1)
            cp3 = cprob.rearrange("p (c n) -> p c n", n=16)[:, :, 0:NCMP]
            f(cp3, cp3, ACT.Exp).then_inc(cexp_ready, 1)
            attention("nsa")
            for a, (dst, bname) in enumerate(((Wt[1], "b_a"), (Wt[2], "b_i"))):
                for k in range(KC):
                    if k < KC - 1:
                        act.wait_ge(h_ready, a * 7 + k + 1)
                    else:
                        act.wait_ge(unit_done, UNIT0["lru"] + a + 1)
                    m = f(dst[:, k * S:(k + 1) * S], psL[:, (a * KC + k) % 4, 0:S], ACT.Sigmoid, bias=V(bname, k))
                    m.then_inc(out_taken, 1)
            act.wait_ge(out_taken, OUT0["lru"] + 16)
            f(zu(ZGA, 16), zu(ZGA, 16), ACT.Sigmoid).then_inc(sig_ready, 1)
            link(f(tiny[:, 40:48], V("lam", 0, 8), ACT.Abs))
            link(f(tiny[:, 40:48], tiny[:, 40:48], ACT.Exp, scale=-1.0))
            f(tiny[:, 40:48], tiny[:, 40:48], ACT.Ln, bias=1.0).then_inc(lru_act, 1)
            act.wait_ge(lru_dve, 2)
            for k in range(KC):
                c = slice(k * S, (k + 1) * S)
                f(Wt[3][:, c], Wt[1][:, c], ACT.Exp, scale=tiny[:, 48 + k:49 + k])
            for k in range(KC):
                c = slice(k * S, (k + 1) * S)
                m = f(Wt[2][:, c], Wt[1][:, c], ACT.Tanh, scale=tiny[:, 40 + k:41 + k])
            m.then_inc(lru_act, 1)
            act.wait_ge(lru_dve, 3)
            f(Wt[2][:], Wt[2][:], ACT.Sqrt).then_inc(lru_act, 1)
            f(zu(ZGR, 8), zu(ZGR, 8), ACT.Gelu_apprx_tanh).then_inc(lru_act, 1)
            norm(1, out_taken, OUT0["out"] + 8)
            rounds(act, 32, lambda j, i: (
                act.wait_ge(vec_in, 16), act.wait_ge(unit_done, UNIT0["mlp1"] + i * 8 + j + 1),
                f(Z[:, bass.ds(i * 8 * S + j * S, S)], psL[:, j % 4, 0:S], ACT.Relu).then_inc(out_taken, 1)))
            norm(2, out_taken, OUT0["mlp2"] + 8)
            norm(3, n_ready, 3)
            act.wait_ge(lam_sum, 1)
            f(tiny[:, 56:58], psO[:, 256:258], ACT.Exp).then_inc(lam_exp, 1)
            act.wait_ge(out_taken, OUT0["ein"] + 24)
            f(AT[:, 0:512], zu(ECKV, 2), ACT.Square).then_inc(ckv_sq, 1)
            act.wait_ge(rv_ready, 5)
            f(rstd[:, 0:S], var[:, 0:S], ACT.Sqrt).then_inc(ckv_ready, 1)
            for n in range(16):
                act.wait_ge(li_ready, n + 1)
                if n >= 2:
                    act.wait_ge(li_added, n - 1)
                w = keys_of(n // 8)
                f(work[:, n % 2, 0:w], psS[:, n % 2, 0:w], ACT.Relu, scale=0.125).then_inc(li_relu, 1)
            attention("dsa")
            attention("diff")
            act.wait_ge(o_copied, 32)
            f(N[:, 0:1024], AT[:, 1024:2048], ACT.Square).then_inc(od_sq, 1)
            for m_ in range(2):
                act.wait_ge(od_rv, m_ + 1)
                f(rstd[:, 0:512], rstd[:, 0:512], ACT.Sqrt).then_inc(od_rstd, 1)

            def peer(l):
                norm(4 + 2 * l, out_taken, OUT0["eout" if l == 0 else "oout"] + 8)
                for T in range(NT):
                    if T:
                        act.wait_ge(idx_ready, l * NT + T)
                    for q in range(4):
                        n = (l * NT + T) * 4 + q
                        act.wait_ge(key_scores, n + 1)
                        f(Z[:, 24 * S + q * 512:24 * S + (q + 1) * 512], psS[:, n % 2, :], ACT.Copy
                          ).then_inc(key_taken, 1)
                    act.wait_ge(best_in, l * NT + T + 1)
                    g_ = gate[:, T * SLOTS:(T + 1) * SLOTS]
                    f(g_, g_, ACT.Exp).then_inc(gexp, 1)
                for T in range(NT):
                    act.wait_ge(row_used, (l * 4 + T + 1) * SLOTS)
                    d_ = dots[:, T * SLOTS:(T + 1) * SLOTS]
                    f(d_, d_, ACT.Gelu_apprx_tanh).then_inc(act_ready, 1)

            peer(0)
            norm(5, turn_taken, TURNS_PEER[0])
            act.wait_ge(f_act, 1)
            link(f(lrow[:], lrow[:], ACT.Abs))
            f(lrow[:], lrow[:], ACT.Exp, scale=-1.0).then_inc(f_act, 1)
            act.wait_ge(f_act, 2)
            f(lrow[:], lrow[:], ACT.Ln, bias=1.0).then_inc(f_act, 1)
            attention("forget")
            peer(1)
            norm(7, turn_taken, TURNS_PEER[1])


def kernel(**a):
    import numpy as np
    import concourse.bacc as bacc
    from concourse.bass_utils import run_bass_kernel_spmd

    a = {k: np.asarray(v) for k, v in a.items()}
    f = np.float32

    def units(w):
        n = w.shape[1] // P
        return w.reshape(KC, P, n, P).transpose(2, 1, 0, 3).reshape(n, P, KC * P)

    def cols(w, *parts):
        u = np.zeros((w.shape[0], P), f)
        for start, count, place in parts:
            u[:, place:place + count] = w[:, start:start + count]
        return u

    w = a["w_in"][0]
    pieces = [cols(w, (64 * j, 64, 0), (64 * (j + 4), 64, 64)) for j in range(4)]
    for start in (512, 640):
        pieces += [cols(w, (start + 64 * g, 64, 0), (start + 64 * g, 64, 64)) for g in range(2)]
    pieces += [w[:, 768:1280], cols(w, (1280, 24, 0)), w[:, 1304:5400]]
    stream = {"in": units(np.concatenate(pieces, 1))}
    stream["cmp"] = np.concatenate([
        units(a[n][0][1024 * u:1024 * (u + 1), P * m:P * (m + 1)])
        for n in ("cmp_k_w1", "cmp_v_w1") for m in range(2) for u in range(2)])
    lru = np.zeros((2, P, KC, P), f)
    for n, key in enumerate(("lru_w_a", "lru_w_i")):
        for h in range(16):
            r = slice(64 * (h % 2), 64 * (h % 2) + 64)
            lru[n, r, h // 2, r] = a[key][0, h]
    stream["lru"] = lru.reshape(2, P, KC * P)
    up = a["w_up_attn"][0].reshape(8, 64, D)[[0, 4, 1, 5, 2, 6, 3, 7]].reshape(4, P, 4, 2, P)
    stream["upattn"] = up.transpose(2, 1, 3, 0, 4).reshape(4, P, KC * P)
    stream["uprnn"] = units(a["w_up_rnn"][0])
    stream["out"] = units(a["w_out"][0])
    stream["mlp1"] = units(a["mlp_w1"][0])
    stream["mlp2"] = a["mlp_w2"][0].reshape(4, KC, P, 8, P).transpose(3, 0, 2, 1, 4).reshape(32, P, KC * P)
    w = a["even_w_in_2"][0]
    stream["ein"] = units(np.concatenate([w[:, 0:1280], cols(w, (1280, 64, 0), (1280, 64, 64)),
                                          cols(w, (1344, 8, 0)), w[:, 1352:2888]], 1))
    uk = a["a_w_uk_2"][0].reshape(2, P, 4, P).transpose(1, 2, 0, 3).reshape(P, KC * P)
    uv = a["a_w_uv_2"][0].reshape(2, P, 512).transpose(1, 0, 2).reshape(P, KC * P)
    stream["ukv"] = np.stack([uk, uv])
    stream["eout"] = units(a["even_w_out_2"][0])
    w = a["odd_w_in_2"][0]
    stream["oin"] = units(np.concatenate(
        [w[:, 0:3072], cols(w, *[(3072, 16, q) for q in (0, 32, 64, 96)])], 1))
    stream["oout"] = units(a["odd_w_out_2"][0])
    for l in range(2):
        stream[f"pq{l}"] = units(a["peer_w_q_2"][l])
    weights = np.ascontiguousarray(np.concatenate([stream[n] for n, _, _ in STREAM]))

    w2k, w2v = a["cmp_k_w2"][0].reshape(2, P, 64), a["cmp_v_w2"][0].reshape(2, P, 64)
    small = np.ascontiguousarray(np.concatenate(
        [np.concatenate([w2k, w2k], 2).transpose(1, 0, 2).reshape(P, 256),
         w2v.transpose(1, 0, 2).reshape(P, 128),
         a["peer_sub_keys_2"].transpose(3, 0, 1, 2).reshape(P, 512)], 1))

    def fm(v):
        return v.reshape(-1, P).T

    def rows(v):
        return np.concatenate([v, np.zeros((P - v.shape[0], v.shape[1]), f)])

    bf = np.zeros((P, 1), f)
    for q in (0, 32, 64, 96):
        bf[q:q + 16, 0] = a["odd_b_forget_2"][0]
    vecs = {
        "norm1": fm(a["norm1_w"]), "norm2": fm(a["norm2_w"]), "final1": fm(a["final_norm_w"]),
        "conv_w": fm(a["conv_w"]), "conv_b": fm(a["conv_b"]), "b_a": fm(a["lru_b_a"]), "b_i": fm(a["lru_b_i"]),
        "lam": fm(a["lru_lambda"]), "c": fm(a["c_2"]), "ada_b": fm(a["ada_b_2"]), "mix": fm(a["norm_mix_2"]),
        "ffn": fm(a["norm_ffn_2"]), "final2": fm(a["norm_final_2"]), "kvn": fm(a["a_kv_norm_2"]),
        "subln": fm(a["b_subln_2"]), "bf": bf, "pos_k": fm(a["cmp_pos_k"]), "pos_v": fm(a["cmp_pos_v"]),
        "blam": rows(a["b_lambda_2"][0].T), "rel": rows(a["rel_bias_2"]),
    }
    vecs = np.ascontiguousarray(np.concatenate([vecs[n] for n in VEC], 1))

    q, k = np.arange(P)[:, None], np.arange(P)[None, :]
    t, n = np.arange(S), np.arange(16)
    seen = (n[None, :] < NCMP) & (16 * n[None, :] + 31 <= t[:, None])
    cmask = seen.reshape(NT, P, 16).transpose(1, 0, 2).reshape(P, 32).astype(f)
    dist = np.arange(S)
    big = 16 + (np.log(np.maximum(dist, 1).astype(f) / 16) / math.log(8) * 16).astype(np.int32)
    bucket = np.where(dist < 16, dist, np.minimum(big, 31))
    buckets = np.zeros((P, 384), f)
    buckets[bucket[::-1], np.arange(S)] = 1
    cons = {
        "ident": np.eye(P, dtype=f), "flip": np.ascontiguousarray(np.eye(P, dtype=f)[::-1]), "mean": np.full((P, P), 1 / D, f), "mean128": np.full((P, P), 1 / P, f),
        "ones": np.ones((P, P), f),
        "causal": np.concatenate([np.zeros((P, P), f), np.where(k <= q, 0, NEG).astype(f)], 1),
        "cmask": cmask, "cbias": np.where(cmask > 0, 0, NEG).astype(f),
        "iota": np.tile(np.arange(16, dtype=f), (P, 1)), "buckets": buckets,
        "ind": ((np.arange(P)[:, None] % 32) == n[None, :]).astype(f),
    }
    cons = np.ascontiguousarray(np.concatenate([cons[n] for n in CON], 1))

    ins = {
        "x_dram": np.ascontiguousarray(a["x"].reshape(S, KC, P).transpose(2, 1, 0).reshape(P, KC * S)),
        "c_row": a["c_2"].reshape(D),
        "ada": np.ascontiguousarray(a["ada_w_2"].transpose(0, 2, 1)).reshape(96, P, D), "weights": weights, "small": small, "vecs": vecs, "cons": cons,
        "experts_u": a["peer_u_2"].reshape(2 * NEXP, D), "experts_v": a["peer_v_2"].reshape(2 * NEXP, D),
    }
    nc = bacc.Bacc("TRN2", target_bir_lowering=False, num_devices=1)
    aps = {k: nc.dram_tensor(k, v.shape, F32, kind="ExternalInput").ap() for k, v in ins.items()}
    out = nc.dram_tensor("out", (P, KC * S), F32, kind="ExternalOutput").ap()
    build(nc, out=out, **aps)
    r = run_bass_kernel_spmd(nc, [ins], core_ids=[0])
    y = r.results[0]["out"]
    return y.reshape(P, KC, S).transpose(2, 1, 0).reshape(1, S, D)
```

```python
import math
from contextlib import ExitStack

import concourse.bass as bass
from concourse import mybir

F32 = mybir.dt.float32
U32 = mybir.dt.uint32
ACT = mybir.ActivationFunctionType
ALU = mybir.AluOpType
AX = mybir.AxisListType

P = 128
S = 256
NT = S // P
D = 1024
KC = D // P
WRING = 8
ARING = 4
GRING = 8
NEG = -1e30
EPS = 1e-6
NCMP = 15
NKEYS = 128
NEXP = NKEYS * NKEYS
TOPK = 16
PH = 8
SLOTS = PH * TOPK
LAM_INIT = 0.8 - 0.6 * math.exp(-0.3 * 0)

STREAM = [("in", 45, 45), ("cmp", 8, 4), ("lru", 2, 16), ("upattn", 4, 8),
          ("uprnn", 8, 8), ("out", 8, 8), ("mlp1", 32, 32), ("mlp2", 32, 8), ("ein", 24, 24),
          ("ukv", 2, 6), ("eout0", 8, 8), ("pq00", 16, 16), ("eout1", 8, 8), ("pq01", 16, 16),
          ("oin0", 25, 25), ("oout0", 8, 8), ("pq10", 16, 16), ("oin1", 25, 25), ("oout1", 8, 8),
          ("pq11", 16, 16)]
UNIT0, OUT0 = {}, {}
_u, _o = 0, 0
for _n, _a, _b in STREAM:
    UNIT0[_n], OUT0[_n] = _u, _o
    _u, _o = _u + _a, _o + _b
UNITS = _u
N_OUT = {n: b for n, _, b in STREAM}

ZQ, ZKC, ZVC, ZKS, ZVS, ZKW, ZVW, ZG, ZXR, ZGR, ZGA, ZGB = 0, 4, 6, 8, 9, 10, 11, 12, 13, 21, 29, 37
EQA, ECKV, EQI, EKI, EWI, EQB, EKB, EVB = 0, 4, 6, 10, 11, 12, 16, 20
OQ, OK, OV, OF = 0, 8, 16, 24

VEC = {}
_c = 0
for _n, _w in [("norm1", 8), ("norm2", 8), ("final1", 8), ("conv_w", 32), ("conv_b", 8), ("b_a", 8),
               ("b_i", 8), ("lam", 8), ("c", 8), ("ada_b", 96), ("mix", 16), ("ffn", 16), ("final2", 8),
               ("kvn", 2), ("subln", 1), ("bf", 1), ("pos_k", 16), ("pos_v", 16), ("blam", 4),
               ("rel", 12)]:
    VEC[_n] = _c
    _c += _w
NVEC = _c
CON = {}
_c = 0
for _n, _w in [("ident", 128), ("flip", 128), ("mean", 128), ("mean128", 128), ("ones", 128), ("causal", 256),
               ("cmask", 32), ("cbias", 32), ("iota", 16), ("buckets", 384), ("ind", 16)]:
    CON[_n] = _c
    _c += _w
NCON = _c


def build(nc, x_dram, c_row, ada, weights, small, vecs, cons, experts_u, experts_v, out):
    ctx = ExitStack()
    with ctx:
        def sb(name, shape, dt=F32):
            return ctx.enter_context(nc.sbuf_tensor(name, shape, dt))

        def ps(name, shape):
            return ctx.enter_context(nc.psum_tensor(name, shape, F32))

        def sem(name):
            return ctx.enter_context(nc.semaphore(name))

        wring = [sb(f"wring{i}", [P, KC * P]) for i in range(WRING)]
        X = sb("X", [P, KC * S])
        N = sb("N", [P, KC * S])
        Z = sb("Z", [P, 45 * S])
        W = sb("W", [P, GRING * D])
        AT = sb("AT", [P, KC * S])
        vec = sb("vec", [P, NVEC])
        con = sb("con", [P, NCON])
        wsm = sb("wsm", [P, 896])
        bias = sb("bias", [P, 12 * P + 12 * S])
        relrow = sb("relrow", [12, 384])
        mod = sb("mod", [P, 96])
        crow = sb("crow", [P, D])
        aring = sb("aring", [P, ARING, D])
        amul = sb("amul", [P, 4 * KC])
        rstd = sb("rstd", [P, 2 * S])
        var = sb("var", [P, 2 * S])
        Sb = sb("Sb", [P, 2, 512])
        Pb = sb("Pb", [P, 2, 512])
        PT = sb("PT", [P, 2, 512])
        mx = sb("mx", [P, 2, 8])
        sums = sb("sums", [P, 2, 8])
        facs = sb("facs", [P, 2, 8])
        VT = sb("VT", [P, 4 * 512])
        G = sb("G", [P, NT, 24])
        sel = [Z[:, u * S:(u + 1) * S] for u in (44, 28)]
        work = Z[:, 42 * S:44 * S].rearrange("p (t s) -> p t s", t=2)
        m8 = sb("m8", [P, NT, 8])
        wi = sb("wi", [P, NT, 8])
        tiny = sb("tiny", [P, 64])
        stage = sb("stage", [P, 4, 4], U32)
        lrow = crow[:, 0:S]
        idx = crow[:, S:S + NT * SLOTS].bitcast(U32)
        dots = crow[:, 2 * S:2 * S + NT * SLOTS]
        gate = crow[:, 3 * S:3 * S + NT * SLOTS]
        psL = ps("psL", [P, 4, 512])
        psS = ps("psS", [P, 2, 512])
        psT = ps("psT", [P, 512])
        psO = ps("psO", [P, 512])
        reld = nc.dram_tensor("rel_rows", [12, 384], F32, kind="Internal").ap()

        def V(name, a=0, b=None):
            b = a + 1 if b is None else b
            return vec[:, VEC[name] + a:VEC[name] + b]

        def C(name, w, parts=P, a=0):
            return con[0:parts, CON[name] + a:CON[name] + a + w]

        def zu(u, n=1, parts=slice(0, P)):
            return Z[parts, u * S:(u + n) * S]

        def chunk(t, k, n=1):
            return t[:, k * S:(k + n) * S]

        def toks(t, u, T, parts=slice(0, P), w=P):
            return t[parts, u * S + T * P:u * S + T * P + w]

        def hid(kv, m):
            a = 1024 + (kv * 2 + m) * 32
            return W[:, a:a + 30]

        bias0, bias1 = bias[:, 0:12 * P], bias[:, 12 * P:]
        FK = aring[:].rearrange("p a d -> p (a d)")
        h_t = [Z[:, (29 + 4 * T) * S:(33 + 4 * T) * S] for T in range(NT)]
        acc = [Z[:, (37 + 4 * T) * S:(41 + 4 * T) * S] for T in range(NT)]

        def query(l, T, hp):
            if l == 0:
                return Z[:, 4 * S + hp * P:4 * S + (hp + 1) * P]
            return toks(Z, (OQ if hp < 8 else OV) + hp % 8, T)

        def scratch(l, T):
            if l == 0 and T == 0:
                return Z[:, 33 * S:41 * S], [Z[:, u * S:(u + 1) * S] for u in (41, 42, 43, 20, 21, 22, 23)]
            return bias[:, 0:8 * S], [bias[:, u * S:(u + 1) * S] for u in range(8, 15)]

        def tile_of(t, u, n, T):
            return t[:, u * S:(u + n) * S].rearrange("p (c s) -> p c s", s=S)[:, :, T * P:(T + 1) * P]

        cprob, kcT, VTc = W[:, 1280:1536], W[:, 1536:1552], W[:, 1664:1792]
        Wt = [W[:, i * KC * S:(i + 1) * KC * S] for i in range(4)]
        ident = C("ident", P)

        x_in, vec_in, con_in, small_in = sem("x_in"), sem("vec_in"), sem("con_in"), sem("small_in")
        landed = [sem(f"unit_landed{i}") for i in range(WRING)]
        unit_done, out_taken = sem("unit_done"), sem("out_taken")
        relrow_ready, relrow_copied, rel_stored = sem("relrow_ready"), sem("relrow_copied"), sem("rel_stored")
        rel_loaded, flipped, bias_ready = sem("rel_loaded"), sem("flipped"), sem("bias_ready")
        c_in, csil_ready, ada_used = sem("c_in"), sem("csil_ready"), sem("ada_used")
        ada_landed = [sem(f"ada_landed{i}") for i in range(ARING)]
        sq_ready, ss_ready, rv_ready, rstd_ready, n_ready = (
            sem(n) for n in ("sq_ready", "ss_ready", "rv_ready", "rstd_ready", "n_ready"))
        dve_step, act_step = sem("dve_step"), sem("act_step")
        scores_ready, smax_ready, exp_done, p_ready = (
            sem(n) for n in ("scores_ready", "smax_ready", "exp_done", "p_ready"))
        pt_ready, pt_copied, o_ready, o_copied = (
            sem(n) for n in ("pt_ready", "pt_copied", "o_ready", "o_copied"))
        turned, turn_taken = sem("turned"), sem("turn_taken")
        gates_ready = sem("gates_ready")
        flat_ready, kv2_ready, kv2_taken = (sem(n) for n in ("flat_ready", "kv2_ready", "kv2_taken"))
        cs_ready, csub_ready, cexp_ready, cp_ready, cpt_ready = (
            sem(n) for n in ("cs_ready", "csub_ready", "cexp_ready", "cp_ready", "cpt_ready"))
        xc_ready, lru_act, lru_dve, h_ready = (sem(n) for n in ("xc_ready", "lru_act", "lru_dve", "h_ready"))
        sig_ready, hsq_ready, pair_ready = sem("sig_ready"), sem("hsq_ready"), sem("pair_ready")
        ckv_sq, ckv_ss, ckv_ready = sem("ckv_sq"), sem("ckv_ss"), sem("ckv_ready")
        lam_in, lam_sum, lam_exp = sem("lam_in"), sem("lam_sum"), sem("lam_exp")
        li_ready, li_relu, li_added, sel_ready = (
            sem(n) for n in ("li_ready", "li_relu", "li_added", "sel_ready"))
        od_sq, od_ss, od_rv, od_rstd, od_ready = (
            sem(n) for n in ("od_sq", "od_ss", "od_rv", "od_rstd", "od_ready"))
        f_act, f_ready = sem("f_act"), sem("f_ready")
        key_scores, key_taken, best_in, gexp = (
            sem(n) for n in ("key_scores", "key_taken", "best_in", "gexp"))
        idx_ready, staged, gather_next = sem("idx_ready"), sem("staged"), sem("gather_next")
        row_landed = [sem(f"row_landed{j}") for j in range(GRING)]
        row_used, act_ready = sem("row_used"), sem("act_ready")
        stored = sem("stored")

        def weights_at(eng, name, j, i=0):
            g = UNIT0[name] + j
            eng.wait_ge(landed[g % WRING], (i + g // WRING + 1) * 16)
            return wring[g % WRING]

        def rounds(eng, n, body, per=8, peel=False):
            full = n // per
            for j in range(per if peel else 0):
                body(j, 0)
            if full > 1:
                with eng.Fori(int(peel), full) as i:
                    for j in range(per):
                        body(j, i)
            else:
                full = 0
            for m in range(full * per, n):
                body(m % per, m // per)

        def keys_of(T):
            return P * (T + 1)

        def causal(T):
            return con[:, CON["causal"] + P * (1 - T):CON["causal"] + S]

        def relbias(h, T):
            return bias0[:, h * P:(h + 1) * P] if T == 0 else bias1[:, h * S:(h + 1) * S]

        jobs = []
        for T in range(NT):
            for h in range(8):
                j, b = h % 4, h // 4
                rows = slice(64 * b, 64 * b + 64)
                jobs.append(dict(kind="nsa", T=T, rows=[rows, rows], q=[ZQ + j] * 2, k=[ZKS, ZKW],
                                 bias=[causal(T)] * 2,
                                 fac=[G[:, T, 3 * h + 1:3 * h + 2], G[:, T, 3 * h + 2:3 * h + 3]],
                                 v=[lambda kt: VT[:, kt * P:(kt + 1) * P],
                                    lambda kt: VT[:, (2 + kt) * P:(3 + kt) * P]],
                                 slot=[0, 0], cmp=T * 8 + h, outs=[(0, rows, j)]))
        for T in range(NT):
            for j in range(4):
                jobs.append(dict(kind="dsa", T=T, rows=[slice(0, 64), slice(64, 128)],
                                 q=[EQA + j] * 2, k=[24 + j] * 2,
                                 bias=[relbias(2 * j, T), relbias(2 * j + 1, T)], fac=[None, None],
                                 v=[lambda kt, j=j: VT[:, kt * 512 + j * P:kt * 512 + (j + 1) * P]] * 2,
                                 slot=[0, 1], cmp=None,
                                 outs=[(0, slice(0, 64), j), (1, slice(64, 128), j)]))
            for h in range(4):
                jobs.append(dict(kind="diff", T=T, rows=[slice(0, 64), slice(64, 128)],
                                 q=[EQB + h] * 2, k=[EKB + h] * 2, bias=[relbias(8 + h, T)] * 2,
                                 fac=[None, tiny[:, 60:61]],
                                 v=[lambda kt, h=h: VT[:, 1024 + kt * 512 + h * P:1024 + kt * 512 + (h + 1) * P]] * 2,
                                 slot=[0, 0], cmp=None, outs=[(0, slice(0, P), 4 + h)]))
        for T in range(NT):
            for j in range(8):
                jobs.append(dict(kind="forget", T=T, rows=[slice(0, 64), slice(64, 128)],
                                 q=[OQ + j] * 2, k=[OK + j] * 2, bias=[causal(T)] * 2, fac=[None, None],
                                 v=[lambda kt, j=j: VT[:, kt * 1024 + j * P:kt * 1024 + (j + 1) * P]] * 2,
                                 slot=[0, 1], cmp=None, head=[2 * j, 2 * j + 1],
                                 outs=[(0, slice(0, 64), j), (1, slice(64, 128), j)]))
        for n, jb in enumerate(jobs):
            jb["n"] = n
        JOBS = {"nsa": jobs[0:16], "even0": jobs[16:24], "even1": jobs[24:32],
                "odd0": jobs[32:40], "odd1": jobs[40:48]}

        ROUNDS = SLOTS // GRING
        NORM = {"even0": 4, "even1": 5, "odd0 mix": 6, "odd0": 7, "odd1 mix": 8, "odd1": 9, "final": 10}
        TURNS_PEER = {(0, 0): 11, (0, 1): 17, (1, 0): 23, (1, 1): 25}

        block = ctx.enter_context(nc.Block())

        @block.sync
        def _(sp):
            sp.dma_start(vec[:], vecs).then_inc(vec_in, 16)
            sp.dma_start(con[:], cons).then_inc(con_in, 16)

            def unit(j, i):
                g = i * WRING + j
                if not isinstance(g, int) or g >= WRING:
                    sp.wait_ge(unit_done, g - WRING + 1)
                src = weights[g] if isinstance(g, int) else weights[bass.ds(g, 1)].rearrange("a p n -> (a p) n")
                sp.dma_start(wring[j][:], src).then_inc(landed[j], 16)

            for j in range(WRING):
                unit(j, 0)
            sp.wait_ge(relrow_copied, 1)
            sp.dma_start(reld, relrow[:]).then_inc(rel_stored, 16)
            sp.wait_ge(rel_stored, 16)
            for T in range(NT):
                w = keys_of(T)
                src = bass.AP(tensor=reld.tensor, offset=P - T * P, ap=[[1, P], [384, 12], [1, w]])
                dst = W[:, T * 12 * P:T * 12 * P + 12 * w]
                sp.dma_start(dst.rearrange("p (h w) -> p h w", h=12), src).then_inc(rel_loaded, 16)
            with sp.Fori(1, UNITS // WRING) as i:
                for j in range(WRING):
                    unit(j, i)
            for g in range(UNITS // WRING * WRING, UNITS):
                unit(g % WRING, g // WRING)
            sp.wait_ge(n_ready, NORM["final"] + 1)
            sp.dma_start(out, N[:]).then_inc(stored, 16)
            sp.wait_ge(stored, 16)

        @block.gpsimd
        def _(pool):
            def ada_load(j, i):
                if not isinstance(i, int):
                    pool.wait_ge(ada_used, i * ARING + j - ARING + 1)
                    src = ada[bass.ds(i * ARING + j, 1)].rearrange("a p n -> (a p) n")
                else:
                    src = ada[j]
                pool.dma_start(aring[:, j, :], src).then_inc(ada_landed[j], 16)

            for j in range(ARING):
                ada_load(j, 0)
            with pool.Fori(1, 96 // ARING) as i:
                for j in range(ARING):
                    ada_load(j, i)
            per, group = 2 * GRING, 4
            for l in range(2):
                for T in range(NT):
                    for n, table in enumerate((experts_u, experts_v)):
                        loop = (l * NT + T) * 2 + n
                        used0 = loop * SLOTS
                        rounds_ = SLOTS // per
                        pool.wait_ge(idx_ready, l * NT + T + 1)

                        def gathers(i, first):
                            for q in range(per // group):
                                if not first:
                                    pool.wait_ge(row_used, i * per + used0 + q * group + group - per)
                                pool.tensor_copy(stage[:, q, :],
                                                 idx[:, bass.ds(i * per + T * SLOTS + q * group, group)]
                                                 ).then_inc(staged, 1)
                                for j in range(group):
                                    c = q * group + j
                                    slot = c % GRING
                                    if j == 0:
                                        pool.wait_ge(staged, i * (per // group) + loop * rounds_ * (per // group) + q + 1)
                                    if not (first and c < GRING):
                                        pool.wait_ge(row_used, i * per + used0 + c - GRING + 1)
                                    pool.sem_inc(gather_next, 1)
                                    pool.indirect_dma_start(
                                        W[:, slot * D:(slot + 1) * D], None, table,
                                        bass.IndirectOffsetOnAxis(ap=stage[:, q, j:j + 1], axis=0)
                                    ).then_inc(row_landed[slot], 16)

                        if loop == 0:
                            gathers(0, True)
                        with pool.Fori(1 if loop == 0 else 0, rounds_) as i:
                            gathers(i, False)

        @block.tensor
        def _(pe):
            def mm(o, l, r, first=True, last=True):
                return pe.matmul(o, l, r, start=first, stop=last)

            def project(name, rhs, cols=S):
                if OUT0[name]:
                    pe.wait_ge(out_taken, OUT0[name])

                def unit(j, i):
                    w = weights_at(pe, name, j, i)
                    if not (isinstance(i, int) and OUT0[name] + i * 8 + j < 4):
                        pe.wait_ge(out_taken, OUT0[name] + i * 8 + j - 3)
                    for k in range(KC):
                        m = mm(psL[:, j % 4, 0:cols], w[:, k * P:(k + 1) * P], rhs(k), k == 0, k == KC - 1)
                    m.then_inc(unit_done, 1)

                rounds(pe, N_OUT[name], unit, peel=OUT0[name] == 0)

            def norm_sum(n, T=None):
                pe.wait_ge(sq_ready, n + 1)
                for k in range(KC):
                    m = mm(psO[:, 0:S if T is None else P], C("mean", P),
                           chunk(N, k) if T is None else toks(N, k, T), k == 0, k == KC - 1)
                m.then_inc(ss_ready, 1)

            def attention(kind):
                js = JOBS[kind]
                if kind in ("even1", "odd0", "odd1"):
                    pe.wait_ge(key_taken, {"even1": 4, "odd0": 8, "odd1": 12}[kind])

                def scores(jb):
                    n, T = jb["n"], jb["T"]
                    if n >= 2:
                        pe.wait_ge(smax_ready, n - 1)
                    w = keys_of(T)
                    for m in range(2):
                        r = jb["rows"][m]
                        o = (psL if m else psS)[:, n % 2, 0:w]
                        last = mm(o, toks(Z, jb["q"][m], T, r), toks(Z, jb["k"][m], 0, r, w),
                                  True, jb["kind"] != "forget")
                        if jb["kind"] == "forget":
                            h = jb["head"][m]
                            last = mm(o, lrow[r, 0:P], FK[r, h * S:h * S + w], False, True)
                    last.then_inc(scores_ready, 1)

                def values(jb):
                    n, T = jb["n"], jb["T"]
                    pe.wait_ge(p_ready, n + 1)
                    if n >= 1:
                        pe.wait_ge(pt_copied, n)
                    at = 0
                    for m in range(2):
                        for kt in range(T + 1):
                            last = pe.transpose(psT[:, at * P:(at + 1) * P],
                                                Pb[:, n % 2, m * S + kt * P:m * S + (kt + 1) * P], ident)
                            at += 1
                    last.then_inc(pt_ready, 1)
                    pe.wait_ge(pt_copied, n + 1)
                    if n >= 1:
                        pe.wait_ge(o_copied, n)
                    for slot in sorted(set(jb["slot"])):
                        parts = [(m, kt) for m in range(2) if jb["slot"][m] == slot for kt in range(T + 1)]
                        o = psO[:, slot * P:(slot + 1) * P]
                        for a, (m, kt) in enumerate(parts):
                            at = m * (T + 1) + kt
                            last = mm(o, jb["v"][m](kt), PT[:, n % 2, at * P:(at + 1) * P], a == 0,
                                      a == len(parts) - 1 and jb["cmp"] is None)
                        if jb["cmp"] is not None:
                            c = jb["cmp"]
                            last = mm(o, VTc[0:NCMP, 0:P], W[0:NCMP, 6144 + c * P:6144 + (c + 1) * P],
                                      False, True)
                    last.then_inc(o_ready, 1)

                scores(js[0])
                scores(js[1])
                for a, jb in enumerate(js):
                    values(jb)
                    if a + 2 < len(js):
                        scores(js[a + 2])

            turns = [0]

            def turn(pairs, tile=psT):
                if turns[0]:
                    pe.wait_ge(turn_taken, turns[0])
                for o, src in pairs:
                    last = pe.transpose(o, src, ident)
                last.then_inc(turned, 1)
                turns[0] += 1

            pe.wait_ge(vec_in, 16)
            pe.wait_ge(con_in, 16)
            mm(psO[0:12, 0:384], vec[0:32, VEC["rel"]:VEC["rel"] + 12], C("buckets", 384, 32)
               ).then_inc(relrow_ready, 1)
            pe.wait_ge(rel_loaded, 32)
            for n in range(9):
                if n >= 2:
                    pe.wait_ge(bias_ready, n - 1)
                mm(psS[:, n % 2, :], C("flip", P), W[:, n * 512:(n + 1) * 512]).then_inc(flipped, 1)
            pe.wait_ge(relrow_copied, 1)
            norm_sum(0)
            pe.wait_ge(n_ready, 1)
            project("in", lambda k: chunk(N, k))
            pe.wait_ge(out_taken, OUT0["in"] + 45)
            turn([(psT[:, (2 * a + kt) * P:(2 * a + kt + 1) * P], toks(Z, u, kt))
                  for a, u in enumerate((ZVS, ZVW)) for kt in range(NT)])
            pe.wait_ge(gates_ready, 1)
            turn([(psT[:, T * P:(T + 1) * P], toks(Z, ZG, T)) for T in range(NT)])
            pe.wait_ge(flat_ready, 8)
            for a in range(4):
                for u in range(2):
                    w = weights_at(pe, "cmp", 2 * a + u)
                    for k in range(KC):
                        i = 8 * u + k
                        r = W[:, (a // 2) * 512 + i * 30:(a // 2) * 512 + (i + 1) * 30]
                        m = mm(psL[:, a, 0:30], w[:, k * P:(k + 1) * P], r, i == 0, i == 15)
                    m.then_inc(unit_done, 1)
            pe.wait_ge(out_taken, OUT0["cmp"] + 4)
            pe.wait_ge(small_in, 16)
            for m_ in range(2):
                mm(psO[:, 0:30], wsm[:, m_ * P:(m_ + 1) * P], hid(0, m_), m_ == 0, m_ == 1)
            for g in range(2):
                for m_ in range(2):
                    m = mm(psO[0:NCMP, 64 + g * 64:128 + g * 64], hid(1, m_)[:, g * NCMP:(g + 1) * NCMP],
                           wsm[:, 256 + m_ * 64:256 + (m_ + 1) * 64], m_ == 0, m_ == 1)
            m.then_inc(kv2_ready, 1)
            pe.wait_ge(kv2_taken, 3)
            pe.wait_ge(turn_taken, 2)
            for T in range(NT):
                for h in range(8):
                    j, b = h % 4, h // 4
                    r = slice(64 * b, 64 * b + 64)
                    m = mm((psT if b else psO)[:, (T * 4 + j) * 16:(T * 4 + j) * 16 + NCMP], toks(Z, ZQ + j, T, r),
                           kcT[r, 0:NCMP])
            m.then_inc(cs_ready, 1)
            pe.wait_ge(cp_ready, 1)
            for c in range(16):
                m = pe.transpose(psL[0:NCMP, c // 4, (c % 4) * P:(c % 4 + 1) * P],
                                 cprob[:, c * 16:c * 16 + NCMP], ident)
            m.then_inc(cpt_ready, 1)
            pe.wait_ge(kv2_taken, 5)
            attention("nsa")
            pe.wait_ge(xc_ready, 1)
            for a in range(2):
                w = weights_at(pe, "lru", a)
                for k in range(KC):
                    o = a * KC + k
                    pe.wait_ge(out_taken, OUT0["lru"] + o - 3 if o >= 4 else OUT0["lru"])
                    m = mm(psL[:, o % 4, 0:S], w[:, k * P:(k + 1) * P], Wt[0][:, k * S:(k + 1) * S])
                    m.then_inc(h_ready if k < KC - 1 else unit_done, 1)
            pe.wait_ge(out_taken, OUT0["upattn"])
            pe.wait_ge(sig_ready, 1)
            pe.wait_ge(o_copied, 16)
            for u in range(4):
                w = weights_at(pe, "upattn", u)
                for b in range(2):
                    o = 2 * u + b
                    if o >= 4:
                        pe.wait_ge(out_taken, OUT0["upattn"] + o - 3)
                    for k in range(4):
                        m = mm(psL[:, o % 4, 0:S], w[:, (b * 4 + k) * P:(b * 4 + k + 1) * P], chunk(AT, k),
                               k == 0, k == 3)
                    if b == 0:
                        m.then_inc(pair_ready, 1)
                m.then_inc(unit_done, 1)
            pe.wait_ge(lru_dve, 4)
            project("uprnn", lambda k: Wt[1][:, k * S:(k + 1) * S])
            pe.wait_ge(out_taken, OUT0["uprnn"] + 8)
            project("out", lambda k: chunk(N, k))
            norm_sum(1)
            pe.wait_ge(n_ready, 2)
            project("mlp1", lambda k: chunk(N, k))
            pe.wait_ge(out_taken, OUT0["mlp2"])
            pe.wait_ge(hsq_ready, 32)

            def mlp2_unit(j, i):
                w = weights_at(pe, "mlp2", j, i)
                if j % 4 == 0:
                    pe.wait_ge(out_taken, OUT0["mlp2"] + i * 2 + j // 4 - 1)
                for k in range(KC):
                    m = mm(psL[:, j // 4, 0:S], w[:, k * P:(k + 1) * P], chunk(Z, (j % 4) * 8 + k),
                           j % 4 == 0 and k == 0, j % 4 == 3 and k == KC - 1)
                m.then_inc(unit_done, 1)

            rounds(pe, 32, mlp2_unit)
            norm_sum(2)
            norm_sum(3)
            pe.wait_ge(n_ready, 4)
            project("ein", lambda k: chunk(N, k))
            pe.wait_ge(out_taken, OUT0["ein"] + 24)
            turn([(psT[:, T * P:(T + 1) * P], toks(Z, EWI, T)) for T in range(NT)])
            pe.wait_ge(lam_in, 1)
            pe.wait_ge(rstd_ready, 4)
            mm(psO[:, 256:258], C("ones", P, 64), tiny[0:64, 0:2]).then_inc(lam_sum, 1)
            pe.wait_ge(lam_exp, 1)
            pe.wait_ge(ckv_sq, 1)
            for k in range(2):
                m = mm(psO[:, 0:S], C("mean", P), AT[:, k * S:(k + 1) * S], k == 0, k == 1)
            m.then_inc(ckv_ss, 1)
            for T in range(NT):
                for h in range(8):
                    n = T * 8 + h
                    if n >= 2:
                        pe.wait_ge(li_relu, n - 1)
                    r = slice(64 * (h % 2), 64 * (h % 2) + 64)
                    mm(psS[:, n % 2, 0:keys_of(T)], toks(Z, EQI + h // 2, T, r),
                       toks(Z, EKI, 0, r, keys_of(T))).then_inc(li_ready, 1)
            for kt in range(NT):
                turn([(psT[:, h * P:(h + 1) * P], toks(Z, EVB + h, kt)) for h in range(4)])
            pe.wait_ge(ckv_ready, 2)
            w = weights_at(pe, "ukv", 0)
            for o in range(4):
                for k in range(2):
                    m = mm(psL[:, o, 0:S], w[:, (o * 2 + k) * P:(o * 2 + k + 1) * P], chunk(Z, ECKV + k),
                           k == 0, k == 1)
                m.then_inc(h_ready if o < 3 else unit_done, 1)
            w = weights_at(pe, "ukv", 1)
            for kt in range(NT):
                pe.wait_ge(out_taken, OUT0["ukv"] + kt + 1)
                for k in range(2):
                    m = mm(psL[:, kt, 0:512], toks(Z, ECKV + k, kt), w[:, k * 512:(k + 1) * 512],
                           k == 0, k == 1)
                m.then_inc(h_ready if kt == 0 else unit_done, 1)
            pe.wait_ge(out_taken, OUT0["ukv"] + 6)
            pe.wait_ge(li_relu, 16)
            pe.wait_ge(turn_taken, 5)
            pe.wait_ge(ckv_ready, 1)

            def even(T):
                attention(f"even{T}")
                pe.wait_ge(od_sq, T + 1)
                pe.wait_ge(o_copied, 24 + 8 * T)
                mm(psO[:, 0:512], C("mean128", P), N[:, 0:512]).then_inc(od_ss, 1)
                pe.wait_ge(od_ready, T + 1)
                project(f"eout{T}", lambda k: toks(AT, k, T), P)
                peer(0, T, NORM[f"even{T}"])

            def peer(l, T, norm):
                norm_sum(norm, T)
                pe.wait_ge(n_ready, norm + 1)
                for q in range(2):
                    turn([(psT[:, a * P:(a + 1) * P], toks(N, q * 4 + a, T)) for a in range(4)])
                project(f"pq{l}{T}", lambda k: toks(N, k, T), P)
                pe.wait_ge(out_taken, OUT0[f"pq{l}{T}"] + 16)
                for q in range(4):
                    n = (l * NT + T) * 4 + q
                    if n >= 2:
                        pe.wait_ge(key_taken, n - 1)
                    for a in range(4):
                        hp = q * 4 + a
                        m = mm(psS[:, n % 2, a * P:(a + 1) * P], query(l, T, hp),
                               wsm[:, 384 + (l * 2 + hp % 2) * P:384 + (l * 2 + hp % 2 + 1) * P])
                    m.then_inc(key_scores, 1)

            def peer_out(l, T):
                pe.wait_ge(row_used, (l * NT + T + 1) * 2 * SLOTS)
                for q in range(2):
                    turn([(psT[:, a * P:(a + 1) * P], acc[T][:, (q * 4 + a) * P:(q * 4 + a + 1) * P])
                          for a in range(4)])

            def odd(T):
                peer_out(0, T)
                norm = NORM[f"odd{T} mix"]
                norm_sum(norm, T)
                pe.wait_ge(n_ready, norm + 1)
                project(f"oin{T}", lambda k: toks(N, k, T), P)
                pe.wait_ge(out_taken, OUT0[f"oin{T}"] + 25)
                for q in range(2):
                    turn([(psT[:, a * P:(a + 1) * P], toks(Z, OV + q * 4 + a, T)) for a in range(4)])
                pe.wait_ge(f_ready, T + 1)
                pe.wait_ge(turn_taken, turns[0])
                attention(f"odd{T}")
                pe.wait_ge(o_copied, 40 + 8 * T)
                project(f"oout{T}", lambda k: toks(AT, k, T), P)
                peer(1, T, NORM[f"odd{T}"])

            even(0)
            even(1)
            odd(0)
            odd(1)
            peer_out(1, 0)
            peer_out(1, 1)
            norm_sum(NORM["final"])

        @block.vector
        def _(dve):
            steps = [0]

            def link(ins):
                steps[0] += 1
                ins.then_inc(dve_step, 1)
                dve.wait_ge(dve_step, steps[0])

            def stt(o, a, s, b, op0, op1):
                return dve.scalar_tensor_tensor(out=o, in0=a, scalar=s, in1=b, op0=op0, op1=op1)

            def ts(o, a, s1, s2, op0, op1=None):
                return dve.tensor_scalar(o, a, s1, s2, op0) if op1 is None else dve.tensor_scalar(o, a, s1, s2, op0, op1)

            def tt(o, a, b, op):
                return dve.tensor_tensor(o, a, b, op)

            def unit_out(name, j, i, take):
                dve.wait_ge(vec_in, 16)
                dve.wait_ge(unit_done, UNIT0[name] + i * 8 + j + 1)
                take(psL[:, j % 4, 0:S], j, i).then_inc(out_taken, 1)

            def project_copy(name, n, dst):
                rounds(dve, n, lambda j, i: unit_out(
                    name, j, i, lambda p, j, i: dve.tensor_copy(dst[:, bass.ds(i * 8 * S + j * S, S)], p)))

            beside = {"l": None}

            def rows(n):
                l, T = beside["l"], beside.get("T")
                if l is None:
                    return
                done = beside["done"]
                n = min(n, 2 * ROUNDS - done)
                if done < ROUNDS < done + n:
                    rows(ROUNDS - done)
                    rows(done + n - ROUNDS)
                    return
                if n <= 0:
                    return
                if done == ROUNDS:
                    dve.wait_ge(act_ready, l * NT + T + 1)
                    g_ = gate[:, T * SLOTS:(T + 1) * SLOTS]
                    tt(g_, g_, dots[:, T * SLOTS:(T + 1) * SLOTS], ALU.mult)
                    link(dve.memset(acc[T], 0.0))
                beside["done"] += n
                base = (l * NT + T) * 2 * ROUNDS
                of_v = done >= ROUNDS
                first = T * SLOTS + (-SLOTS if of_v else 0)

                def one_round(i):
                    for s in range(GRING):
                        r = W[:, s * D:(s + 1) * D]
                        dve.wait_ge(row_landed[s], (i + base + 1) * 16)
                        col = i * GRING + first + s
                        if not of_v:
                            dve.scalar_tensor_tensor(out=r, in0=r, scalar=1.0, in1=h_t[T], op0=ALU.mult, op1=ALU.mult,
                                                     accum_out=dots[:, bass.ds(col, 1)]).then_inc(row_used, 1)
                        else:
                            dve.scalar_tensor_tensor(out=acc[T], in0=r, scalar=gate[:, bass.ds(col, 1)],
                                                     in1=acc[T], op0=ALU.mult, op1=ALU.add).then_inc(row_used, 1)
                            dve.wait_ge(row_used, (i + base) * GRING + s + 1)

                if n == 1:
                    one_round(done)
                else:
                    with dve.Fori(done, done + n) as i:
                        one_round(i)

            def gather(l, T):
                beside.update(l=l, T=T, done=0)

            def residual(name, gcol=None, T=None):
                for o in range(8):
                    if o % 4 == 0:
                        rows(1)
                    dve.wait_ge(unit_done, UNIT0[name] + o + 1)
                    p = psL[:, o % 4, 0:S if T is None else P]
                    x = chunk(X, o) if T is None else toks(X, o, T)
                    if gcol is None:
                        tt(x, p, x, ALU.add).then_inc(out_taken, 1)
                    else:
                        stt(x, p, mod[:, gcol + o:gcol + o + 1], x, ALU.mult, ALU.add).then_inc(out_taken, 1)
                dve.wait_ge(out_taken, OUT0[name] + 8)

            def norm(n, wcol, shift=None, dst=None, T=None):
                dst = N if dst is None else dst
                w = S if T is None else P

                def part(t, k):
                    return chunk(t, k) if T is None else toks(t, k, T)

                dve.wait_ge(ss_ready, n + 1)
                link(ts(var[:, 0:w], psO[:, 0:w], EPS, None, ALU.add))
                dve.reciprocal(var[:, 0:w], var[:, 0:w]).then_inc(rv_ready, 1)
                dve.wait_ge(rstd_ready, n + 1)
                for k in range(KC):
                    m = stt(part(dst, k), part(X, k), wcol(k), rstd[:, 0:w], ALU.mult, ALU.mult)
                if shift is not None:
                    link(m)
                    for k in range(KC):
                        m = ts(part(dst, k), part(dst, k), mod[:, shift + k:shift + k + 1], None, ALU.add)
                m.then_inc(n_ready, 1)

            def attention(kind):
                js = JOBS[kind]

                def front(jb):
                    n, T, b = jb["n"], jb["T"], jb["n"] % 2
                    w = keys_of(T)
                    dve.wait_ge(scores_ready, n + 1)
                    if n >= 2:
                        dve.wait_ge(exp_done, n - 1)
                    for m in range(2):
                        ins = stt(Sb[:, b, m * S:m * S + w], (psL if m else psS)[:, b, 0:w], 0.125, jb["bias"][m],
                                  ALU.mult, ALU.add)
                    link(ins)
                    if jb["kind"] == "dsa":
                        for m in range(2):
                            s = Sb[:, b, m * S:m * S + w]
                            ins = tt(s, s, sel[T][:, 0:w], ALU.add)
                        link(ins)
                    link(dve.tensor_reduce(mx[:, b, 0:2], Sb[:, b, :].rearrange("p (m w) -> p m w", m=2)[:, :, 0:w],
                                           AX.X, ALU.max))
                    ts(mx[:, b, 2:4], mx[:, b, 0:2], -1.0, None, ALU.mult).then_inc(smax_ready, 1)

                def scale(jb):
                    n, T, b = jb["n"], jb["T"], jb["n"] % 2
                    w = keys_of(T)
                    dve.wait_ge(exp_done, n + 1)
                    link(dve.reciprocal(facs[:, b, 0:2], sums[:, b, 0:2]))
                    for m in range(2):
                        if jb["fac"][m] is not None:
                            ins = tt(facs[:, b, m:m + 1], facs[:, b, m:m + 1], jb["fac"][m], ALU.mult)
                    if any(f is not None for f in jb["fac"]):
                        link(ins)
                    for m in range(2):
                        p_ = Pb[:, b, m * S:m * S + w]
                        ins = ts(p_, p_, facs[:, b, m:m + 1], None, ALU.mult)
                    ins.then_inc(p_ready, 1)

                def take(jb):
                    n, T = jb["n"], jb["T"]
                    dve.wait_ge(o_ready, n + 1)
                    for slot, rows, unit in jb["outs"]:
                        ins = dve.tensor_copy(toks(AT, unit, T, rows), psO[rows, slot * P:(slot + 1) * P])
                    ins.then_inc(o_copied, 1)

                front(js[0])
                for a, jb in enumerate(js):
                    if a + 1 < len(js):
                        front(js[a + 1])
                    scale(jb)
                    if a:
                        take(js[a - 1])
                    rows(1)
                take(js[-1])

            turns = [0]

            def turn_take(o, src):
                dve.wait_ge(turned, turns[0] + 1)
                turns[0] += 1
                dve.tensor_copy(o, src).then_inc(turn_taken, 1)

            dve.wait_ge(relrow_ready, 1)
            dve.tensor_copy(relrow[:], psO[0:12, 0:384]).then_inc(relrow_copied, 1)
            for n in range(9):
                dve.wait_ge(flipped, n + 1)
                T = n // 3 > 0
                w = keys_of(T)
                dst = bias1[:, (n - 3) * 512:(n - 2) * 512] if T else bias0[:, n * 512:(n + 1) * 512]
                tt(dst.rearrange("p (h w) -> p h w", w=w), psS[:, n % 2, :].rearrange("p (h w) -> p h w", w=w),
                   causal(T)[:, None, :].to_broadcast([P, 512 // w, w]), ALU.add).then_inc(bias_ready, 1)

            def ada_unit(slot, o, used):
                dve.wait_ge(ada_landed[slot], used)
                dve.scalar_tensor_tensor(out=aring[:, slot, :], in0=aring[:, slot, :], scalar=1.0, in1=crow[:],
                                         op0=ALU.mult, op1=ALU.mult, accum_out=mod[:, bass.ds(o, 1)]
                                         ).then_inc(ada_used, 1)

            norm(0, lambda k: V("norm1", k))
            dve.wait_ge(csil_ready, 1)

            def in_and_ada(j, i):
                unit_out("in", j, i, lambda p, j, i: dve.tensor_copy(Z[:, bass.ds(i * 8 * S + j * S, S)], p))
                ada_unit(j % ARING, i * 8 + j, (i * 2 + j // ARING + 1) * 16)

            rounds(dve, 45, in_and_ada)
            for o in range(45, 48):
                ada_unit(o % ARING, o, (o // ARING + 1) * 16)
            dve.wait_ge(out_taken, OUT0["in"] + 45)
            turn_take(VT[:, 0:512], psT[:])
            for kv, (u, pos) in enumerate(((ZKC, "pos_k"), (ZVC, "pos_v"))):
                for odd in range(2):
                    r = slice(64 * odd, 64 * odd + 64)
                    z = Z[r, u * S:(u + 2) * S].rearrange("p (g n a) -> p a g n", g=2, a=16)
                    f = W[r, kv * 512:kv * 512 + 480].rearrange("p (i g n) -> p i g n", i=16, g=2)
                    for late in range(2):
                        src = z[:, odd::2, :, late:late + NCMP]
                        b = vec[r, VEC[pos] + late * 8:VEC[pos] + late * 8 + 8]
                        for g in range(2):
                            m = tt(f[:, late * 8:late * 8 + 8, g, :], src[:, :, g, :],
                                   b[:, :, None].to_broadcast([64, 8, NCMP]), ALU.add)
                        m.then_inc(flat_ready, 1)
            dve.wait_ge(turned, 2)
            turns[0] += 1
            dve.tensor_copy(G[:], psT[:, 0:2 * P].rearrange("p (t c) -> p t c", t=2)[:, :, 0:24]).then_inc(turn_taken, 1)
            dve.wait_ge(kv2_ready, 1)
            dve.tensor_copy(kcT[0:64, 0:NCMP], psO[0:64, 0:NCMP]).then_inc(kv2_taken, 1)
            dve.tensor_copy(kcT[64:128, 0:NCMP], psO[64:128, NCMP:2 * NCMP]).then_inc(kv2_taken, 1)
            dve.tensor_copy(VTc[0:NCMP, 0:P], psO[0:NCMP, 64:192]).then_inc(kv2_taken, 1)
            dve.wait_ge(cs_ready, 1)
            cp3 = cprob.rearrange("p (c n) -> p c n", n=16)[:, :, 0:NCMP]
            po3 = [t[:, 0:128].rearrange("p (c n) -> p c n", n=16)[:, :, 0:NCMP] for t in (psO, psT)]

            def c_t(name, T, n=8):
                a = CON[name] + T * 16
                return con[:, a:a + NCMP][:, None, :].to_broadcast([P, n, NCMP])

            for T in range(NT):
                for b in range(2):
                    m = stt(cp3[:, T * 8 + 4 * b:T * 8 + 4 * b + 4, :], po3[b][:, T * 4:T * 4 + 4, :], 0.125,
                            c_t("cbias", T, 4), ALU.mult, ALU.add)
            link(m)
            link(dve.tensor_reduce(tiny[:, 0:16], cp3, AX.X, ALU.max))
            tt(cp3, cp3, tiny[:, 0:16][:, :, None].to_broadcast([P, 16, NCMP]), ALU.subtract).then_inc(csub_ready, 1)
            dve.wait_ge(cexp_ready, 1)
            for T in range(NT):
                m = tt(cp3[:, T * 8:T * 8 + 8, :], cp3[:, T * 8:T * 8 + 8, :], c_t("cmask", T), ALU.mult)
            link(m)
            link(dve.tensor_reduce(tiny[:, 16:32], cp3, AX.X, ALU.add))
            link(ts(tiny[:, 16:32], tiny[:, 16:32], 1e-20, None, ALU.max))
            link(dve.reciprocal(tiny[:, 16:32], tiny[:, 16:32]))
            dve.wait_ge(turn_taken, 2)
            for T in range(NT):
                g = G[:, T, :].rearrange("p (h b) -> p h b", b=3)[:, :, 0]
                m = tt(tiny[:, 16 + 8 * T:24 + 8 * T], tiny[:, 16 + 8 * T:24 + 8 * T], g, ALU.mult)
            link(m)
            tt(cp3, cp3, tiny[:, 16:32][:, :, None].to_broadcast([P, 16, NCMP]), ALU.mult).then_inc(cp_ready, 1)
            dve.wait_ge(cpt_ready, 1)
            for q in range(2):
                dve.tensor_copy(W[0:NCMP, 6144 + q * 1024:6144 + (q + 1) * 1024].rearrange("p (b n) -> p b n", b=2),
                                psL[0:NCMP, 2 * q:2 * q + 2, :]).then_inc(kv2_taken, 1)
            attention("nsa")
            for k in range(KC):
                m = ts(chunk(Wt[0], k), zu(ZXR + k), V("conv_w", 3 * 8 + k), V("conv_b", k), ALU.mult, ALU.add)
            link(m)
            for i in range(3):
                sh = 3 - i
                for k in range(KC):
                    o = chunk(Wt[0], k)[:, sh:S]
                    m = stt(o, zu(ZXR + k)[:, 0:S - sh], V("conv_w", i * 8 + k), o, ALU.mult, ALU.add)
                if i < 2:
                    link(m)
            m.then_inc(xc_ready, 1)
            dve.wait_ge(xc_ready, 1)
            dve.wait_ge(out_taken, OUT0["lru"] + 16)
            tt(Wt[0][:], Wt[0][:], Wt[2][:], ALU.mult).then_inc(lru_dve, 1)
            dve.wait_ge(lru_act, 1)
            link(ts(tiny[:, 32:40], V("lam", 0, 8), -1.0, 0.0, ALU.mult, ALU.max))
            link(tt(tiny[:, 32:40], tiny[:, 32:40], tiny[:, 40:48], ALU.add))
            ts(tiny[:, 40:48], tiny[:, 32:40], 8.0, None, ALU.mult)
            ts(tiny[:, 48:56], tiny[:, 32:40], -8.0, None, ALU.mult).then_inc(lru_dve, 1)
            dve.wait_ge(lru_act, 2)
            link(tt(Wt[1][:], Wt[3][:], Wt[3][:], ALU.mult))
            stt(Wt[2][:], Wt[1][:], 1.0, Wt[2][:], ALU.add, ALU.mult).then_inc(lru_dve, 1)
            dve.wait_ge(lru_act, 3)
            link(tt(Wt[2][:], Wt[2][:], Wt[0][:], ALU.mult))
            for k in range(KC):
                c = slice(k * S, (k + 1) * S)
                m = dve.tensor_tensor_scan(Wt[1][:, c], Wt[3][:, c], Wt[2][:, c], 0.0, ALU.mult, ALU.add)
            link(m)
            dve.wait_ge(lru_act, 4)
            tt(Wt[1][:], Wt[1][:], zu(ZGR, 8), ALU.mult).then_inc(lru_dve, 1)
            dve.wait_ge(sig_ready, 1)
            for o in range(8):
                if o % 2:
                    dve.wait_ge(unit_done, UNIT0["upattn"] + o // 2 + 1)
                else:
                    dve.wait_ge(pair_ready, o // 2 + 1)
                tt(chunk(N, o), psL[:, o % 4, 0:S], zu(ZGA + o), ALU.mult).then_inc(out_taken, 1)
            for o in range(8):
                dve.wait_ge(unit_done, UNIT0["uprnn"] + o + 1)
                link(tt(zu(ZGB + o), psL[:, o % 4, 0:S], zu(ZGB + o), ALU.mult))
                tt(chunk(N, o), chunk(N, o), zu(ZGB + o), ALU.add).then_inc(out_taken, 1)
            residual("out")
            norm(1, lambda k: V("norm2", k))
            def square_and_ada(j, i):
                dve.wait_ge(vec_in, 16)
                dve.wait_ge(out_taken, OUT0["mlp1"] + i * 8 + j + 1)
                z = Z[:, bass.ds(i * 8 * S + j * S, S)]
                tt(z, z, z, ALU.mult).then_inc(hsq_ready, 1)
                for a in range(j * 3 // 2, (j + 1) * 3 // 2):
                    ada_unit(a % ARING, i * 12 + 48 + a, (i * 3 + 12 + a // ARING + 1) * 16)

            rounds(dve, 32, square_and_ada)
            for o in range(8):
                dve.wait_ge(unit_done, UNIT0["mlp2"] + 4 * o + 4)
                tt(chunk(X, o), psL[:, o % 2, 0:S], chunk(X, o), ALU.add).then_inc(out_taken, 1)
            dve.wait_ge(out_taken, OUT0["mlp2"] + 8)
            norm(2, lambda k: V("final1", k), dst=X)
            dve.wait_ge(n_ready, 3)
            dve.wait_ge(ada_used, 96)
            link(tt(mod[:], mod[:], V("ada_b", 0, 96), ALU.add))
            for l in range(2):
                for a, wname in enumerate(("mix", "ffn")):
                    o = (2 * l + a) * KC
                    m = stt(amul[:, o:o + KC], mod[:, l * 48 + a * 24 + 8:l * 48 + a * 24 + 16], 1.0,
                            V(wname, l * 8, l * 8 + 8), ALU.add, ALU.mult)
            link(m)

            norm(3, lambda k: amul[:, k:k + 1], shift=0)
            tt(tiny[0:64, 0:2], vec[0:64, VEC["blam"]:VEC["blam"] + 4:2], vec[0:64, VEC["blam"] + 1:VEC["blam"] + 4:2],
               ALU.mult).then_inc(lam_in, 1)
            project_copy("ein", 24, Z)
            dve.wait_ge(turned, turns[0] + 1)
            turns[0] += 1
            ts(wi[:], psT[:, 0:2 * P].rearrange("p (t c) -> p t c", t=2)[:, :, 0:8], 8.0 ** -0.5, None, ALU.mult
               ).then_inc(turn_taken, 1)
            dve.wait_ge(lam_exp, 1)
            link(tt(tiny[:, 59:60], tiny[:, 57:58], tiny[:, 56:57], ALU.subtract))
            link(ts(tiny[:, 60:61], tiny[:, 59:60], -LAM_INIT, None, ALU.add))
            dve.wait_ge(ckv_ss, 1)
            link(ts(var[:, 0:S], psO[:, 0:S], 4.0, EPS, ALU.mult, ALU.add))
            dve.reciprocal(var[:, 0:S], var[:, 0:S]).then_inc(rv_ready, 1)
            dve.wait_ge(ckv_ready, 1)
            for k in range(2):
                m = stt(zu(ECKV + k), zu(ECKV + k), V("kvn", k), rstd[:, 0:S], ALU.mult, ALU.mult)
            m.then_inc(ckv_ready, 1)
            dve.wait_ge(turn_taken, turns[0])
            for T in range(NT):
                w = keys_of(T)
                for h in range(8):
                    n = T * 8 + h
                    dve.wait_ge(li_relu, n + 1)
                    src = work[:, n % 2, 0:w]
                    if h == 0:
                        m = ts(sel[T][:, 0:w], src, wi[:, T, h:h + 1], None, ALU.mult)
                    else:
                        m = stt(sel[T][:, 0:w], src, wi[:, T, h:h + 1], sel[T][:, 0:w], ALU.mult, ALU.add)
                    m.then_inc(li_added, 1)
                    dve.wait_ge(li_added, n + 1)
                link(tt(sel[T][:, 0:w], sel[T][:, 0:w], causal(T), ALU.add))
            for kt in range(NT):
                turn_take(VT[:, 1024 + kt * 512:1024 + (kt + 1) * 512], psT[:])
            for o in range(4):
                if o < 3:
                    dve.wait_ge(h_ready, 14 + o + 1)
                else:
                    dve.wait_ge(unit_done, UNIT0["ukv"] + 1)
                dve.tensor_copy(zu(24 + o), psL[:, o, 0:S]).then_inc(out_taken, 1)
            for kt in range(NT):
                if kt == 0:
                    dve.wait_ge(h_ready, 18)
                else:
                    dve.wait_ge(unit_done, UNIT0["ukv"] + 2)
                dve.tensor_copy(VT[:, kt * 512:(kt + 1) * 512], psL[:, kt, :]).then_inc(out_taken, 1)
            dve.wait_ge(bias_ready, 9)

            def even(T):
                s = sel[T][:, 0:keys_of(T)]
                for r in range(8):
                    link(dve.max(out=m8[:, T, :], in_=s))
                    link(dve.match_replace(out=s, in_to_replace=m8[:, T, :], in_values=s, imm_value=-3e38))
                link(ts(s, s, -2e38, NEG, ALU.is_gt, ALU.mult))
                attention(f"even{T}")
                dve.wait_ge(od_ss, T + 1)
                link(ts(var[:, 0:512], psO[:, 0:512], EPS, None, ALU.add))
                dve.reciprocal(rstd[:, 0:512], var[:, 0:512]).then_inc(od_rv, 1)
                dve.wait_ge(od_rstd, T + 1)
                o = tile_of(AT, 4, 4, T)
                link(stt(o, o, V("subln"), rstd[:, 0:512].rearrange("p (c s) -> p c s", c=4), ALU.mult, ALU.mult))
                ts(o, o, 1.0 - LAM_INIT, None, ALU.mult).then_inc(od_ready, 1)
                residual(f"eout{T}", 16, T)
                peer(0, T, NORM[f"even{T}"], 5)

            def peer(l, T, n, rounds_):
                rows(1)
                norm(n, lambda k: amul[:, (2 * l + 1) * KC + k:(2 * l + 1) * KC + k + 1], shift=l * 48 + 24, T=T)
                rows(rounds_)
                turns[0] += 2
                sc8, small7 = scratch(l, T)
                sc = sc8.rearrange("p (q n) -> p q n", q=16)
                val = small7[0].rearrange("p (q n) -> p q n", q=16)
                vix = small7[1].bitcast(U32).rearrange("p (q n) -> p q n", q=16)
                ixf = small7[2].rearrange("p (q n) -> p q n", q=16)
                best = small7[3][:, 0:P].rearrange("p (q n) -> p q n", q=8)
                bix = small7[3][:, P:S].bitcast(U32)
                ab = small7[4].bitcast(U32)
                abf = small7[5]
                sides = small7[6]
                cand = sc8.rearrange("p (h i j) -> p h i j", h=8, i=16)
                candh = sc8.rearrange("p (h n) -> p h n", h=8)

                def best16(src, v, ix, cnt):
                    for a in range(cnt):
                        m = dve.max(out=v[:, a, 0:8], in_=src[:, a, :])
                    link(m)
                    rows(1)
                    for a in range(cnt):
                        dve.max_index(out=ix[:, a, 0:8], in_max=v[:, a, 0:8], in_values=src[:, a, :])
                    for a in range(cnt):
                        m = dve.match_replace(out=src[:, a, :], in_to_replace=v[:, a, 0:8],
                                              in_values=src[:, a, :], imm_value=-3e38)
                    link(m)
                    rows(1)
                    for a in range(cnt):
                        m = dve.max(out=v[:, a, 8:16], in_=src[:, a, :])
                    link(m)
                    for a in range(cnt):
                        m = dve.max_index(out=ix[:, a, 8:16], in_max=v[:, a, 8:16], in_values=src[:, a, :])
                    link(m)

                dve.wait_ge(key_taken, (l * NT + T + 1) * 4)
                best16(sc, val, vix, 16)
                link(dve.tensor_copy(ixf, vix))
                v4 = val.rearrange("p (h s) n -> p h s n", s=2)
                link(tt(cand, v4[:, :, 0, :][:, :, :, None].to_broadcast([P, 8, 16, 16]),
                        v4[:, :, 1, :][:, :, None, :].to_broadcast([P, 8, 16, 16]), ALU.add))
                bx = bix.rearrange("p (q n) -> p q n", q=8)
                best16(candh, best, bx, 8)
                dve.tensor_scalar(ab[:, 0:P], bix, 4, None, ALU.logical_shift_right)
                link(dve.tensor_scalar(ab[:, P:2 * P], bix, 15, None, ALU.bitwise_and))
                link(dve.tensor_copy(abf, ab))
                f4 = ixf.rearrange("p (h s) n -> p h s n", s=2)
                for side in range(2):
                    pick = abf[:, side * P:(side + 1) * P].rearrange("p (h k) -> p h k", h=8)
                    it = con[:, CON["iota"]:CON["iota"] + 16]
                    link(tt(cand, pick[:, :, :, None].to_broadcast([P, 8, 16, 16]),
                            it[:, None, None, :].to_broadcast([P, 8, 16, 16]), ALU.is_equal))
                    link(tt(cand, cand, f4[:, :, side, :][:, :, None, :].to_broadcast([P, 8, 16, 16]), ALU.mult))
                    rows(1)
                    link(dve.tensor_reduce(
                        sides[:, side * P:(side + 1) * P].rearrange("p (h k) -> p h k", h=8),
                        cand, AX.X, ALU.add))
                link(stt(abf[:, 0:P], sides[:, 0:P], float(NKEYS), sides[:, P:2 * P], ALU.mult, ALU.add))
                ts(idx[:, T * SLOTS:(T + 1) * SLOTS], abf[:, 0:P], float(l * NEXP), None, ALU.add
                   ).then_inc(idx_ready, 1)
                gt = gate[:, T * SLOTS:(T + 1) * SLOTS].rearrange("p (h k) -> p h k", h=8)
                tt(gt, best, best[:, :, 0:1].to_broadcast([P, 8, 16]), ALU.subtract).then_inc(best_in, 1)
                dve.wait_ge(gexp, l * NT + T + 1)
                link(dve.tensor_reduce(tiny[:, 0:8], gt, AX.X, ALU.add))
                link(dve.reciprocal(tiny[:, 0:8], tiny[:, 0:8]))
                link(tt(gt, gt, tiny[:, 0:8][:, :, None].to_broadcast([P, 8, 16]), ALU.mult))
                rows(2 * ROUNDS)
                gather(l, T)

            def peer_out(l, T):
                gcol = l * 48 + 40
                for q in range(2):
                    dve.wait_ge(turned, turns[0] + 1)
                    turns[0] += 1
                    for a in range(4):
                        k = q * 4 + a
                        m = stt(toks(X, k, T), psT[:, a * P:(a + 1) * P], mod[:, gcol + k:gcol + k + 1],
                                toks(X, k, T), ALU.mult, ALU.add)
                    m.then_inc(turn_taken, 1)
                dve.wait_ge(turn_taken, turns[0])
                assert turns[0] == TURNS_PEER[l, T]

            def odd(T):
                peer_out(0, T)
                rows(1)
                norm(NORM[f"odd{T} mix"], lambda k: amul[:, 2 * KC + k:2 * KC + k + 1], shift=48, T=T)
                rows(7)
                turns[0] += 2
                dve.wait_ge(out_taken, OUT0[f"oin{T}"] + 25)
                f, row = toks(Z, OF, T), lrow[:, 0:P]
                link(ts(f, f, V("bf"), None, ALU.add))
                dve.tensor_copy(row, f).then_inc(f_act, 1)
                link(ts(f, f, 0.0, None, ALU.min))
                dve.wait_ge(f_act, 3 * T + 3)
                link(tt(f, f, row, ALU.subtract))
                if T:
                    link(tt(f[:, 0:1], f[:, 0:1], tiny[:, 61:62], ALU.add))
                link(dve.memset(row, 1.0))
                link(dve.tensor_tensor_scan(var[:, 0:P], row, f, 0.0, ALU.mult, ALU.add))
                dve.tensor_copy(tiny[:, 61:62], var[:, P - 1:P])
                link(ts(f, var[:, 0:P], 8.0, None, ALU.mult))
                for q in (0, 64):
                    dve.tensor_copy(row[q:q + 32, :], f[q:q + 32, :])
                    m = dve.memset(row[q + 32:q + 64, :], -1.0)
                link(m)
                for q in (0, 64):
                    m = dve.memset(f[q:q + 32, :], 1.0)
                link(m)
                for h in range(16):
                    m = ts(FK[:, h * S + T * P:h * S + (T + 1) * P], f, C("ind", 1, P, h), None, ALU.mult)
                m.then_inc(f_ready, 1)
                attention(f"odd{T}")
                residual(f"oout{T}", 48 + 16, T)
                peer(1, T, NORM[f"odd{T}"], 4)

            even(0)
            even(1)
            odd(0)
            odd(1)
            peer_out(1, 0)
            rows(2 * ROUNDS)
            peer_out(1, 1)
            norm(NORM["final"], lambda k: V("final2", k))

        @block.scalar
        def _(act):
            steps = [0]

            def link(ins):
                steps[0] += 1
                ins.then_inc(act_step, 1)
                act.wait_ge(act_step, steps[0])

            def f(o, i, fn, **k):
                return act.activation(o, i, fn, **k)

            def norm(n, done, count, T=None):
                w = S if T is None else P
                act.wait_ge(done, count)
                if T is None:
                    f(N[:], X[:], ACT.Square).then_inc(sq_ready, 1)
                else:
                    f(tile_of(N, 0, KC, T), tile_of(X, 0, KC, T), ACT.Square).then_inc(sq_ready, 1)
                act.wait_ge(rv_ready, n + 1 + (n > 3))
                f(rstd[:, 0:w], var[:, 0:w], ACT.Sqrt).then_inc(rstd_ready, 1)

            def attention(kind):
                js = JOBS[kind]

                def exps(jb):
                    n, b = jb["n"], jb["n"] % 2
                    w = keys_of(jb["T"])
                    act.wait_ge(smax_ready, n + 1)
                    if n >= 2:
                        act.wait_ge(pt_ready, n - 1)
                    for m in range(2):
                        ins = f(Pb[:, b, m * S:m * S + w], Sb[:, b, m * S:m * S + w], ACT.Exp,
                                bias=mx[:, b, 2 + m:3 + m], accum_out=sums[:, b, m:m + 1])
                    ins.then_inc(exp_done, 1)

                def turned_maps(jb):
                    n, T = jb["n"], jb["T"]
                    act.wait_ge(pt_ready, n + 1)
                    if n >= 2:
                        act.wait_ge(o_ready, n - 1)
                    w = 2 * (T + 1) * P
                    f(PT[:, n % 2, 0:w], psT[:, 0:w], ACT.Copy).then_inc(pt_copied, 1)

                exps(js[0])
                for a, jb in enumerate(js):
                    if a + 1 < len(js):
                        exps(js[a + 1])
                    turned_maps(jb)

            act.dma_start(X[:], x_dram).then_inc(x_in, 16)
            act.dma_start(crow[:], c_row.partition_broadcast(P)).then_inc(c_in, 16)
            act.dma_start(wsm[:], small).then_inc(small_in, 16)
            act.wait_ge(vec_in, 16)
            act.wait_ge(c_in, 16)
            f(crow[:], crow[:], ACT.Silu).then_inc(csil_ready, 1)
            norm(0, x_in, 16)
            act.wait_ge(out_taken, OUT0["in"] + 45)
            f(zu(ZG), zu(ZG), ACT.Sigmoid).then_inc(gates_ready, 1)
            for a in range(4):
                act.wait_ge(unit_done, UNIT0["cmp"] + 2 * a + 2)
                f(hid(a // 2, a % 2), psL[:, a, 0:30], ACT.Gelu_apprx_tanh).then_inc(out_taken, 1)
            act.wait_ge(csub_ready, 1)
            cp3 = cprob.rearrange("p (c n) -> p c n", n=16)[:, :, 0:NCMP]
            f(cp3, cp3, ACT.Exp).then_inc(cexp_ready, 1)
            attention("nsa")
            for a, (dst, bname) in enumerate(((Wt[1], "b_a"), (Wt[2], "b_i"))):
                for k in range(KC):
                    if k < KC - 1:
                        act.wait_ge(h_ready, a * 7 + k + 1)
                    else:
                        act.wait_ge(unit_done, UNIT0["lru"] + a + 1)
                    m = f(dst[:, k * S:(k + 1) * S], psL[:, (a * KC + k) % 4, 0:S], ACT.Sigmoid, bias=V(bname, k))
                    m.then_inc(out_taken, 1)
            act.wait_ge(out_taken, OUT0["lru"] + 16)
            f(zu(ZGA, 16), zu(ZGA, 16), ACT.Sigmoid).then_inc(sig_ready, 1)
            link(f(tiny[:, 40:48], V("lam", 0, 8), ACT.Abs))
            link(f(tiny[:, 40:48], tiny[:, 40:48], ACT.Exp, scale=-1.0))
            f(tiny[:, 40:48], tiny[:, 40:48], ACT.Ln, bias=1.0).then_inc(lru_act, 1)
            act.wait_ge(lru_dve, 2)
            for k in range(KC):
                c = slice(k * S, (k + 1) * S)
                f(Wt[3][:, c], Wt[1][:, c], ACT.Exp, scale=tiny[:, 48 + k:49 + k])
            for k in range(KC):
                c = slice(k * S, (k + 1) * S)
                m = f(Wt[2][:, c], Wt[1][:, c], ACT.Tanh, scale=tiny[:, 40 + k:41 + k])
            m.then_inc(lru_act, 1)
            act.wait_ge(lru_dve, 3)
            f(Wt[2][:], Wt[2][:], ACT.Sqrt).then_inc(lru_act, 1)
            f(zu(ZGR, 8), zu(ZGR, 8), ACT.Gelu_apprx_tanh).then_inc(lru_act, 1)
            norm(1, out_taken, OUT0["out"] + 8)
            rounds(act, 32, lambda j, i: (
                act.wait_ge(vec_in, 16), act.wait_ge(unit_done, UNIT0["mlp1"] + i * 8 + j + 1),
                f(Z[:, bass.ds(i * 8 * S + j * S, S)], psL[:, j % 4, 0:S], ACT.Relu).then_inc(out_taken, 1)))
            norm(2, out_taken, OUT0["mlp2"] + 8)
            norm(3, n_ready, 3)
            act.wait_ge(lam_sum, 1)
            f(tiny[:, 56:58], psO[:, 256:258], ACT.Exp).then_inc(lam_exp, 1)
            act.wait_ge(out_taken, OUT0["ein"] + 24)
            f(AT[:, 0:512], zu(ECKV, 2), ACT.Square).then_inc(ckv_sq, 1)
            act.wait_ge(rv_ready, 5)
            f(rstd[:, 0:S], var[:, 0:S], ACT.Sqrt).then_inc(ckv_ready, 1)
            for n in range(16):
                act.wait_ge(li_ready, n + 1)
                if n >= 2:
                    act.wait_ge(li_added, n - 1)
                w = keys_of(n // 8)
                f(work[:, n % 2, 0:w], psS[:, n % 2, 0:w], ACT.Relu, scale=0.125).then_inc(li_relu, 1)

            turns = [5]

            def turn_take(o, src):
                act.wait_ge(turned, turns[0] + 1)
                turns[0] += 1
                f(o, src, ACT.Copy).then_inc(turn_taken, 1)

            def project_copy(name, n, base, unit_w):
                rounds(act, n, lambda j, i: (
                    act.wait_ge(vec_in, 16), act.wait_ge(unit_done, UNIT0[name] + i * 8 + j + 1),
                    f(Z[:, bass.ds(i * 8 * unit_w + base + j * unit_w, P)], psL[:, j % 4, 0:P], ACT.Copy
                      ).then_inc(out_taken, 1)))

            def dots_gelu(l, T):
                act.wait_ge(row_used, ((l * NT + T) * 2 + 1) * SLOTS)
                d_ = dots[:, T * SLOTS:(T + 1) * SLOTS]
                f(d_, d_, ACT.Gelu_apprx_tanh).then_inc(act_ready, 1)

            def peer(l, T, n, name):
                norm(n, out_taken, OUT0[name] + 8, T)
                for q in range(2):
                    turn_take(h_t[T][:, q * 512:(q + 1) * 512], psT[:])
                if l == 0:
                    project_copy(f"pq{l}{T}", 16, 4 * S, P)
                else:
                    for i in range(2):
                        for j in range(8):
                            act.wait_ge(unit_done, UNIT0[f"pq{l}{T}"] + i * 8 + j + 1)
                            f(query(l, T, i * 8 + j), psL[:, j % 4, 0:P], ACT.Copy).then_inc(out_taken, 1)
                sc8, _ = scratch(l, T)
                g = l * NT + T
                if g:
                    act.wait_ge(idx_ready, g)
                for q in range(4):
                    act.wait_ge(key_scores, g * 4 + q + 1)
                    f(sc8[:, q * 512:(q + 1) * 512], psS[:, q % 2, :], ACT.Copy).then_inc(key_taken, 1)

            def best_exp(l, T):
                act.wait_ge(best_in, l * NT + T + 1)
                g_ = gate[:, T * SLOTS:(T + 1) * SLOTS]
                f(g_, g_, ACT.Exp).then_inc(gexp, 1)

            def even(T):
                attention(f"even{T}")
                act.wait_ge(o_copied, 24 + 8 * T)
                f(N[:, 0:512].rearrange("p (c s) -> p c s", c=4), tile_of(AT, 4, 4, T), ACT.Square).then_inc(od_sq, 1)
                act.wait_ge(od_rv, T + 1)
                f(rstd[:, 0:512], rstd[:, 0:512], ACT.Sqrt).then_inc(od_rstd, 1)
                peer(0, T, NORM[f"even{T}"], f"eout{T}")
                if T:
                    dots_gelu(0, 0)
                best_exp(0, T)

            def odd(T):
                turns[0] += 2
                norm(NORM[f"odd{T} mix"], turn_taken, TURNS_PEER[0, T], T)
                project_copy(f"oin{T}", 25, T * P, S)
                for q in range(2):
                    turn_take(VT[:, T * D + q * 512:T * D + (q + 1) * 512], psT[:])
                row = lrow[:, 0:P]
                act.wait_ge(f_act, 3 * T + 1)
                link(f(row, row, ACT.Abs))
                f(row, row, ACT.Exp, scale=-1.0).then_inc(f_act, 1)
                act.wait_ge(f_act, 3 * T + 2)
                f(row, row, ACT.Ln, bias=1.0).then_inc(f_act, 1)
                attention(f"odd{T}")
                dots_gelu(T, 1 - T)
                peer(1, T, NORM[f"odd{T}"], f"oout{T}")
                best_exp(1, T)

            even(0)
            even(1)
            odd(0)
            odd(1)
            dots_gelu(1, 1)
            norm(NORM["final"], turn_taken, TURNS_PEER[1, 1])


def kernel(**a):
    import numpy as np
    import concourse.bacc as bacc
    from concourse.bass_utils import run_bass_kernel_spmd

    a = {k: np.asarray(v) for k, v in a.items()}
    f = np.float32

    def units(w):
        n = w.shape[1] // P
        return w.reshape(KC, P, n, P).transpose(2, 1, 0, 3).reshape(n, P, KC * P)

    def cols(w, *parts):
        u = np.zeros((w.shape[0], P), f)
        for start, count, place in parts:
            u[:, place:place + count] = w[:, start:start + count]
        return u

    w = a["w_in"][0]
    pieces = [cols(w, (64 * j, 64, 0), (64 * (j + 4), 64, 64)) for j in range(4)]
    for start in (512, 640):
        pieces += [cols(w, (start + 64 * g, 64, 0), (start + 64 * g, 64, 64)) for g in range(2)]
    pieces += [w[:, 768:1280], cols(w, (1280, 24, 0)), w[:, 1304:5400]]
    stream = {"in": units(np.concatenate(pieces, 1))}
    stream["cmp"] = np.concatenate([
        units(a[n][0][1024 * u:1024 * (u + 1), P * m:P * (m + 1)])
        for n in ("cmp_k_w1", "cmp_v_w1") for m in range(2) for u in range(2)])
    lru = np.zeros((2, P, KC, P), f)
    for n, key in enumerate(("lru_w_a", "lru_w_i")):
        for h in range(16):
            r = slice(64 * (h % 2), 64 * (h % 2) + 64)
            lru[n, r, h // 2, r] = a[key][0, h]
    stream["lru"] = lru.reshape(2, P, KC * P)
    up = a["w_up_attn"][0].reshape(8, 64, D)[[0, 4, 1, 5, 2, 6, 3, 7]].reshape(4, P, 4, 2, P)
    stream["upattn"] = up.transpose(2, 1, 3, 0, 4).reshape(4, P, KC * P)
    stream["uprnn"] = units(a["w_up_rnn"][0])
    stream["out"] = units(a["w_out"][0])
    stream["mlp1"] = units(a["mlp_w1"][0])
    stream["mlp2"] = a["mlp_w2"][0].reshape(4, KC, P, 8, P).transpose(3, 0, 2, 1, 4).reshape(32, P, KC * P)
    w = a["even_w_in_2"][0]
    stream["ein"] = units(np.concatenate([w[:, 0:1280], cols(w, (1280, 64, 0), (1280, 64, 64)),
                                          cols(w, (1344, 8, 0)), w[:, 1352:2888]], 1))
    uk = a["a_w_uk_2"][0].reshape(2, P, 4, P).transpose(1, 2, 0, 3).reshape(P, KC * P)
    uv = a["a_w_uv_2"][0].reshape(2, P, 512).transpose(1, 0, 2).reshape(P, KC * P)
    stream["ukv"] = np.stack([uk, uv])
    stream["eout0"] = stream["eout1"] = units(a["even_w_out_2"][0])
    w = a["odd_w_in_2"][0]
    stream["oin0"] = stream["oin1"] = units(np.concatenate(
        [w[:, 0:3072], cols(w, *[(3072, 16, q) for q in (0, 32, 64, 96)])], 1))
    stream["oout0"] = stream["oout1"] = units(a["odd_w_out_2"][0])
    for l in range(2):
        stream[f"pq{l}0"] = stream[f"pq{l}1"] = units(a["peer_w_q_2"][l])
    weights = np.ascontiguousarray(np.concatenate([stream[n] for n, _, _ in STREAM]))

    w2k, w2v = a["cmp_k_w2"][0].reshape(2, P, 64), a["cmp_v_w2"][0].reshape(2, P, 64)
    small = np.ascontiguousarray(np.concatenate(
        [np.concatenate([w2k, w2k], 2).transpose(1, 0, 2).reshape(P, 256),
         w2v.transpose(1, 0, 2).reshape(P, 128),
         a["peer_sub_keys_2"].transpose(3, 0, 1, 2).reshape(P, 512)], 1))

    def fm(v):
        return v.reshape(-1, P).T

    def rows(v):
        return np.concatenate([v, np.zeros((P - v.shape[0], v.shape[1]), f)])

    bf = np.zeros((P, 1), f)
    for q in (0, 32, 64, 96):
        bf[q:q + 16, 0] = a["odd_b_forget_2"][0]
    vecs = {
        "norm1": fm(a["norm1_w"]), "norm2": fm(a["norm2_w"]), "final1": fm(a["final_norm_w"]),
        "conv_w": fm(a["conv_w"]), "conv_b": fm(a["conv_b"]), "b_a": fm(a["lru_b_a"]), "b_i": fm(a["lru_b_i"]),
        "lam": fm(a["lru_lambda"]), "c": fm(a["c_2"]), "ada_b": fm(a["ada_b_2"]), "mix": fm(a["norm_mix_2"]),
        "ffn": fm(a["norm_ffn_2"]), "final2": fm(a["norm_final_2"]), "kvn": fm(a["a_kv_norm_2"]),
        "subln": fm(a["b_subln_2"]), "bf": bf, "pos_k": fm(a["cmp_pos_k"]), "pos_v": fm(a["cmp_pos_v"]),
        "blam": rows(a["b_lambda_2"][0].T), "rel": rows(a["rel_bias_2"]),
    }
    vecs = np.ascontiguousarray(np.concatenate([vecs[n] for n in VEC], 1))

    q, k = np.arange(P)[:, None], np.arange(P)[None, :]
    t, n = np.arange(S), np.arange(16)
    seen = (n[None, :] < NCMP) & (16 * n[None, :] + 31 <= t[:, None])
    cmask = seen.reshape(NT, P, 16).transpose(1, 0, 2).reshape(P, 32).astype(f)
    dist = np.arange(S)
    big = 16 + (np.log(np.maximum(dist, 1).astype(f) / 16) / math.log(8) * 16).astype(np.int32)
    bucket = np.where(dist < 16, dist, np.minimum(big, 31))
    buckets = np.zeros((P, 384), f)
    buckets[bucket[::-1], np.arange(S)] = 1
    cons = {
        "ident": np.eye(P, dtype=f), "flip": np.ascontiguousarray(np.eye(P, dtype=f)[::-1]), "mean": np.full((P, P), 1 / D, f), "mean128": np.full((P, P), 1 / P, f),
        "ones": np.ones((P, P), f),
        "causal": np.concatenate([np.zeros((P, P), f), np.where(k <= q, 0, NEG).astype(f)], 1),
        "cmask": cmask, "cbias": np.where(cmask > 0, 0, NEG).astype(f),
        "iota": np.tile(np.arange(16, dtype=f), (P, 1)), "buckets": buckets,
        "ind": ((np.arange(P)[:, None] % 32) == n[None, :]).astype(f),
    }
    cons = np.ascontiguousarray(np.concatenate([cons[n] for n in CON], 1))

    ins = {
        "x_dram": np.ascontiguousarray(a["x"].reshape(S, KC, P).transpose(2, 1, 0).reshape(P, KC * S)),
        "c_row": a["c_2"].reshape(D),
        "ada": np.ascontiguousarray(a["ada_w_2"].transpose(0, 2, 1)).reshape(96, P, D), "weights": weights, "small": small, "vecs": vecs, "cons": cons,
        "experts_u": a["peer_u_2"].reshape(2 * NEXP, D), "experts_v": a["peer_v_2"].reshape(2 * NEXP, D),
    }
    nc = bacc.Bacc("TRN2", target_bir_lowering=False, num_devices=1)
    aps = {k: nc.dram_tensor(k, v.shape, F32, kind="ExternalInput").ap() for k, v in ins.items()}
    out = nc.dram_tensor("out", (P, KC * S), F32, kind="ExternalOutput").ap()
    build(nc, out=out, **aps)
    r = run_bass_kernel_spmd(nc, [ins], core_ids=[0])
    y = r.results[0]["out"]
    return y.reshape(P, KC, S).transpose(2, 1, 0).reshape(1, S, D)
```

```python
import math
from contextlib import ExitStack

import concourse.bass as bass
from concourse import mybir

F32 = mybir.dt.float32
U32 = mybir.dt.uint32
ACT = mybir.ActivationFunctionType
ALU = mybir.AluOpType
AX = mybir.AxisListType

P = 128
S = 256
NT = S // P
D = 1024
KC = D // P
WRING = 8
ARING = 4
GRING = 8
NEG = -1e30
EPS = 1e-6
NCMP = 15
NKEYS = 128
NEXP = NKEYS * NKEYS
TOPK = 16
PH = 8
SLOTS = PH * TOPK
LAM_INIT = 0.8 - 0.6 * math.exp(-0.3 * 0)

STREAM = [("in", 13, 13), ("in2a", 4, 4), ("cmp", 8, 4), ("in2b", 28, 28), ("lru", 2, 16), ("upattn", 4, 8),
          ("uprnn", 8, 8), ("out", 8, 8), ("mlp1", 32, 32), ("mlp2", 32, 8), ("ein", 12, 12),
          ("ein2", 12, 12), ("ukv", 2, 6), ("eout0", 8, 8), ("pq00a", 8, 8), ("pq00b", 8, 8), ("eout1", 8, 8), ("pq01a", 8, 8), ("pq01b", 8, 8),
          ("oin0", 25, 25), ("oout0", 8, 8), ("pq10a", 8, 8), ("pq10b", 8, 8), ("oin1", 25, 25), ("oout1", 8, 8),
          ("pq11a", 8, 8), ("pq11b", 8, 8)]
UNIT0, OUT0 = {}, {}
_u, _o = 0, 0
for _n, _a, _b in STREAM:
    UNIT0[_n], OUT0[_n] = _u, _o
    _u, _o = _u + _a, _o + _b
UNITS = _u
N_OUT = {n: b for n, _, b in STREAM}

ZQ, ZKC, ZVC, ZKS, ZVS, ZKW, ZVW, ZG, ZXR, ZGR, ZGA, ZGB = 0, 4, 6, 8, 9, 10, 11, 12, 13, 21, 29, 37
EQA, ECKV, EQI, EKI, EWI, EQB, EKB, EVB = 0, 4, 6, 10, 11, 12, 16, 20
OQ, OK, OV, OF = 0, 8, 16, 24

VEC = {}
_c = 0
for _n, _w in [("norm1", 8), ("norm2", 8), ("final1", 8), ("conv_w", 32), ("conv_b", 8), ("b_a", 8),
               ("b_i", 8), ("lam", 8), ("c", 8), ("ada_b", 96), ("mix", 16), ("ffn", 16), ("final2", 8),
               ("kvn", 2), ("subln", 1), ("bf", 1), ("pos_k", 16), ("pos_v", 16), ("blam", 4),
               ("rel", 12)]:
    VEC[_n] = _c
    _c += _w
NVEC = _c
CON = {}
_c = 0
for _n, _w in [("ident", 128), ("flip", 128), ("mean", 128), ("mean128", 128), ("ones", 128), ("causal", 256),
               ("cmask", 32), ("cbias", 32), ("iota", 16), ("buckets", 384), ("ind", 16)]:
    CON[_n] = _c
    _c += _w
NCON = _c


def build(nc, x_dram, c_row, ada, weights, small, vecs, cons, experts_u, experts_v, out):
    ctx = ExitStack()
    with ctx:
        def sb(name, shape, dt=F32):
            return ctx.enter_context(nc.sbuf_tensor(name, shape, dt))

        def ps(name, shape):
            return ctx.enter_context(nc.psum_tensor(name, shape, F32))

        def sem(name):
            return ctx.enter_context(nc.semaphore(name))

        wring = [sb(f"wring{i}", [P, KC * P]) for i in range(WRING)]
        X = sb("X", [P, KC * S])
        N = sb("N", [P, KC * S])
        Z = sb("Z", [P, 45 * S])
        W = sb("W", [P, GRING * D])
        AT = sb("AT", [P, KC * S])
        vec = sb("vec", [P, NVEC])
        con = sb("con", [P, NCON])
        wsm = sb("wsm", [P, 896])
        bias = sb("bias", [P, 12 * P + 12 * S])
        relrow = sb("relrow", [12, 384])
        mod = sb("mod", [P, 96])
        crow = sb("crow", [P, D])
        aring = sb("aring", [P, ARING, D])
        amul = sb("amul", [P, 4 * KC])
        rstd = sb("rstd", [P, 2 * S])
        var = sb("var", [P, 2 * S])
        Sb = sb("Sb", [P, 2, 512])
        Pb = sb("Pb", [P, 2, 512])
        PT = sb("PT", [P, 2, 512])
        mx = sb("mx", [P, 2, 8])
        sums = sb("sums", [P, 2, 8])
        facs = sb("facs", [P, 2, 8])
        VT = sb("VT", [P, 4 * 512])
        G = sb("G", [P, NT, 24])
        sel = [Z[:, u * S:(u + 1) * S] for u in (44, 28)]
        work = Z[:, 42 * S:44 * S].rearrange("p (t s) -> p t s", t=2)
        m8 = sb("m8", [P, NT, 8])
        wi = sb("wi", [P, NT, 8])
        tiny = sb("tiny", [P, 64])
        stage = sb("stage", [P, 4, 4], U32)
        lrow = crow[:, 0:S]
        idx = crow[:, S:S + NT * SLOTS].bitcast(U32)
        dots = crow[:, 2 * S:2 * S + NT * SLOTS]
        gate = crow[:, 3 * S:3 * S + NT * SLOTS]
        psL = ps("psL", [P, 4, 512])
        psS = ps("psS", [P, 2, 512])
        psT = ps("psT", [P, 512])
        psO = ps("psO", [P, 512])
        reld = nc.dram_tensor("rel_rows", [12, 384], F32, kind="Internal").ap()

        def V(name, a=0, b=None):
            b = a + 1 if b is None else b
            return vec[:, VEC[name] + a:VEC[name] + b]

        def C(name, w, parts=P, a=0):
            return con[0:parts, CON[name] + a:CON[name] + a + w]

        def zu(u, n=1, parts=slice(0, P)):
            return Z[parts, u * S:(u + n) * S]

        def chunk(t, k, n=1):
            return t[:, k * S:(k + n) * S]

        def toks(t, u, T, parts=slice(0, P), w=P):
            return t[parts, u * S + T * P:u * S + T * P + w]

        def hid(kv, m):
            a = 1024 + (kv * 2 + m) * 32
            return W[:, a:a + 30]

        bias0, bias1 = bias[:, 0:12 * P], bias[:, 12 * P:]
        FK = aring[:].rearrange("p a d -> p (a d)")
        h_t = [Z[:, (29 + 4 * T) * S:(33 + 4 * T) * S] for T in range(NT)]
        acc = [Z[:, (37 + 4 * T) * S:(41 + 4 * T) * S] for T in range(NT)]

        def query(l, T, hp):
            if l == 0:
                return Z[:, 4 * S + hp * P:4 * S + (hp + 1) * P]
            return toks(Z, (OQ if hp < 8 else OV) + hp % 8, T)

        def scratch(l, T):
            if l == 0 and T == 0:
                return Z[:, 33 * S:41 * S], [Z[:, u * S:(u + 1) * S] for u in (41, 42, 43, 20, 21, 22, 23)]
            return bias[:, 0:8 * S], [bias[:, u * S:(u + 1) * S] for u in range(8, 15)]

        def tile_of(t, u, n, T):
            return t[:, u * S:(u + n) * S].rearrange("p (c s) -> p c s", s=S)[:, :, T * P:(T + 1) * P]

        cprob, kcT, VTc = W[:, 1280:1536], W[:, 1536:1552], W[:, 1664:1792]
        Wt = [W[:, i * KC * S:(i + 1) * KC * S] for i in (1, 0, 2, 3)]
        ident = C("ident", P)

        x_in, vec_in, con_in, small_in = sem("x_in"), sem("vec_in"), sem("con_in"), sem("small_in")
        landed = [sem(f"unit_landed{i}") for i in range(WRING)]
        unit_done, out_taken = sem("unit_done"), sem("out_taken")
        relrow_ready, relrow_copied, rel_stored = sem("relrow_ready"), sem("relrow_copied"), sem("rel_stored")
        rel_loaded, flipped, bias_ready = sem("rel_loaded"), sem("flipped"), sem("bias_ready")
        c_in, csil_ready, ada_used = sem("c_in"), sem("csil_ready"), sem("ada_used")
        ada_landed = [sem(f"ada_landed{i}") for i in range(ARING)]
        sq_ready, ss_ready, rv_ready, rstd_ready, n_ready = (
            sem(n) for n in ("sq_ready", "ss_ready", "rv_ready", "rstd_ready", "n_ready"))
        dve_step, act_step = sem("dve_step"), sem("act_step")
        scores_ready, smax_ready, exp_done, p_ready = (
            sem(n) for n in ("scores_ready", "smax_ready", "exp_done", "p_ready"))
        pt_ready, pt_copied, o_ready, o_copied = (
            sem(n) for n in ("pt_ready", "pt_copied", "o_ready", "o_copied"))
        turned, turn_taken = sem("turned"), sem("turn_taken")
        gates_ready = sem("gates_ready")
        flat_ready, kv2_ready, kv2_taken = (sem(n) for n in ("flat_ready", "kv2_ready", "kv2_taken"))
        cs_ready, csub_ready, cexp_ready, cp_ready, cpt_ready = (
            sem(n) for n in ("cs_ready", "csub_ready", "cexp_ready", "cp_ready", "cpt_ready"))
        xc_ready, lru_act, lru_dve, h_ready = (sem(n) for n in ("xc_ready", "lru_act", "lru_dve", "h_ready"))
        final_chunk = sem("final_chunk")
        sig_ready, hsq_ready, pair_ready = sem("sig_ready"), sem("hsq_ready"), sem("pair_ready")
        ckv_sq, ckv_ss, ckv_ready = sem("ckv_sq"), sem("ckv_ss"), sem("ckv_ready")
        lam_in, lam_sum, lam_exp = sem("lam_in"), sem("lam_sum"), sem("lam_exp")
        li_ready, li_relu, li_added, sel_ready = (
            sem(n) for n in ("li_ready", "li_relu", "li_added", "sel_ready"))
        od_sq, od_ss, od_rv, od_rstd, od_ready = (
            sem(n) for n in ("od_sq", "od_ss", "od_rv", "od_rstd", "od_ready"))
        f_act, f_ready = sem("f_act"), sem("f_ready")
        key_scores, key_taken, best_in, gexp = (
            sem(n) for n in ("key_scores", "key_taken", "best_in", "gexp"))
        idx_ready, staged, gather_next = sem("idx_ready"), sem("staged"), sem("gather_next")
        row_landed = [sem(f"row_landed{j}") for j in range(GRING)]
        row_used, act_ready = sem("row_used"), sem("act_ready")
        stored = sem("stored")

        IN2_BEFORE = 12

        def in2_at(u):
            return ("in2a", u) if u < 4 else ("in2b", u - 4)

        def in2_beside(a):
            return range(IN2_BEFORE + min(a, 4) + a, IN2_BEFORE + min(a + 1, 4) + a + 1)

        def weights_at(eng, name, j, i=0):
            g = UNIT0[name] + j
            eng.wait_ge(landed[g % WRING], (i + g // WRING + 1) * 16)
            return wring[g % WRING]

        def rounds(eng, n, body, per=8, peel=False):
            full = n // per
            peel = peel and full > 1
            for j in range(per if peel else 0):
                body(j, 0)
            if full > 1:
                with eng.Fori(int(peel), full) as i:
                    for j in range(per):
                        body(j, i)
            else:
                full = 0
            for m in range(full * per, n):
                body(m % per, m // per)

        def hid_bank(a):
            return psL[:, a, :] if a < 2 else psS[:, a - 2, :]

        def keys_of(T):
            return P * (T + 1)

        def causal(T):
            return con[:, CON["causal"] + P * (1 - T):CON["causal"] + S]

        def relbias(h, T):
            return bias0[:, h * P:(h + 1) * P] if T == 0 else bias1[:, h * S:(h + 1) * S]

        jobs = []
        for T in range(NT):
            for h in range(8):
                j, b = h % 4, h // 4
                rows = slice(64 * b, 64 * b + 64)
                jobs.append(dict(kind="nsa", T=T, rows=[rows, rows], q=[ZQ + j] * 2, k=[ZKS, ZKW],
                                 bias=[causal(T)] * 2,
                                 fac=[G[:, T, 3 * h + 1:3 * h + 2], G[:, T, 3 * h + 2:3 * h + 3]],
                                 v=[lambda kt: VT[:, kt * P:(kt + 1) * P],
                                    lambda kt: VT[:, (2 + kt) * P:(3 + kt) * P]],
                                 slot=[0, 0], cmp=T * 8 + h, outs=[(0, rows, j)]))
        for T in range(NT):
            for j in range(4):
                jobs.append(dict(kind="dsa", T=T, rows=[slice(0, 64), slice(64, 128)],
                                 q=[EQA + j] * 2, k=[24 + j] * 2,
                                 bias=[relbias(2 * j, T), relbias(2 * j + 1, T)], fac=[None, None],
                                 v=[lambda kt, j=j: VT[:, kt * 512 + j * P:kt * 512 + (j + 1) * P]] * 2,
                                 slot=[0, 1], cmp=None,
                                 outs=[(0, slice(0, 64), j), (1, slice(64, 128), j)]))
            for h in range(4):
                jobs.append(dict(kind="diff", T=T, rows=[slice(0, 64), slice(64, 128)],
                                 q=[EQB + h] * 2, k=[EKB + h] * 2, bias=[relbias(8 + h, T)] * 2,
                                 fac=[None, tiny[:, 60:61]],
                                 v=[lambda kt, h=h: VT[:, 1024 + kt * 512 + h * P:1024 + kt * 512 + (h + 1) * P]] * 2,
                                 slot=[0, 0], cmp=None, outs=[(0, slice(0, P), 4 + h)]))
        for T in range(NT):
            for j in range(8):
                jobs.append(dict(kind="forget", T=T, rows=[slice(0, 64), slice(64, 128)],
                                 q=[OQ + j] * 2, k=[OK + j] * 2, bias=[causal(T)] * 2, fac=[None, None],
                                 v=[lambda kt, j=j: VT[:, kt * 1024 + j * P:kt * 1024 + (j + 1) * P]] * 2,
                                 slot=[0, 1], cmp=None, head=[2 * j, 2 * j + 1],
                                 outs=[(0, slice(0, 64), j), (1, slice(64, 128), j)]))
        for n, jb in enumerate(jobs):
            jb["n"] = n
        JOBS = {"nsa": jobs[0:16], "even0": jobs[16:24], "even1": jobs[24:32],
                "odd0": jobs[32:40], "odd1": jobs[40:48]}

        ROUNDS = SLOTS // GRING
        NORM = {"even0": 4, "even1": 5, "odd0 mix": 6, "odd0": 7, "odd1 mix": 8, "odd1": 9, "final": 10}
        TURNS_PEER = {(0, 0): 11, (0, 1): 17, (1, 0): 23, (1, 1): 25}

        block = ctx.enter_context(nc.Block())

        @block.sync
        def _(sp):
            sp.dma_start(vec[:], vecs).then_inc(vec_in, 16)
            sp.dma_start(con[:], cons).then_inc(con_in, 16)

            def unit(j, i):
                g = i * WRING + j
                if not isinstance(g, int) or g >= WRING:
                    sp.wait_ge(unit_done, g - WRING + 1)
                src = weights[g] if isinstance(g, int) else weights[bass.ds(g, 1)].rearrange("a p n -> (a p) n")
                sp.dma_start(wring[j][:], src).then_inc(landed[j], 16)

            for j in range(WRING):
                unit(j, 0)
            sp.wait_ge(relrow_copied, 1)
            sp.dma_start(reld, relrow[:]).then_inc(rel_stored, 16)
            sp.wait_ge(rel_stored, 16)
            for T in range(NT):
                w = keys_of(T)
                src = bass.AP(tensor=reld.tensor, offset=P - T * P, ap=[[1, P], [384, 12], [1, w]])
                dst = W[:, T * 12 * P:T * 12 * P + 12 * w]
                sp.dma_start(dst.rearrange("p (h w) -> p h w", h=12), src).then_inc(rel_loaded, 16)
            with sp.Fori(1, UNITS // WRING) as i:
                for j in range(WRING):
                    unit(j, i)
            for g in range(UNITS // WRING * WRING, UNITS):
                unit(g % WRING, g // WRING)
            sp.wait_ge(n_ready, NORM["final"] + 1)
            sp.dma_start(out, N[:]).then_inc(stored, 16)
            sp.wait_ge(stored, 16)

        @block.gpsimd
        def _(pool):
            def ada_load(j, i):
                if not isinstance(i, int):
                    pool.wait_ge(ada_used, i * ARING + j - ARING + 1)
                    src = ada[bass.ds(i * ARING + j, 1)].rearrange("a p n -> (a p) n")
                else:
                    src = ada[j]
                pool.dma_start(aring[:, j, :], src).then_inc(ada_landed[j], 16)

            for j in range(ARING):
                ada_load(j, 0)
            with pool.Fori(1, 96 // ARING) as i:
                for j in range(ARING):
                    ada_load(j, i)
            per, group = 2 * GRING, 4
            for l in range(2):
                for T in range(NT):
                    for n, table in enumerate((experts_u, experts_v)):
                        loop = (l * NT + T) * 2 + n
                        used0 = loop * SLOTS
                        rounds_ = SLOTS // per
                        pool.wait_ge(idx_ready, 2 * (l * NT + T) + 1)

                        def gathers(i, first):
                            for q in range(per // group):
                                if not first:
                                    pool.wait_ge(row_used, i * per + used0 + q * group + group - per)
                                pool.tensor_copy(stage[:, q, :],
                                                 idx[:, bass.ds(i * per + T * SLOTS + q * group, group)]
                                                 ).then_inc(staged, 1)
                                for j in range(group):
                                    c = q * group + j
                                    slot = c % GRING
                                    if j == 0:
                                        pool.wait_ge(staged, i * (per // group) + loop * rounds_ * (per // group) + q + 1)
                                    if not (first and c < GRING):
                                        pool.wait_ge(row_used, i * per + used0 + c - GRING + 1)
                                    pool.sem_inc(gather_next, 1)
                                    pool.indirect_dma_start(
                                        W[:, slot * D:(slot + 1) * D], None, table,
                                        bass.IndirectOffsetOnAxis(ap=stage[:, q, j:j + 1], axis=0)
                                    ).then_inc(row_landed[slot], 16)

                        if loop == 0:
                            gathers(0, True)
                        with pool.Fori(1 if loop == 0 else 0, rounds_ // 2) as i:
                            gathers(i, False)
                        pool.wait_ge(idx_ready, 2 * (l * NT + T) + 2)
                        with pool.Fori(rounds_ // 2, rounds_) as i:
                            gathers(i, False)

        @block.tensor
        def _(pe):
            def mm(o, l, r, first=True, last=True):
                return pe.matmul(o, l, r, start=first, stop=last)

            def project(name, rhs, cols=S):
                if OUT0[name]:
                    pe.wait_ge(out_taken, OUT0[name])

                def unit(j, i):
                    w = weights_at(pe, name, j, i)
                    if not (isinstance(i, int) and OUT0[name] + i * 8 + j < 4):
                        pe.wait_ge(out_taken, OUT0[name] + i * 8 + j - 3)
                    for k in range(KC):
                        m = mm(psL[:, j % 4, 0:cols], w[:, k * P:(k + 1) * P], rhs(k), k == 0, k == KC - 1)
                    m.then_inc(unit_done, 1)

                rounds(pe, N_OUT[name], unit, peel=OUT0[name] == 0)

            def in2_unit(u):
                name, at = in2_at(u)
                w = weights_at(pe, name, at)
                if u < 2:
                    pe.wait_ge(out_taken, OUT0["in2a"])
                else:
                    last, at = in2_at(u - 2)
                    pe.wait_ge(out_taken, OUT0[last] + at + 1)
                for k in range(KC):
                    m = mm(psL[:, 2 + u % 2, 0:S], w[:, k * P:(k + 1) * P], chunk(N, k), k == 0, k == KC - 1)
                m.then_inc(unit_done, 1)

            def norm_sum(n, T=None, sq=N):
                for k in range(KC):
                    pe.wait_ge(sq_ready, n * KC + k + 1)
                    m = mm(psO[:, 0:S if T is None else P], C("mean", P),
                           chunk(sq, k) if T is None else toks(sq, k, T), k == 0, k == KC - 1)
                m.then_inc(ss_ready, 1)

            def attention(kind):
                js = JOBS[kind]
                if kind in ("even1", "odd0", "odd1"):
                    pe.wait_ge(key_taken, {"even1": 4, "odd0": 8, "odd1": 12}[kind])

                def scores(jb):
                    n, T = jb["n"], jb["T"]
                    if n >= 2:
                        pe.wait_ge(smax_ready, n - 1)
                    w = keys_of(T)
                    for m in range(2):
                        r = jb["rows"][m]
                        o = (psL if m else psS)[:, n % 2, 0:w]
                        last = mm(o, toks(Z, jb["q"][m], T, r), toks(Z, jb["k"][m], 0, r, w),
                                  True, jb["kind"] != "forget")
                        if jb["kind"] == "forget":
                            h = jb["head"][m]
                            last = mm(o, lrow[r, 0:P], FK[r, h * S:h * S + w], False, True)
                    last.then_inc(scores_ready, 1)

                def turn_maps(jb):
                    n, T = jb["n"], jb["T"]
                    pe.wait_ge(p_ready, n + 1)
                    if n >= 1:
                        pe.wait_ge(pt_copied, n)
                    at = 0
                    for m in range(2):
                        for kt in range(T + 1):
                            last = pe.transpose(psT[:, at * P:(at + 1) * P],
                                                Pb[:, n % 2, m * S + kt * P:m * S + (kt + 1) * P], ident)
                            at += 1
                    last.then_inc(pt_ready, 1)

                def values(jb):
                    n, T = jb["n"], jb["T"]
                    pe.wait_ge(pt_copied, n + 1)
                    if n >= 1:
                        pe.wait_ge(o_copied, n)
                    for slot in sorted(set(jb["slot"])):
                        parts = [(m, kt) for m in range(2) if jb["slot"][m] == slot for kt in range(T + 1)]
                        o = psO[:, slot * P:(slot + 1) * P]
                        for a, (m, kt) in enumerate(parts):
                            at = m * (T + 1) + kt
                            last = mm(o, jb["v"][m](kt), PT[:, n % 2, at * P:(at + 1) * P], a == 0,
                                      a == len(parts) - 1 and jb["cmp"] is None)
                        if jb["cmp"] is not None:
                            c = jb["cmp"]
                            last = mm(o, VTc[0:NCMP, 0:P], W[0:NCMP, 6144 + c * P:6144 + (c + 1) * P],
                                      False, True)
                    last.then_inc(o_ready, 1)

                scores(js[0])
                scores(js[1])
                for a, jb in enumerate(js):
                    turn_maps(jb)
                    if a + 2 < len(js):
                        scores(js[a + 2])
                    if kind == "nsa":
                        for u in in2_beside(a):
                            in2_unit(u)
                    values(jb)

            turns = [0]

            def turn(pairs, tile=psT):
                if turns[0]:
                    pe.wait_ge(turn_taken, turns[0])
                for o, src in pairs:
                    last = pe.transpose(o, src, ident)
                last.then_inc(turned, 1)
                turns[0] += 1

            pe.wait_ge(vec_in, 16)
            pe.wait_ge(con_in, 16)
            mm(psO[0:12, 0:384], vec[0:32, VEC["rel"]:VEC["rel"] + 12], C("buckets", 384, 32)
               ).then_inc(relrow_ready, 1)
            pe.wait_ge(relrow_copied, 1)
            norm_sum(0)
            pe.wait_ge(n_ready, 1)
            project("in", lambda k: chunk(N, k))
            in2_unit(0)
            in2_unit(1)
            pe.wait_ge(rel_loaded, 32)
            for n in range(9):
                if n >= 2:
                    pe.wait_ge(bias_ready, n - 1)
                mm(psS[:, n % 2, :], C("flip", P), W[:, n * 512:(n + 1) * 512]).then_inc(flipped, 1)
            pe.wait_ge(out_taken, OUT0["in"] + 13)
            turn([(psT[:, (2 * a + kt) * P:(2 * a + kt + 1) * P], toks(Z, u, kt))
                  for a, u in enumerate((ZVS, ZVW)) for kt in range(NT)])
            pe.wait_ge(gates_ready, 1)
            turn([(psT[:, T * P:(T + 1) * P], toks(Z, ZG, T)) for T in range(NT)])
            in2_unit(2)
            in2_unit(3)
            pe.wait_ge(bias_ready, 9)
            pe.wait_ge(flat_ready, 8)
            for a in range(4):
                for u in range(2):
                    w = weights_at(pe, "cmp", 2 * a + u)
                    for k in range(KC):
                        i = 8 * u + k
                        r = W[:, (a // 2) * 512 + i * 30:(a // 2) * 512 + (i + 1) * 30]
                        m = mm(hid_bank(a)[:, 0:30], w[:, k * P:(k + 1) * P], r, i == 0, i == 15)
                    m.then_inc(unit_done, 1)
            in2_unit(4)
            in2_unit(5)
            pe.wait_ge(out_taken, OUT0["cmp"] + 4)
            pe.wait_ge(small_in, 16)
            for m_ in range(2):
                mm(psO[:, 0:30], wsm[:, m_ * P:(m_ + 1) * P], hid(0, m_), m_ == 0, m_ == 1)
            for g in range(2):
                for m_ in range(2):
                    m = mm(psO[0:NCMP, 64 + g * 64:128 + g * 64], hid(1, m_)[:, g * NCMP:(g + 1) * NCMP],
                           wsm[:, 256 + m_ * 64:256 + (m_ + 1) * 64], m_ == 0, m_ == 1)
            m.then_inc(kv2_ready, 1)
            in2_unit(6)
            in2_unit(7)
            pe.wait_ge(kv2_taken, 3)
            pe.wait_ge(turn_taken, 2)
            for T in range(NT):
                for h in range(8):
                    j, b = h % 4, h // 4
                    r = slice(64 * b, 64 * b + 64)
                    m = mm((psT if b else psO)[:, (T * 4 + j) * 16:(T * 4 + j) * 16 + NCMP], toks(Z, ZQ + j, T, r),
                           kcT[r, 0:NCMP])
            m.then_inc(cs_ready, 1)
            for u in range(8, 11):
                in2_unit(u)
            pe.wait_ge(cp_ready, 1)
            for c in range(16):
                m = pe.transpose(hid_bank(c // 4)[0:NCMP, (c % 4) * P:(c % 4 + 1) * P],
                                 cprob[:, c * 16:c * 16 + NCMP], ident)
            m.then_inc(cpt_ready, 1)
            in2_unit(11)
            pe.wait_ge(kv2_taken, 5)
            attention("nsa")
            pe.wait_ge(xc_ready, KC)
            for a in range(2):
                w = weights_at(pe, "lru", a)
                for k in range(KC):
                    o = a * KC + k
                    pe.wait_ge(out_taken, OUT0["lru"] + o - 3 if o >= 4 else OUT0["lru"])
                    m = mm(psL[:, o % 4, 0:S], w[:, k * P:(k + 1) * P], Wt[0][:, k * S:(k + 1) * S])
                    m.then_inc(h_ready if k < KC - 1 else unit_done, 1)
            pe.wait_ge(out_taken, OUT0["upattn"])
            pe.wait_ge(sig_ready, 1)
            pe.wait_ge(o_copied, 16)
            for u in range(4):
                w = weights_at(pe, "upattn", u)
                for b in range(2):
                    o = 2 * u + b
                    if o >= 4:
                        pe.wait_ge(out_taken, OUT0["upattn"] + o - 3)
                    for k in range(4):
                        m = mm(psL[:, o % 4, 0:S], w[:, (b * 4 + k) * P:(b * 4 + k + 1) * P], chunk(AT, k),
                               k == 0, k == 3)
                    if b == 0:
                        m.then_inc(pair_ready, 1)
                m.then_inc(unit_done, 1)
            pe.wait_ge(lru_dve, 4)
            project("uprnn", lambda k: Wt[1][:, k * S:(k + 1) * S])
            pe.wait_ge(out_taken, OUT0["uprnn"] + 8)
            project("out", lambda k: chunk(N, k))
            norm_sum(1, sq=Z)
            pe.wait_ge(n_ready, 2)
            project("mlp1", lambda k: chunk(N, k))
            pe.wait_ge(out_taken, OUT0["mlp2"])
            pe.wait_ge(hsq_ready, 32)

            def mlp2_unit(j, i):
                w = weights_at(pe, "mlp2", j, i)
                if j % 4 == 0:
                    pe.wait_ge(out_taken, OUT0["mlp2"] + i * 2 + j // 4 - 1)
                for k in range(KC):
                    m = mm(psL[:, j // 4, 0:S], w[:, k * P:(k + 1) * P], chunk(Z, (j % 4) * 8 + k),
                           j % 4 == 0 and k == 0, j % 4 == 3 and k == KC - 1)
                m.then_inc(unit_done, 1)

            rounds(pe, 32, mlp2_unit)
            norm_sum(2)
            norm_sum(3)
            pe.wait_ge(n_ready, 4)
            project("ein", lambda k: chunk(N, k))
            pe.wait_ge(out_taken, OUT0["ein"] + 12)
            turn([(psT[:, T * P:(T + 1) * P], toks(Z, EWI, T)) for T in range(NT)])
            pe.wait_ge(lam_in, 1)
            pe.wait_ge(rstd_ready, 4)
            mm(psO[:, 256:258], C("ones", P, 64), tiny[0:64, 0:2]).then_inc(lam_sum, 1)

            def ein2_unit(u):
                w = weights_at(pe, "ein2", u)
                pe.wait_ge(out_taken, OUT0["ein2"] + u - 3)
                for k in range(KC):
                    m = mm(psL[:, u % 4, 0:S], w[:, k * P:(k + 1) * P], chunk(N, k), k == 0, k == KC - 1)
                m.then_inc(unit_done, 1)

            ein2_unit(0)
            ein2_unit(1)
            pe.wait_ge(lam_exp, 1)
            pe.wait_ge(ckv_sq, 1)
            for k in range(2):
                m = mm(psO[:, 0:S], C("mean", P), AT[:, k * S:(k + 1) * S], k == 0, k == 1)
            m.then_inc(ckv_ss, 1)
            for T in range(NT):
                for h in range(8):
                    n = T * 8 + h
                    if n >= 2:
                        pe.wait_ge(li_relu, n - 1)
                    r = slice(64 * (h % 2), 64 * (h % 2) + 64)
                    mm(psS[:, n % 2, 0:keys_of(T)], toks(Z, EQI + h // 2, T, r),
                       toks(Z, EKI, 0, r, keys_of(T))).then_inc(li_ready, 1)
                    if n + 2 < N_OUT["ein2"]:
                        ein2_unit(n + 2)
            pe.wait_ge(out_taken, OUT0["ein2"] + 12)
            for kt in range(NT):
                turn([(psT[:, h * P:(h + 1) * P], toks(Z, EVB + h, kt)) for h in range(4)])
            pe.wait_ge(ckv_ready, 2)
            w = weights_at(pe, "ukv", 0)
            for o in range(4):
                for k in range(2):
                    m = mm(psL[:, o, 0:S], w[:, (o * 2 + k) * P:(o * 2 + k + 1) * P], chunk(Z, ECKV + k),
                           k == 0, k == 1)
                m.then_inc(h_ready if o < 3 else unit_done, 1)
            w = weights_at(pe, "ukv", 1)
            for kt in range(NT):
                pe.wait_ge(out_taken, OUT0["ukv"] + kt + 1)
                for k in range(2):
                    m = mm(psL[:, kt, 0:512], toks(Z, ECKV + k, kt), w[:, k * 512:(k + 1) * 512],
                           k == 0, k == 1)
                m.then_inc(h_ready if kt == 0 else unit_done, 1)
            pe.wait_ge(out_taken, OUT0["ukv"] + 6)
            pe.wait_ge(li_relu, 16)
            pe.wait_ge(turn_taken, 5)
            pe.wait_ge(ckv_ready, 1)

            def even(T):
                attention(f"even{T}")
                pe.wait_ge(od_sq, T + 1)
                pe.wait_ge(o_copied, 24 + 8 * T)
                mm(psO[:, 0:512], C("mean128", P), N[:, 0:512]).then_inc(od_ss, 1)
                pe.wait_ge(od_ready, T + 1)
                project(f"eout{T}", lambda k: toks(AT, k, T), P)
                peer(0, T, NORM[f"even{T}"])

            def peer(l, T, norm):
                norm_sum(norm, T)
                pe.wait_ge(n_ready, norm + 1)
                for half, name in enumerate((f"pq{l}{T}a", f"pq{l}{T}b")):
                    project(name, lambda k: toks(N, k, T), P)
                    pe.wait_ge(out_taken, OUT0[name] + 8)
                    for q in range(2 * half, 2 * half + 2):
                        n = (l * NT + T) * 4 + q
                        if n >= 2:
                            pe.wait_ge(key_taken, n - 1)
                        for a in range(4):
                            hp = q * 4 + a
                            m = mm(psS[:, n % 2, a * P:(a + 1) * P], query(l, T, hp),
                                   wsm[:, 384 + (l * 2 + hp % 2) * P:384 + (l * 2 + hp % 2 + 1) * P])
                        m.then_inc(key_scores, 1)
                    if half == 0:
                        for q in range(2):
                            turn([(psT[:, a * P:(a + 1) * P], toks(N, q * 4 + a, T)) for a in range(4)])

            def peer_out(l, T):
                pe.wait_ge(row_used, (l * NT + T + 1) * 2 * SLOTS)
                for q in range(2):
                    turn([(psT[:, a * P:(a + 1) * P], acc[T][:, (q * 4 + a) * P:(q * 4 + a + 1) * P])
                          for a in range(4)])

            def odd(T):
                peer_out(0, T)
                norm = NORM[f"odd{T} mix"]
                norm_sum(norm, T)
                pe.wait_ge(n_ready, norm + 1)
                project(f"oin{T}", lambda k: toks(N, k, T), P)
                pe.wait_ge(out_taken, OUT0[f"oin{T}"] + 25)
                for q in range(2):
                    turn([(psT[:, a * P:(a + 1) * P], toks(Z, OV + q * 4 + a, T)) for a in range(4)])
                pe.wait_ge(f_ready, T + 1)
                pe.wait_ge(turn_taken, turns[0])
                attention(f"odd{T}")
                pe.wait_ge(o_copied, 40 + 8 * T)
                project(f"oout{T}", lambda k: toks(AT, k, T), P)
                peer(1, T, NORM[f"odd{T}"])

            even(0)
            even(1)
            odd(0)
            odd(1)
            peer_out(1, 0)
            peer_out(1, 1)
            norm_sum(NORM["final"])

        @block.vector
        def _(dve):
            steps = [0]

            def link(ins):
                steps[0] += 1
                ins.then_inc(dve_step, 1)
                dve.wait_ge(dve_step, steps[0])

            def stt(o, a, s, b, op0, op1):
                return dve.scalar_tensor_tensor(out=o, in0=a, scalar=s, in1=b, op0=op0, op1=op1)

            def ts(o, a, s1, s2, op0, op1=None):
                return dve.tensor_scalar(o, a, s1, s2, op0) if op1 is None else dve.tensor_scalar(o, a, s1, s2, op0, op1)

            def tt(o, a, b, op):
                return dve.tensor_tensor(o, a, b, op)

            def unit_out(name, j, i, take):
                dve.wait_ge(vec_in, 16)
                dve.wait_ge(unit_done, UNIT0[name] + i * 8 + j + 1)
                take(psL[:, j % 4, 0:S], j, i).then_inc(out_taken, 1)

            def project_copy(name, n, dst):
                rounds(dve, n, lambda j, i: unit_out(
                    name, j, i, lambda p, j, i: dve.tensor_copy(dst[:, bass.ds(i * 8 * S + j * S, S)], p)))

            def beside_nsa(a):
                for o in range(16 + 2 * a, 18 + 2 * a):
                    ada_unit(o % ARING, o, (o // ARING + 1) * 16)
                k = a - 2
                if 0 <= k < KC:
                    dve.wait_ge(out_taken, OUT0["in2b"] + 4)
                    link(ts(chunk(Wt[0], k), zu(ZXR + k), V("conv_w", 3 * 8 + k), V("conv_b", k), ALU.mult, ALU.add))
                    for i in range(3):
                        sh = 3 - i
                        o = chunk(Wt[0], k)[:, sh:S]
                        m = stt(o, zu(ZXR + k)[:, 0:S - sh], V("conv_w", i * 8 + k), o, ALU.mult, ALU.add)
                        if i < 2:
                            link(m)
                    m.then_inc(xc_ready, 1)

            beside = {"l": None}

            def rows(n):
                l, T = beside["l"], beside.get("T")
                if l is None:
                    return
                done = beside["done"]
                n = min(n, 2 * ROUNDS - done)
                if done < ROUNDS < done + n:
                    rows(ROUNDS - done)
                    rows(done + n - ROUNDS)
                    return
                if n <= 0:
                    return
                if done == ROUNDS:
                    dve.wait_ge(act_ready, l * NT + T + 1)
                    g_ = gate[:, T * SLOTS:(T + 1) * SLOTS]
                    tt(g_, g_, dots[:, T * SLOTS:(T + 1) * SLOTS], ALU.mult)
                    link(dve.memset(acc[T], 0.0))
                beside["done"] += n
                base = (l * NT + T) * 2 * ROUNDS
                of_v = done >= ROUNDS
                first = T * SLOTS + (-SLOTS if of_v else 0)

                def one_round(i):
                    for s in range(GRING):
                        r = W[:, s * D:(s + 1) * D]
                        dve.wait_ge(row_landed[s], (i + base + 1) * 16)
                        col = i * GRING + first + s
                        if not of_v:
                            dve.scalar_tensor_tensor(out=r, in0=r, scalar=1.0, in1=h_t[T], op0=ALU.mult, op1=ALU.mult,
                                                     accum_out=dots[:, bass.ds(col, 1)]).then_inc(row_used, 1)
                        else:
                            dve.scalar_tensor_tensor(out=acc[T], in0=r, scalar=gate[:, bass.ds(col, 1)],
                                                     in1=acc[T], op0=ALU.mult, op1=ALU.add).then_inc(row_used, 1)
                            dve.wait_ge(row_used, (i + base) * GRING + s + 1)

                if n == 1:
                    one_round(done)
                else:
                    with dve.Fori(done, done + n) as i:
                        one_round(i)

            def gather(l, T):
                beside.update(l=l, T=T, done=0)

            def residual(name, gcol=None, T=None):
                for o in range(8):
                    if o % 4 == 0:
                        rows(1)
                    dve.wait_ge(unit_done, UNIT0[name] + o + 1)
                    p = psL[:, o % 4, 0:S if T is None else P]
                    x = chunk(X, o) if T is None else toks(X, o, T)
                    if gcol is None:
                        tt(x, p, x, ALU.add).then_inc(out_taken, 1)
                    else:
                        stt(x, p, mod[:, gcol + o:gcol + o + 1], x, ALU.mult, ALU.add).then_inc(out_taken, 1)
                dve.wait_ge(out_taken, OUT0[name] + 8)

            def norm(n, wcol, shift=None, dst=None, T=None):
                dst = N if dst is None else dst
                w = S if T is None else P

                def part(t, k):
                    return chunk(t, k) if T is None else toks(t, k, T)

                dve.wait_ge(ss_ready, n + 1)
                link(ts(var[:, 0:w], psO[:, 0:w], EPS, None, ALU.add))
                dve.reciprocal(var[:, 0:w], var[:, 0:w]).then_inc(rv_ready, 1)
                dve.wait_ge(rstd_ready, n + 1)
                for k in range(KC):
                    m = stt(part(dst, k), part(X, k), wcol(k), rstd[:, 0:w], ALU.mult, ALU.mult)
                    if dst is X and k < KC - 1:
                        m.then_inc(final_chunk, 1)
                if shift is not None:
                    link(m)
                    for k in range(KC):
                        m = ts(part(dst, k), part(dst, k), mod[:, shift + k:shift + k + 1], None, ALU.add)
                m.then_inc(n_ready, 1)

            def attention(kind):
                js = JOBS[kind]

                def front(jb):
                    n, T, b = jb["n"], jb["T"], jb["n"] % 2
                    w = keys_of(T)
                    dve.wait_ge(scores_ready, n + 1)
                    if n >= 2:
                        dve.wait_ge(exp_done, n - 1)
                    for m in range(2):
                        ins = stt(Sb[:, b, m * S:m * S + w], (psL if m else psS)[:, b, 0:w], 0.125, jb["bias"][m],
                                  ALU.mult, ALU.add)
                    link(ins)
                    if jb["kind"] == "dsa":
                        for m in range(2):
                            s = Sb[:, b, m * S:m * S + w]
                            ins = tt(s, s, sel[T][:, 0:w], ALU.add)
                        link(ins)
                    link(dve.tensor_reduce(mx[:, b, 0:2], Sb[:, b, :].rearrange("p (m w) -> p m w", m=2)[:, :, 0:w],
                                           AX.X, ALU.max))
                    ts(mx[:, b, 2:4], mx[:, b, 0:2], -1.0, None, ALU.mult).then_inc(smax_ready, 1)

                def scale(jb):
                    n, T, b = jb["n"], jb["T"], jb["n"] % 2
                    w = keys_of(T)
                    dve.wait_ge(exp_done, n + 1)
                    link(dve.reciprocal(facs[:, b, 0:2], sums[:, b, 0:2]))
                    for m in range(2):
                        if jb["fac"][m] is not None:
                            ins = tt(facs[:, b, m:m + 1], facs[:, b, m:m + 1], jb["fac"][m], ALU.mult)
                    if any(f is not None for f in jb["fac"]):
                        link(ins)
                    for m in range(2):
                        p_ = Pb[:, b, m * S:m * S + w]
                        ins = ts(p_, p_, facs[:, b, m:m + 1], None, ALU.mult)
                    ins.then_inc(p_ready, 1)

                def take(jb):
                    n, T = jb["n"], jb["T"]
                    dve.wait_ge(o_ready, n + 1)
                    for slot, rows, unit in jb["outs"]:
                        ins = dve.tensor_copy(toks(AT, unit, T, rows), psO[rows, slot * P:(slot + 1) * P])
                    ins.then_inc(o_copied, 1)

                front(js[0])
                for a, jb in enumerate(js):
                    if a + 1 < len(js):
                        front(js[a + 1])
                    scale(jb)
                    if a:
                        take(js[a - 1])
                    if kind == "nsa":
                        beside_nsa(a)
                    else:
                        rows(1)
                take(js[-1])

            turns = [0]

            def turn_take(o, src):
                dve.wait_ge(turned, turns[0] + 1)
                turns[0] += 1
                dve.tensor_copy(o, src).then_inc(turn_taken, 1)

            dve.wait_ge(relrow_ready, 1)
            dve.tensor_copy(relrow[:], psO[0:12, 0:384]).then_inc(relrow_copied, 1)

            def ada_unit(slot, o, used):
                dve.wait_ge(ada_landed[slot], used)
                dve.scalar_tensor_tensor(out=aring[:, slot, :], in0=aring[:, slot, :], scalar=1.0, in1=crow[:],
                                         op0=ALU.mult, op1=ALU.mult, accum_out=mod[:, bass.ds(o, 1)]
                                         ).then_inc(ada_used, 1)

            norm(0, lambda k: V("norm1", k))
            dve.wait_ge(csil_ready, 1)

            def in_and_ada(j, i):
                unit_out("in", j, i, lambda p, j, i: dve.tensor_copy(Z[:, bass.ds(i * 8 * S + j * S, S)], p))
                ada_unit(j % ARING, i * 8 + j, (i * 2 + j // ARING + 1) * 16)

            rounds(dve, 13, in_and_ada)
            for o in range(13, 16):
                ada_unit(o % ARING, o, (o // ARING + 1) * 16)
            for n in range(9):
                dve.wait_ge(flipped, n + 1)
                T = n // 3 > 0
                w = keys_of(T)
                dst = bias1[:, (n - 3) * 512:(n - 2) * 512] if T else bias0[:, n * 512:(n + 1) * 512]
                tt(dst.rearrange("p (h w) -> p h w", w=w), psS[:, n % 2, :].rearrange("p (h w) -> p h w", w=w),
                   causal(T)[:, None, :].to_broadcast([P, 512 // w, w]), ALU.add).then_inc(bias_ready, 1)
            dve.wait_ge(out_taken, OUT0["in"] + 13)
            turn_take(VT[:, 0:512], psT[:])
            for kv, (u, pos) in enumerate(((ZKC, "pos_k"), (ZVC, "pos_v"))):
                for odd in range(2):
                    r = slice(64 * odd, 64 * odd + 64)
                    z = Z[r, u * S:(u + 2) * S].rearrange("p (g n a) -> p a g n", g=2, a=16)
                    f = W[r, kv * 512:kv * 512 + 480].rearrange("p (i g n) -> p i g n", i=16, g=2)
                    for late in range(2):
                        src = z[:, odd::2, :, late:late + NCMP]
                        b = vec[r, VEC[pos] + late * 8:VEC[pos] + late * 8 + 8]
                        for g in range(2):
                            m = tt(f[:, late * 8:late * 8 + 8, g, :], src[:, :, g, :],
                                   b[:, :, None].to_broadcast([64, 8, NCMP]), ALU.add)
                        m.then_inc(flat_ready, 1)
            dve.wait_ge(turned, 2)
            turns[0] += 1
            dve.tensor_copy(G[:], psT[:, 0:2 * P].rearrange("p (t c) -> p t c", t=2)[:, :, 0:24]).then_inc(turn_taken, 1)
            dve.wait_ge(kv2_ready, 1)
            dve.tensor_copy(kcT[0:64, 0:NCMP], psO[0:64, 0:NCMP]).then_inc(kv2_taken, 1)
            dve.tensor_copy(kcT[64:128, 0:NCMP], psO[64:128, NCMP:2 * NCMP]).then_inc(kv2_taken, 1)
            dve.tensor_copy(VTc[0:NCMP, 0:P], psO[0:NCMP, 64:192]).then_inc(kv2_taken, 1)
            dve.wait_ge(cs_ready, 1)
            cp3 = cprob.rearrange("p (c n) -> p c n", n=16)[:, :, 0:NCMP]
            po3 = [t[:, 0:128].rearrange("p (c n) -> p c n", n=16)[:, :, 0:NCMP] for t in (psO, psT)]

            def c_t(name, T, n=8):
                a = CON[name] + T * 16
                return con[:, a:a + NCMP][:, None, :].to_broadcast([P, n, NCMP])

            for T in range(NT):
                for b in range(2):
                    m = stt(cp3[:, T * 8 + 4 * b:T * 8 + 4 * b + 4, :], po3[b][:, T * 4:T * 4 + 4, :], 0.125,
                            c_t("cbias", T, 4), ALU.mult, ALU.add)
            link(m)
            link(dve.tensor_reduce(tiny[:, 0:16], cp3, AX.X, ALU.max))
            tt(cp3, cp3, tiny[:, 0:16][:, :, None].to_broadcast([P, 16, NCMP]), ALU.subtract).then_inc(csub_ready, 1)
            dve.wait_ge(cexp_ready, 1)
            for T in range(NT):
                m = tt(cp3[:, T * 8:T * 8 + 8, :], cp3[:, T * 8:T * 8 + 8, :], c_t("cmask", T), ALU.mult)
            link(m)
            link(dve.tensor_reduce(tiny[:, 16:32], cp3, AX.X, ALU.add))
            link(ts(tiny[:, 16:32], tiny[:, 16:32], 1e-20, None, ALU.max))
            link(dve.reciprocal(tiny[:, 16:32], tiny[:, 16:32]))
            dve.wait_ge(turn_taken, 2)
            for T in range(NT):
                g = G[:, T, :].rearrange("p (h b) -> p h b", b=3)[:, :, 0]
                m = tt(tiny[:, 16 + 8 * T:24 + 8 * T], tiny[:, 16 + 8 * T:24 + 8 * T], g, ALU.mult)
            link(m)
            tt(cp3, cp3, tiny[:, 16:32][:, :, None].to_broadcast([P, 16, NCMP]), ALU.mult).then_inc(cp_ready, 1)
            dve.wait_ge(cpt_ready, 1)
            for q in range(2):
                dve.tensor_copy(W[0:NCMP, 6144 + q * 1024:6144 + (q + 1) * 1024].rearrange("p (b n) -> p b n", b=2),
                                (psS if q else psL)[0:NCMP, 0:2, :]).then_inc(kv2_taken, 1)
            attention("nsa")
            dve.wait_ge(xc_ready, KC)
            dve.wait_ge(out_taken, OUT0["lru"] + 16)
            tt(Wt[0][:], Wt[0][:], Wt[2][:], ALU.mult).then_inc(lru_dve, 1)
            dve.wait_ge(lru_act, 1)
            link(ts(tiny[:, 32:40], V("lam", 0, 8), -1.0, 0.0, ALU.mult, ALU.max))
            link(tt(tiny[:, 32:40], tiny[:, 32:40], tiny[:, 40:48], ALU.add))
            ts(tiny[:, 40:48], tiny[:, 32:40], 8.0, None, ALU.mult)
            ts(tiny[:, 48:56], tiny[:, 32:40], -8.0, None, ALU.mult).then_inc(lru_dve, 1)
            dve.wait_ge(lru_act, 2)
            link(tt(Wt[1][:], Wt[3][:], Wt[3][:], ALU.mult))
            stt(Wt[2][:], Wt[1][:], 1.0, Wt[2][:], ALU.add, ALU.mult).then_inc(lru_dve, 1)
            dve.wait_ge(lru_act, 3)
            link(tt(Wt[2][:], Wt[2][:], Wt[0][:], ALU.mult))
            for k in range(KC):
                c = slice(k * S, (k + 1) * S)
                m = dve.tensor_tensor_scan(Wt[1][:, c], Wt[3][:, c], Wt[2][:, c], 0.0, ALU.mult, ALU.add)
            link(m)
            dve.wait_ge(lru_act, 4)
            tt(Wt[1][:], Wt[1][:], zu(ZGR, 8), ALU.mult).then_inc(lru_dve, 1)
            dve.wait_ge(sig_ready, 1)
            for o in range(8):
                if o % 2:
                    dve.wait_ge(unit_done, UNIT0["upattn"] + o // 2 + 1)
                else:
                    dve.wait_ge(pair_ready, o // 2 + 1)
                tt(chunk(N, o), psL[:, o % 4, 0:S], zu(ZGA + o), ALU.mult).then_inc(out_taken, 1)
            for o in range(8):
                dve.wait_ge(unit_done, UNIT0["uprnn"] + o + 1)
                link(tt(zu(ZGB + o), psL[:, o % 4, 0:S], zu(ZGB + o), ALU.mult))
                tt(chunk(N, o), chunk(N, o), zu(ZGB + o), ALU.add).then_inc(out_taken, 1)
            residual("out")
            norm(1, lambda k: V("norm2", k))
            def square_and_ada(j, i):
                dve.wait_ge(vec_in, 16)
                dve.wait_ge(out_taken, OUT0["mlp1"] + i * 8 + j + 1)
                z = Z[:, bass.ds(i * 8 * S + j * S, S)]
                tt(z, z, z, ALU.mult).then_inc(hsq_ready, 1)
                for a in range(j * 3 // 2, (j + 1) * 3 // 2):
                    ada_unit(a % ARING, i * 12 + 48 + a, (i * 3 + 12 + a // ARING + 1) * 16)

            rounds(dve, 32, square_and_ada)
            for o in range(8):
                dve.wait_ge(unit_done, UNIT0["mlp2"] + 4 * o + 4)
                tt(chunk(X, o), psL[:, o % 2, 0:S], chunk(X, o), ALU.add).then_inc(out_taken, 1)
            dve.wait_ge(out_taken, OUT0["mlp2"] + 8)
            norm(2, lambda k: V("final1", k), dst=X)
            dve.wait_ge(n_ready, 3)
            dve.wait_ge(ada_used, 96)
            link(tt(mod[:], mod[:], V("ada_b", 0, 96), ALU.add))
            for l in range(2):
                for a, wname in enumerate(("mix", "ffn")):
                    o = (2 * l + a) * KC
                    m = stt(amul[:, o:o + KC], mod[:, l * 48 + a * 24 + 8:l * 48 + a * 24 + 16], 1.0,
                            V(wname, l * 8, l * 8 + 8), ALU.add, ALU.mult)
            link(m)

            norm(3, lambda k: amul[:, k:k + 1], shift=0)
            tt(tiny[0:64, 0:2], vec[0:64, VEC["blam"]:VEC["blam"] + 4:2], vec[0:64, VEC["blam"] + 1:VEC["blam"] + 4:2],
               ALU.mult).then_inc(lam_in, 1)
            project_copy("ein", 12, Z)
            dve.wait_ge(turned, turns[0] + 1)
            turns[0] += 1
            ts(wi[:], psT[:, 0:2 * P].rearrange("p (t c) -> p t c", t=2)[:, :, 0:8], 8.0 ** -0.5, None, ALU.mult
               ).then_inc(turn_taken, 1)
            dve.wait_ge(lam_exp, 1)
            link(tt(tiny[:, 59:60], tiny[:, 57:58], tiny[:, 56:57], ALU.subtract))
            link(ts(tiny[:, 60:61], tiny[:, 59:60], -LAM_INIT, None, ALU.add))
            dve.wait_ge(ckv_ss, 1)
            link(ts(var[:, 0:S], psO[:, 0:S], 4.0, EPS, ALU.mult, ALU.add))
            dve.reciprocal(var[:, 0:S], var[:, 0:S]).then_inc(rv_ready, 1)
            dve.wait_ge(ckv_ready, 1)
            for k in range(2):
                m = stt(zu(ECKV + k), zu(ECKV + k), V("kvn", k), rstd[:, 0:S], ALU.mult, ALU.mult)
            m.then_inc(ckv_ready, 1)
            def select(T):
                s = sel[T][:, 0:keys_of(T)]
                for r in range(8):
                    link(dve.max(out=m8[:, T, :], in_=s))
                    link(dve.match_replace(out=s, in_to_replace=m8[:, T, :], in_values=s, imm_value=-3e38))
                link(ts(s, s, -2e38, NEG, ALU.is_gt, ALU.mult))

            dve.wait_ge(turn_taken, turns[0])
            for T in range(NT):
                w = keys_of(T)
                for h in range(8):
                    n = T * 8 + h
                    dve.wait_ge(li_relu, n + 1)
                    src = work[:, n % 2, 0:w]
                    if h == 0:
                        m = ts(sel[T][:, 0:w], src, wi[:, T, h:h + 1], None, ALU.mult)
                    else:
                        m = stt(sel[T][:, 0:w], src, wi[:, T, h:h + 1], sel[T][:, 0:w], ALU.mult, ALU.add)
                    m.then_inc(li_added, 1)
                    dve.wait_ge(li_added, n + 1)
                link(tt(sel[T][:, 0:w], sel[T][:, 0:w], causal(T), ALU.add))
                if T == 0:
                    select(0)
            for kt in range(NT):
                turn_take(VT[:, 1024 + kt * 512:1024 + (kt + 1) * 512], psT[:])
            for o in range(4):
                if o < 3:
                    dve.wait_ge(h_ready, 14 + o + 1)
                else:
                    dve.wait_ge(unit_done, UNIT0["ukv"] + 1)
                dve.tensor_copy(zu(24 + o), psL[:, o, 0:S]).then_inc(out_taken, 1)
            for kt in range(NT):
                if kt == 0:
                    dve.wait_ge(h_ready, 18)
                else:
                    dve.wait_ge(unit_done, UNIT0["ukv"] + 2)
                dve.tensor_copy(VT[:, kt * 512:(kt + 1) * 512], psL[:, kt, :]).then_inc(out_taken, 1)
            dve.wait_ge(bias_ready, 9)

            def even(T):
                if T:
                    select(1)
                attention(f"even{T}")
                dve.wait_ge(od_ss, T + 1)
                link(ts(var[:, 0:512], psO[:, 0:512], EPS, None, ALU.add))
                dve.reciprocal(rstd[:, 0:512], var[:, 0:512]).then_inc(od_rv, 1)
                dve.wait_ge(od_rstd, T + 1)
                o = tile_of(AT, 4, 4, T)
                link(stt(o, o, V("subln"), rstd[:, 0:512].rearrange("p (c s) -> p c s", c=4), ALU.mult, ALU.mult))
                ts(o, o, 1.0 - LAM_INIT, None, ALU.mult).then_inc(od_ready, 1)
                residual(f"eout{T}", 16, T)
                peer(0, T, NORM[f"even{T}"], 2, 3, 13)

            def peer(l, T, n, before, first, second):
                rows(1)
                norm(n, lambda k: amul[:, (2 * l + 1) * KC + k:(2 * l + 1) * KC + k + 1], shift=l * 48 + 24, T=T)
                rows(before)
                turns[0] += 2
                search(l, T, 0, first)
                search(l, T, 1, second)
                best = scratch(l, T)[1][3][:, 0:P].rearrange("p (q n) -> p q n", q=8)
                gt = gate[:, T * SLOTS:(T + 1) * SLOTS].rearrange("p (h k) -> p h k", h=8)
                tt(gt, best, best[:, :, 0:1].to_broadcast([P, 8, 16]), ALU.subtract).then_inc(best_in, 1)
                dve.wait_ge(gexp, l * NT + T + 1)
                link(dve.tensor_reduce(tiny[:, 0:8], gt, AX.X, ALU.add))
                link(dve.reciprocal(tiny[:, 0:8], tiny[:, 0:8]))
                link(tt(gt, gt, tiny[:, 0:8][:, :, None].to_broadcast([P, 8, 16]), ALU.mult))
                rows(2 * ROUNDS)
                gather(l, T)

            def search(l, T, half, rounds_):
                sc8, small7 = scratch(l, T)
                H = P // 2
                sc = sc8[:, half * 8 * P:(half + 1) * 8 * P]

                def mine(t, parts=1):
                    return t[:, half * parts * H:(half + 1) * parts * H]

                lists = sc.rearrange("p (q n) -> p q n", q=8)
                val = mine(small7[0], 2).rearrange("p (q n) -> p q n", q=8)
                vix = mine(small7[1], 2).bitcast(U32).rearrange("p (q n) -> p q n", q=8)
                ixf = mine(small7[2], 2).rearrange("p (q n) -> p q n", q=8)
                best = mine(small7[3][:, 0:P]).rearrange("p (q n) -> p q n", q=4)
                bix = mine(small7[3][:, P:S]).bitcast(U32)
                ab, abf, sides = mine(small7[4], 2).bitcast(U32), mine(small7[5], 2), mine(small7[6], 2)
                cand = sc.rearrange("p (h i j) -> p h i j", h=4, i=16)
                candh = sc.rearrange("p (h n) -> p h n", h=4)
                point = [0]

                def between():
                    point[0] += 1
                    rows(rounds_ * point[0] // 16 - rounds_ * (point[0] - 1) // 16)

                def best16(src, v, ix, cnt):
                    for a in range(cnt):
                        m = dve.max(out=v[:, a, 0:8], in_=src[:, a, :])
                    link(m)
                    between()
                    for a in range(cnt):
                        dve.max_index(out=ix[:, a, 0:8], in_max=v[:, a, 0:8], in_values=src[:, a, :])
                    between()
                    for a in range(cnt):
                        m = dve.match_replace(out=src[:, a, :], in_to_replace=v[:, a, 0:8],
                                              in_values=src[:, a, :], imm_value=-3e38)
                    link(m)
                    between()
                    for a in range(cnt):
                        m = dve.max(out=v[:, a, 8:16], in_=src[:, a, :])
                    link(m)
                    between()
                    for a in range(cnt):
                        m = dve.max_index(out=ix[:, a, 8:16], in_max=v[:, a, 8:16], in_values=src[:, a, :])
                    link(m)
                    between()

                dve.wait_ge(key_taken, (l * NT + T) * 4 + 2 * half + 2)
                best16(lists, val, vix, 8)
                link(dve.tensor_copy(ixf, vix))
                v4 = val.rearrange("p (h s) n -> p h s n", s=2)
                link(tt(cand, v4[:, :, 0, :][:, :, :, None].to_broadcast([P, 4, 16, 16]),
                        v4[:, :, 1, :][:, :, None, :].to_broadcast([P, 4, 16, 16]), ALU.add))
                between()
                best16(candh, best, bix.rearrange("p (q n) -> p q n", q=4), 4)
                dve.tensor_scalar(ab[:, 0:H], bix, 4, None, ALU.logical_shift_right)
                link(dve.tensor_scalar(ab[:, H:2 * H], bix, 15, None, ALU.bitwise_and))
                link(dve.tensor_copy(abf, ab))
                f4 = ixf.rearrange("p (h s) n -> p h s n", s=2)
                for side in range(2):
                    pick = abf[:, side * H:(side + 1) * H].rearrange("p (h k) -> p h k", h=4)
                    it = con[:, CON["iota"]:CON["iota"] + 16]
                    link(tt(cand, pick[:, :, :, None].to_broadcast([P, 4, 16, 16]),
                            it[:, None, None, :].to_broadcast([P, 4, 16, 16]), ALU.is_equal))
                    between()
                    link(tt(cand, cand, f4[:, :, side, :][:, :, None, :].to_broadcast([P, 4, 16, 16]), ALU.mult))
                    between()
                    link(dve.tensor_reduce(sides[:, side * H:(side + 1) * H].rearrange("p (h k) -> p h k", h=4),
                                           cand, AX.X, ALU.add))
                    if side == 0:
                        between()
                link(stt(abf[:, 0:H], sides[:, 0:H], float(NKEYS), sides[:, H:2 * H], ALU.mult, ALU.add))
                at = T * SLOTS + half * H
                ts(idx[:, at:at + H], abf[:, 0:H], float(l * NEXP), None, ALU.add).then_inc(idx_ready, 1)

            def peer_out(l, T):
                gcol = l * 48 + 40
                for q in range(2):
                    dve.wait_ge(turned, turns[0] + 1)
                    turns[0] += 1
                    for a in range(4):
                        k = q * 4 + a
                        m = stt(toks(X, k, T), psT[:, a * P:(a + 1) * P], mod[:, gcol + k:gcol + k + 1],
                                toks(X, k, T), ALU.mult, ALU.add)
                    m.then_inc(turn_taken, 1)
                dve.wait_ge(turn_taken, turns[0])
                assert turns[0] == TURNS_PEER[l, T]

            def odd(T):
                peer_out(0, T)
                rows(1)
                norm(NORM[f"odd{T} mix"], lambda k: amul[:, 2 * KC + k:2 * KC + k + 1], shift=48, T=T)
                rows(7)
                turns[0] += 2
                dve.wait_ge(out_taken, OUT0[f"oin{T}"] + 25)
                f, row = toks(Z, OF, T), lrow[:, 0:P]
                link(ts(f, f, V("bf"), None, ALU.add))
                dve.tensor_copy(row, f).then_inc(f_act, 1)
                link(ts(f, f, 0.0, None, ALU.min))
                dve.wait_ge(f_act, 3 * T + 3)
                link(tt(f, f, row, ALU.subtract))
                if T:
                    link(tt(f[:, 0:1], f[:, 0:1], tiny[:, 61:62], ALU.add))
                link(dve.memset(row, 1.0))
                link(dve.tensor_tensor_scan(var[:, 0:P], row, f, 0.0, ALU.mult, ALU.add))
                dve.tensor_copy(tiny[:, 61:62], var[:, P - 1:P])
                link(ts(f, var[:, 0:P], 8.0, None, ALU.mult))
                for q in (0, 64):
                    dve.tensor_copy(row[q:q + 32, :], f[q:q + 32, :])
                    m = dve.memset(row[q + 32:q + 64, :], -1.0)
                link(m)
                for q in (0, 64):
                    m = dve.memset(f[q:q + 32, :], 1.0)
                link(m)
                for h in range(16):
                    m = ts(FK[:, h * S + T * P:h * S + (T + 1) * P], f, C("ind", 1, P, h), None, ALU.mult)
                m.then_inc(f_ready, 1)
                attention(f"odd{T}")
                residual(f"oout{T}", 48 + 16, T)
                peer(1, T, NORM[f"odd{T}"], 2, 4, 7)

            even(0)
            even(1)
            odd(0)
            odd(1)
            peer_out(1, 0)
            rows(2 * ROUNDS)
            peer_out(1, 1)
            norm(NORM["final"], lambda k: V("final2", k))

        @block.scalar
        def _(act):
            steps = [0]

            def link(ins):
                steps[0] += 1
                ins.then_inc(act_step, 1)
                act.wait_ge(act_step, steps[0])

            def f(o, i, fn, **k):
                return act.activation(o, i, fn, **k)

            def outputs_of(name):
                return [(out_taken, OUT0[name] + k + 1) for k in range(KC)]

            def norm(n, waits, T=None, sq=N):
                w = S if T is None else P
                for k, (done, count) in enumerate(waits):
                    act.wait_ge(done, count)
                    o, x = (chunk(sq, k), chunk(X, k)) if T is None else (toks(sq, k, T), toks(X, k, T))
                    f(o, x, ACT.Square).then_inc(sq_ready, 1)
                act.wait_ge(rv_ready, n + 1 + (n > 3))
                f(rstd[:, 0:w], var[:, 0:w], ACT.Sqrt).then_inc(rstd_ready, 1)

            def take_in2(us):
                for u in us:
                    name, at = in2_at(u)
                    act.wait_ge(unit_done, UNIT0[name] + at + 1)
                    f(zu(ZXR + u), psL[:, 2 + u % 2, 0:S], ACT.Copy).then_inc(out_taken, 1)

            def attention(kind):
                js = JOBS[kind]

                def exps(jb):
                    n, b = jb["n"], jb["n"] % 2
                    w = keys_of(jb["T"])
                    act.wait_ge(smax_ready, n + 1)
                    if n >= 2:
                        act.wait_ge(pt_ready, n - 1)
                    for m in range(2):
                        ins = f(Pb[:, b, m * S:m * S + w], Sb[:, b, m * S:m * S + w], ACT.Exp,
                                bias=mx[:, b, 2 + m:3 + m], accum_out=sums[:, b, m:m + 1])
                    ins.then_inc(exp_done, 1)

                def turned_maps(jb):
                    n, T = jb["n"], jb["T"]
                    act.wait_ge(pt_ready, n + 1)
                    if n >= 2:
                        act.wait_ge(o_ready, n - 1)
                    w = 2 * (T + 1) * P
                    f(PT[:, n % 2, 0:w], psT[:, 0:w], ACT.Copy).then_inc(pt_copied, 1)

                exps(js[0])
                for a, jb in enumerate(js):
                    if a + 1 < len(js):
                        exps(js[a + 1])
                    turned_maps(jb)
                    if kind == "nsa":
                        take_in2(in2_beside(a))

            act.dma_start(X[:], x_dram).then_inc(x_in, 16)
            act.dma_start(crow[:], c_row.partition_broadcast(P)).then_inc(c_in, 16)
            act.dma_start(wsm[:], small).then_inc(small_in, 16)
            act.wait_ge(vec_in, 16)
            act.wait_ge(c_in, 16)
            f(crow[:], crow[:], ACT.Silu).then_inc(csil_ready, 1)
            norm(0, [(x_in, 16)] * KC)
            act.wait_ge(out_taken, OUT0["in"] + 13)
            f(zu(ZG), zu(ZG), ACT.Sigmoid).then_inc(gates_ready, 1)
            take_in2(range(0, 4))
            for a in range(4):
                act.wait_ge(unit_done, UNIT0["cmp"] + 2 * a + 2)
                f(hid(a // 2, a % 2), hid_bank(a)[:, 0:30], ACT.Gelu_apprx_tanh).then_inc(out_taken, 1)
            take_in2(range(4, 8))
            act.wait_ge(csub_ready, 1)
            cp3 = cprob.rearrange("p (c n) -> p c n", n=16)[:, :, 0:NCMP]
            f(cp3, cp3, ACT.Exp).then_inc(cexp_ready, 1)
            take_in2(range(8, IN2_BEFORE))
            attention("nsa")
            for a, (dst, bname) in enumerate(((Wt[1], "b_a"), (Wt[2], "b_i"))):
                for k in range(KC):
                    if k < KC - 1:
                        act.wait_ge(h_ready, a * 7 + k + 1)
                    else:
                        act.wait_ge(unit_done, UNIT0["lru"] + a + 1)
                    m = f(dst[:, k * S:(k + 1) * S], psL[:, (a * KC + k) % 4, 0:S], ACT.Sigmoid, bias=V(bname, k))
                    m.then_inc(out_taken, 1)
            act.wait_ge(out_taken, OUT0["lru"] + 16)
            f(zu(ZGA, 16), zu(ZGA, 16), ACT.Sigmoid).then_inc(sig_ready, 1)
            link(f(tiny[:, 40:48], V("lam", 0, 8), ACT.Abs))
            link(f(tiny[:, 40:48], tiny[:, 40:48], ACT.Exp, scale=-1.0))
            f(tiny[:, 40:48], tiny[:, 40:48], ACT.Ln, bias=1.0).then_inc(lru_act, 1)
            act.wait_ge(lru_dve, 2)
            for k in range(KC):
                c = slice(k * S, (k + 1) * S)
                f(Wt[3][:, c], Wt[1][:, c], ACT.Exp, scale=tiny[:, 48 + k:49 + k])
            for k in range(KC):
                c = slice(k * S, (k + 1) * S)
                m = f(Wt[2][:, c], Wt[1][:, c], ACT.Tanh, scale=tiny[:, 40 + k:41 + k])
            m.then_inc(lru_act, 1)
            act.wait_ge(lru_dve, 3)
            f(Wt[2][:], Wt[2][:], ACT.Sqrt).then_inc(lru_act, 1)
            f(zu(ZGR, 8), zu(ZGR, 8), ACT.Gelu_apprx_tanh).then_inc(lru_act, 1)
            norm(1, outputs_of("out"), sq=Z)
            rounds(act, 32, lambda j, i: (
                act.wait_ge(vec_in, 16), act.wait_ge(unit_done, UNIT0["mlp1"] + i * 8 + j + 1),
                f(Z[:, bass.ds(i * 8 * S + j * S, S)], psL[:, j % 4, 0:S], ACT.Relu).then_inc(out_taken, 1)))
            norm(2, outputs_of("mlp2"))
            norm(3, [(final_chunk, k + 1) for k in range(KC - 1)] + [(n_ready, 3)])
            act.wait_ge(lam_sum, 1)
            f(tiny[:, 56:58], psO[:, 256:258], ACT.Exp).then_inc(lam_exp, 1)
            act.wait_ge(out_taken, OUT0["ein"] + 12)
            f(AT[:, 0:512], zu(ECKV, 2), ACT.Square).then_inc(ckv_sq, 1)

            def take_ein2(u):
                act.wait_ge(unit_done, UNIT0["ein2"] + u + 1)
                f(zu(EQB + u), psL[:, u % 4, 0:S], ACT.Copy).then_inc(out_taken, 1)

            take_ein2(0)
            take_ein2(1)
            act.wait_ge(rv_ready, 5)
            f(rstd[:, 0:S], var[:, 0:S], ACT.Sqrt).then_inc(ckv_ready, 1)
            for n in range(16):
                act.wait_ge(li_ready, n + 1)
                if n >= 2:
                    act.wait_ge(li_added, n - 1)
                w = keys_of(n // 8)
                f(work[:, n % 2, 0:w], psS[:, n % 2, 0:w], ACT.Relu, scale=0.125).then_inc(li_relu, 1)
                if n + 2 < N_OUT["ein2"]:
                    take_ein2(n + 2)
            turns = [5]

            def turn_take(o, src):
                act.wait_ge(turned, turns[0] + 1)
                turns[0] += 1
                f(o, src, ACT.Copy).then_inc(turn_taken, 1)

            def project_copy(name, n, base, unit_w):
                rounds(act, n, lambda j, i: (
                    act.wait_ge(vec_in, 16), act.wait_ge(unit_done, UNIT0[name] + i * 8 + j + 1),
                    f(Z[:, bass.ds(i * 8 * unit_w + base + j * unit_w, P)], psL[:, j % 4, 0:P], ACT.Copy
                      ).then_inc(out_taken, 1)))

            def dots_gelu(l, T):
                act.wait_ge(row_used, ((l * NT + T) * 2 + 1) * SLOTS)
                d_ = dots[:, T * SLOTS:(T + 1) * SLOTS]
                f(d_, d_, ACT.Gelu_apprx_tanh).then_inc(act_ready, 1)

            def peer(l, T, n, name):
                norm(n, outputs_of(name), T)
                sc8, _ = scratch(l, T)
                g = l * NT + T
                for half, name in enumerate((f"pq{l}{T}a", f"pq{l}{T}b")):
                    for j in range(8):
                        act.wait_ge(unit_done, UNIT0[name] + j + 1)
                        f(query(l, T, half * 8 + j), psL[:, j % 4, 0:P], ACT.Copy).then_inc(out_taken, 1)
                    if half == 0 and g:
                        act.wait_ge(idx_ready, 2 * g)
                    for q in range(2 * half, 2 * half + 2):
                        act.wait_ge(key_scores, g * 4 + q + 1)
                        f(sc8[:, q * 512:(q + 1) * 512], psS[:, q % 2, :], ACT.Copy).then_inc(key_taken, 1)
                    if half == 0:
                        for q in range(2):
                            turn_take(h_t[T][:, q * 512:(q + 1) * 512], psT[:])

            def best_exp(l, T):
                act.wait_ge(best_in, l * NT + T + 1)
                g_ = gate[:, T * SLOTS:(T + 1) * SLOTS]
                f(g_, g_, ACT.Exp).then_inc(gexp, 1)

            def even(T):
                attention(f"even{T}")
                act.wait_ge(o_copied, 24 + 8 * T)
                f(N[:, 0:512].rearrange("p (c s) -> p c s", c=4), tile_of(AT, 4, 4, T), ACT.Square).then_inc(od_sq, 1)
                act.wait_ge(od_rv, T + 1)
                f(rstd[:, 0:512], rstd[:, 0:512], ACT.Sqrt).then_inc(od_rstd, 1)
                peer(0, T, NORM[f"even{T}"], f"eout{T}")
                if T:
                    dots_gelu(0, 0)
                best_exp(0, T)

            def odd(T):
                turns[0] += 2
                norm(NORM[f"odd{T} mix"], [(turn_taken, TURNS_PEER[0, T])] * KC, T)
                project_copy(f"oin{T}", 25, T * P, S)
                for q in range(2):
                    turn_take(VT[:, T * D + q * 512:T * D + (q + 1) * 512], psT[:])
                row = lrow[:, 0:P]
                act.wait_ge(f_act, 3 * T + 1)
                link(f(row, row, ACT.Abs))
                f(row, row, ACT.Exp, scale=-1.0).then_inc(f_act, 1)
                act.wait_ge(f_act, 3 * T + 2)
                f(row, row, ACT.Ln, bias=1.0).then_inc(f_act, 1)
                attention(f"odd{T}")
                dots_gelu(T, 1 - T)
                peer(1, T, NORM[f"odd{T}"], f"oout{T}")
                best_exp(1, T)

            even(0)
            even(1)
            odd(0)
            odd(1)
            dots_gelu(1, 1)
            norm(NORM["final"], [(turn_taken, TURNS_PEER[1, 1])] * KC)


def kernel(**a):
    import numpy as np
    import concourse.bacc as bacc
    from concourse.bass_utils import run_bass_kernel_spmd

    a = {k: np.asarray(v) for k, v in a.items()}
    f = np.float32

    def units(w):
        n = w.shape[1] // P
        return w.reshape(KC, P, n, P).transpose(2, 1, 0, 3).reshape(n, P, KC * P)

    def cols(w, *parts):
        u = np.zeros((w.shape[0], P), f)
        for start, count, place in parts:
            u[:, place:place + count] = w[:, start:start + count]
        return u

    w = a["w_in"][0]
    pieces = [cols(w, (64 * j, 64, 0), (64 * (j + 4), 64, 64)) for j in range(4)]
    for start in (512, 640):
        pieces += [cols(w, (start + 64 * g, 64, 0), (start + 64 * g, 64, 64)) for g in range(2)]
    pieces += [w[:, 768:1280], cols(w, (1280, 24, 0)), w[:, 1304:5400]]
    first = units(np.concatenate(pieces, 1))
    stream = {"in": first[:13], "in2a": first[13:17], "in2b": first[17:]}
    stream["cmp"] = np.concatenate([
        units(a[n][0][1024 * u:1024 * (u + 1), P * m:P * (m + 1)])
        for n in ("cmp_k_w1", "cmp_v_w1") for m in range(2) for u in range(2)])
    lru = np.zeros((2, P, KC, P), f)
    for n, key in enumerate(("lru_w_a", "lru_w_i")):
        for h in range(16):
            r = slice(64 * (h % 2), 64 * (h % 2) + 64)
            lru[n, r, h // 2, r] = a[key][0, h]
    stream["lru"] = lru.reshape(2, P, KC * P)
    up = a["w_up_attn"][0].reshape(8, 64, D)[[0, 4, 1, 5, 2, 6, 3, 7]].reshape(4, P, 4, 2, P)
    stream["upattn"] = up.transpose(2, 1, 3, 0, 4).reshape(4, P, KC * P)
    stream["uprnn"] = units(a["w_up_rnn"][0])
    stream["out"] = units(a["w_out"][0])
    stream["mlp1"] = units(a["mlp_w1"][0])
    stream["mlp2"] = a["mlp_w2"][0].reshape(4, KC, P, 8, P).transpose(3, 0, 2, 1, 4).reshape(32, P, KC * P)
    w = a["even_w_in_2"][0]
    ein = units(np.concatenate([w[:, 0:1280], cols(w, (1280, 64, 0), (1280, 64, 64)),
                                          cols(w, (1344, 8, 0)), w[:, 1352:2888]], 1))
    stream["ein"], stream["ein2"] = ein[:12], ein[12:]
    uk = a["a_w_uk_2"][0].reshape(2, P, 4, P).transpose(1, 2, 0, 3).reshape(P, KC * P)
    uv = a["a_w_uv_2"][0].reshape(2, P, 512).transpose(1, 0, 2).reshape(P, KC * P)
    stream["ukv"] = np.stack([uk, uv])
    stream["eout0"] = stream["eout1"] = units(a["even_w_out_2"][0])
    w = a["odd_w_in_2"][0]
    stream["oin0"] = stream["oin1"] = units(np.concatenate(
        [w[:, 0:3072], cols(w, *[(3072, 16, q) for q in (0, 32, 64, 96)])], 1))
    stream["oout0"] = stream["oout1"] = units(a["odd_w_out_2"][0])
    for l in range(2):
        queries = units(a["peer_w_q_2"][l])
        for T in range(NT):
            stream[f"pq{l}{T}a"], stream[f"pq{l}{T}b"] = queries[:8], queries[8:]
    weights = np.ascontiguousarray(np.concatenate([stream[n] for n, _, _ in STREAM]))

    w2k, w2v = a["cmp_k_w2"][0].reshape(2, P, 64), a["cmp_v_w2"][0].reshape(2, P, 64)
    small = np.ascontiguousarray(np.concatenate(
        [np.concatenate([w2k, w2k], 2).transpose(1, 0, 2).reshape(P, 256),
         w2v.transpose(1, 0, 2).reshape(P, 128),
         a["peer_sub_keys_2"].transpose(3, 0, 1, 2).reshape(P, 512)], 1))

    def fm(v):
        return v.reshape(-1, P).T

    def rows(v):
        return np.concatenate([v, np.zeros((P - v.shape[0], v.shape[1]), f)])

    bf = np.zeros((P, 1), f)
    for q in (0, 32, 64, 96):
        bf[q:q + 16, 0] = a["odd_b_forget_2"][0]
    vecs = {
        "norm1": fm(a["norm1_w"]), "norm2": fm(a["norm2_w"]), "final1": fm(a["final_norm_w"]),
        "conv_w": fm(a["conv_w"]), "conv_b": fm(a["conv_b"]), "b_a": fm(a["lru_b_a"]), "b_i": fm(a["lru_b_i"]),
        "lam": fm(a["lru_lambda"]), "c": fm(a["c_2"]), "ada_b": fm(a["ada_b_2"]), "mix": fm(a["norm_mix_2"]),
        "ffn": fm(a["norm_ffn_2"]), "final2": fm(a["norm_final_2"]), "kvn": fm(a["a_kv_norm_2"]),
        "subln": fm(a["b_subln_2"]), "bf": bf, "pos_k": fm(a["cmp_pos_k"]), "pos_v": fm(a["cmp_pos_v"]),
        "blam": rows(a["b_lambda_2"][0].T), "rel": rows(a["rel_bias_2"]),
    }
    vecs = np.ascontiguousarray(np.concatenate([vecs[n] for n in VEC], 1))

    q, k = np.arange(P)[:, None], np.arange(P)[None, :]
    t, n = np.arange(S), np.arange(16)
    seen = (n[None, :] < NCMP) & (16 * n[None, :] + 31 <= t[:, None])
    cmask = seen.reshape(NT, P, 16).transpose(1, 0, 2).reshape(P, 32).astype(f)
    dist = np.arange(S)
    big = 16 + (np.log(np.maximum(dist, 1).astype(f) / 16) / math.log(8) * 16).astype(np.int32)
    bucket = np.where(dist < 16, dist, np.minimum(big, 31))
    buckets = np.zeros((P, 384), f)
    buckets[bucket[::-1], np.arange(S)] = 1
    cons = {
        "ident": np.eye(P, dtype=f), "flip": np.ascontiguousarray(np.eye(P, dtype=f)[::-1]), "mean": np.full((P, P), 1 / D, f), "mean128": np.full((P, P), 1 / P, f),
        "ones": np.ones((P, P), f),
        "causal": np.concatenate([np.zeros((P, P), f), np.where(k <= q, 0, NEG).astype(f)], 1),
        "cmask": cmask, "cbias": np.where(cmask > 0, 0, NEG).astype(f),
        "iota": np.tile(np.arange(16, dtype=f), (P, 1)), "buckets": buckets,
        "ind": ((np.arange(P)[:, None] % 32) == n[None, :]).astype(f),
    }
    cons = np.ascontiguousarray(np.concatenate([cons[n] for n in CON], 1))

    ins = {
        "x_dram": np.ascontiguousarray(a["x"].reshape(S, KC, P).transpose(2, 1, 0).reshape(P, KC * S)),
        "c_row": a["c_2"].reshape(D),
        "ada": np.ascontiguousarray(a["ada_w_2"].transpose(0, 2, 1)).reshape(96, P, D), "weights": weights, "small": small, "vecs": vecs, "cons": cons,
        "experts_u": a["peer_u_2"].reshape(2 * NEXP, D), "experts_v": a["peer_v_2"].reshape(2 * NEXP, D),
    }
    nc = bacc.Bacc("TRN2", target_bir_lowering=False, num_devices=1)
    aps = {k: nc.dram_tensor(k, v.shape, F32, kind="ExternalInput").ap() for k, v in ins.items()}
    out = nc.dram_tensor("out", (P, KC * S), F32, kind="ExternalOutput").ap()
    build(nc, out=out, **aps)
    r = run_bass_kernel_spmd(nc, [ins], core_ids=[0])
    y = r.results[0]["out"]
    return y.reshape(P, KC, S).transpose(2, 1, 0).reshape(1, S, D)
```
